# Optimizing a Trainium2 kernel written in Bass

```python
import math
import jax
import jax.numpy as jnp
from jax import lax
import numpy as np

D_MODEL = 1024
BATCH = 1
SEQ = 512
DEPTH = 2

MEM_LEN = 256
N_EVEN = (DEPTH + 1) // 2
N_ODD = DEPTH // 2
NORM_EPS = 1e-6

RW_HEAD_DIM = 64
RW_DIM = D_MODEL // 2
RW_HEADS = RW_DIM // RW_HEAD_DIM
RW_DECAY_RANK = 64
RW_A_RANK = 64
RW_GATE_RANK = 128
RW_GN_EPS = 64e-5
RW_PROJ = 3 * RW_DIM + RW_DECAY_RANK + RW_A_RANK + RW_GATE_RANK

SSD_HEAD_DIM = 64
SSD_DIM = D_MODEL // 2
SSD_HEADS = SSD_DIM // SSD_HEAD_DIM
SSD_GROUPS = 2
SSD_STATE = 128
SSD_CONV = 3
SSD_CHUNK = 128
SSD_CONV_DIM = SSD_DIM + 2 * SSD_GROUPS * SSD_STATE
SSD_PROJ = SSD_DIM + SSD_CONV_DIM + SSD_HEADS

AB_PROJ = RW_PROJ + SSD_PROJ
AB_OUT = RW_DIM + SSD_DIM

HG_HEADS = 8
HG_KEY_DIM = 128
HG_VAL_DIM = D_MODEL // HG_HEADS
HG_KEY_WIDTH = HG_HEADS * HG_KEY_DIM
HG_VAL_WIDTH = HG_HEADS * HG_VAL_DIM
HG_CHUNK = 64
HG_PROJ = 3 * HG_KEY_WIDTH + 2 * HG_VAL_WIDTH

XA_HEADS = 4
XA_HEAD_DIM = D_MODEL // XA_HEADS
FFN_DIM = ((8 * D_MODEL + 3 * 256 - 1) // (3 * 256)) * 256

kernel_name = "bidir_rwkv7_mamba2_hgrn2_hybrid_block"

def rms_norm(x, gain):
    xf = x.astype(jnp.float32)
    y = xf * lax.rsqrt(jnp.mean(xf * xf, axis=-1, keepdims=True) + NORM_EPS)
    return (y * gain.astype(jnp.float32)).astype(x.dtype)

def flip_time(z):
    return jnp.flip(z, axis=1)

def centred_shift(z):
    prev = jnp.pad(z[:, :-1], ((0, 0), (1, 0), (0, 0)))
    nxt = jnp.pad(z[:, 1:], ((0, 0), (0, 1), (0, 0)))
    return 0.5 * (prev + nxt)

def centred_depthwise_conv(u, w, b):
    out = lax.conv_general_dilated(
        u, w[:, None, :].astype(u.dtype), window_strides=(1,),
        padding=[(SSD_CONV // 2, SSD_CONV // 2)],
        dimension_numbers=('NWC', 'WIO', 'NWC'), feature_group_count=u.shape[-1])
    return out + b.astype(u.dtype)

def rwkv7_scan(r, w, k, v, kk, a):
    nb, _, nh, n = r.shape

    def step(state, inp):
        r_t, w_t, k_t, v_t, kk_t, a_t = inp
        sa = jnp.einsum('bhvk,bhk->bhv', state, -kk_t)
        state = (state * w_t[:, :, None, :]
                 + sa[..., None] * (kk_t * a_t)[:, :, None, :]
                 + v_t[..., None] * k_t[:, :, None, :])
        return state, jnp.einsum('bhvk,bhk->bhv', state, r_t)

    xs = tuple(jnp.moveaxis(z, 1, 0) for z in (r, w, k, v, kk, a))
    _, out = lax.scan(step, jnp.zeros((nb, nh, n, n), jnp.float32), xs)
    return jnp.moveaxis(out, 0, 1)

def rwkv7_branch(p, w0, w2, a0, a2, g2, k_k, k_a, r_k, gn_w, gn_b):
    nb, t, _ = p.shape
    o1, o2, o3 = RW_DIM, 2 * RW_DIM, 3 * RW_DIM
    o4 = o3 + RW_DECAY_RANK
    o5 = o4 + RW_A_RANK
    r, k, v = p[..., :o1], p[..., o1:o2], p[..., o2:o3]
    wd, ad, gd = p[..., o3:o4], p[..., o4:o5], p[..., o5:]

    def heads(z):
        return z.reshape(nb, t, RW_HEADS, RW_HEAD_DIM)

    a = jax.nn.sigmoid(a0 + ad @ a2)
    g = jax.nn.sigmoid(gd) @ g2
    kk = heads(k * k_k)
    kk = kk / jnp.maximum(jnp.linalg.norm(kk, axis=-1, keepdims=True), 1e-12)
    k = k * (1.0 + (a - 1.0) * k_a)
    w_lora = jnp.tanh(wd)

    def decay(d):
        w = -jax.nn.softplus(-(w0[d] + w_lora @ w2[d])) - 0.5
        return heads(jnp.exp(-jnp.exp(w)))

    rh, kh, vh, ah = heads(r), heads(k), heads(v), heads(a)
    o_fwd = rwkv7_scan(rh, decay(0), kh, vh, kk, ah)
    o_bwd = flip_time(rwkv7_scan(flip_time(rh), flip_time(decay(1)), flip_time(kh),
                                 flip_time(vh), flip_time(kk), flip_time(ah)))
    o = o_fwd + o_bwd
    mu = jnp.mean(o, axis=-1, keepdims=True)
    var = jnp.mean(jnp.square(o - mu), axis=-1, keepdims=True)
    o = (o - mu) * lax.rsqrt(var + RW_GN_EPS)
    o = o * gn_w.reshape(RW_HEADS, RW_HEAD_DIM) + gn_b.reshape(RW_HEADS, RW_HEAD_DIM)
    o = o + jnp.sum(rh * kh * r_k, axis=-1, keepdims=True) * vh
    return o.reshape(nb, t, RW_DIM) * g

def ssd_chunked(xs, dt, a, bm, cm):
    nb, t = xs.shape[0], xs.shape[1]
    nc, L = t // SSD_CHUNK, SSD_CHUNK
    J = SSD_HEADS // SSD_GROUPS
    xdt = (xs * dt[..., None]).reshape(nb, nc, L, SSD_GROUPS, J, SSD_HEAD_DIM)
    la = (dt * a).reshape(nb, nc, L, SSD_GROUPS, J).transpose(0, 3, 4, 1, 2)
    bc = bm.reshape(nb, nc, L, SSD_GROUPS, SSD_STATE)
    cc = cm.reshape(nb, nc, L, SSD_GROUPS, SSD_STATE)
    cum = jnp.cumsum(la, axis=-1)
    tri = jnp.tril(jnp.ones((L, L), bool))
    decay = jnp.exp(jnp.where(tri, cum[..., :, None] - cum[..., None, :], -jnp.inf))
    scores = jnp.einsum('bclgn,bcsgn->bgcls', cc, bc)
    y_diag = jnp.einsum('bgjcls,bcsgjp->bclgjp', scores[:, :, None] * decay, xdt)
    states = jnp.einsum('bclgn,bgjcl,bclgjp->bcgjpn', bc, jnp.exp(cum[..., -1:] - cum), xdt)
    tot = jnp.pad(cum[..., -1], ((0, 0), (0, 0), (0, 0), (1, 0)))
    ctot = jnp.cumsum(tot, axis=-1)
    tri_c = jnp.tril(jnp.ones((nc + 1, nc + 1), bool))
    decay_c = jnp.exp(jnp.where(tri_c, ctot[..., :, None] - ctot[..., None, :], -jnp.inf))
    states = jnp.concatenate([jnp.zeros_like(states[:, :1]), states], axis=1)
    carried = jnp.einsum('bgjzc,bcgjpn->bzgjpn', decay_c, states)[:, :-1]
    y_off = jnp.einsum('bclgn,bcgjpn,bgjcl->bclgjp', cc, carried, jnp.exp(cum))
    return (y_diag + y_off).reshape(nb, t, SSD_HEADS, SSD_HEAD_DIM)

def ssd_branch(p, conv_w, conv_b, dt_bias, a_log, d_skip, norm_w):
    nb, t, _ = p.shape
    gn = SSD_GROUPS * SSD_STATE
    z = p[..., :SSD_DIM].astype(jnp.float32)
    xbc = p[..., SSD_DIM:SSD_DIM + SSD_CONV_DIM]
    dt_raw = p[..., SSD_DIM + SSD_CONV_DIM:].astype(jnp.float32)
    xbc = jax.nn.silu(centred_depthwise_conv(xbc, conv_w, conv_b)).astype(jnp.float32)
    xs = xbc[..., :SSD_DIM].reshape(nb, t, SSD_HEADS, SSD_HEAD_DIM)
    bm = xbc[..., SSD_DIM:SSD_DIM + gn].reshape(nb, t, SSD_GROUPS, SSD_STATE)
    cm = xbc[..., SSD_DIM + gn:].reshape(nb, t, SSD_GROUPS, SSD_STATE)
    dt_f = jax.nn.softplus(dt_raw + dt_bias[0])
    dt_b = jax.nn.softplus(dt_raw + dt_bias[1])
    y_f = ssd_chunked(xs, dt_f, -jnp.exp(a_log[0]), bm, cm)
    y_b = flip_time(ssd_chunked(flip_time(xs), flip_time(dt_b), -jnp.exp(a_log[1]),
                                flip_time(bm), flip_time(cm)))
    y = y_f + y_b + d_skip[:, None] * xs
    y = (y.reshape(nb, t, SSD_DIM) * jax.nn.silu(z)).reshape(nb, t, SSD_GROUPS, SSD_DIM // SSD_GROUPS)
    y = y * lax.rsqrt(jnp.mean(y * y, axis=-1, keepdims=True) + NORM_EPS)
    return y.reshape(nb, t, SSD_DIM) * norm_w

def rwkv_ssd_mixer(h, w_in, w_out, rw_mu, rw_w0, rw_w2, rw_a0, rw_a2, rw_g2, rw_k_k, rw_k_a,
                   rw_r_k, rw_gn_w, rw_gn_b, ssd_conv_w, ssd_conv_b, ssd_dt_bias, ssd_a_log,
                   ssd_d, ssd_norm_w):
    p = h @ w_in
    p_rw = p[..., :RW_PROJ].astype(jnp.float32)
    p_rw = p_rw + rw_mu * (centred_shift(p_rw) - p_rw)
    o_rw = rwkv7_branch(p_rw, rw_w0, rw_w2, rw_a0, rw_a2, rw_g2, rw_k_k, rw_k_a, rw_r_k,
                        rw_gn_w, rw_gn_b)
    o_ssd = ssd_branch(p[..., RW_PROJ:], ssd_conv_w, ssd_conv_b, ssd_dt_bias, ssd_a_log,
                       ssd_d, ssd_norm_w)
    o = jnp.concatenate([o_rw, o_ssd], axis=-1).astype(h.dtype)
    return o @ w_out

def gla_chunked(q, k, v, log_f):
    nb, t, nh, dk = q.shape
    dv = v.shape[-1]
    nc, L = t // HG_CHUNK, HG_CHUNK

    def to_chunks(z):
        return z.reshape(nb, nc, L, nh, z.shape[-1]).transpose(1, 0, 3, 2, 4)

    tri = jnp.tril(jnp.ones((L, L), bool))[..., None]

    def step(state, inp):
        qc, kc, vc, gc = inp
        bcum = jnp.cumsum(gc, axis=2)
        decay = jnp.exp(jnp.where(tri, bcum[:, :, :, None, :] - bcum[:, :, None, :, :], -jnp.inf))
        attn = jnp.einsum('bhld,bhlsd,bhsd->bhls', qc, decay, kc)
        out = (jnp.einsum('bhls,bhsv->bhlv', attn, vc)
               + jnp.einsum('bhld,bhdv->bhlv', qc * jnp.exp(bcum), state))
        last = bcum[:, :, -1:, :]
        state = (state * jnp.exp(bcum[:, :, -1, :])[..., None]
                 + jnp.einsum('bhsd,bhsv->bhdv', kc * jnp.exp(last - bcum), vc))
        return state, out

    xs = (to_chunks(q), to_chunks(k), to_chunks(v), to_chunks(log_f))
    _, out = lax.scan(step, jnp.zeros((nb, nh, dk, dv), jnp.float32), xs)
    return out.transpose(1, 0, 3, 2, 4).reshape(nb, t, nh, dv)

def hgrn2_mixer(h, w_in, w_out, norm_w, lb):
    nb, t, _ = h.shape
    kw, vw = HG_KEY_WIDTH, HG_VAL_WIDTH
    p = (h @ w_in).astype(jnp.float32)
    q, f_fwd, f_bwd = p[..., :kw], p[..., kw:2 * kw], p[..., 2 * kw:3 * kw]
    i, g = p[..., 3 * kw:3 * kw + vw], p[..., 3 * kw + vw:]

    def kheads(z):
        return z.reshape(nb, t, HG_HEADS, HG_KEY_DIM)

    def gates(f_raw):
        f = lb + (1.0 - lb) * jax.nn.sigmoid(f_raw)
        return kheads(1.0 - f), kheads(jnp.log(f))

    k_f, lf_f = gates(f_fwd)
    k_b, lf_b = gates(f_bwd)
    qh = kheads(q)
    ih = i.reshape(nb, t, HG_HEADS, HG_VAL_DIM)
    o = (gla_chunked(qh, k_f, ih, lf_f)
         + flip_time(gla_chunked(flip_time(qh), flip_time(k_b), flip_time(ih), flip_time(lf_b))))
    o = o * lax.rsqrt(jnp.mean(o * o, axis=-1, keepdims=True) + NORM_EPS)
    o = o * norm_w.reshape(HG_HEADS, HG_VAL_DIM)
    o = o.reshape(nb, t, vw) * jax.nn.silu(g)
    return o.astype(h.dtype) @ w_out

def memory_cross_attention(h, m, wq, wkv, wo):
    nb, t, _ = h.shape
    nm = m.shape[1]
    q = (h @ wq).reshape(nb, t, XA_HEADS, XA_HEAD_DIM)
    kv = m @ wkv
    k = kv[..., :D_MODEL].reshape(nb, nm, XA_HEADS, XA_HEAD_DIM)
    v = kv[..., D_MODEL:].reshape(nb, nm, XA_HEADS, XA_HEAD_DIM)
    s = jnp.einsum('bthd,bmhd->bhtm', q, k).astype(jnp.float32) * (XA_HEAD_DIM ** -0.5)
    pr = jax.nn.softmax(s, axis=-1).astype(v.dtype)
    o = jnp.einsum('bhtm,bmhd->bthd', pr, v).reshape(nb, t, D_MODEL)
    return o @ wo

def swiglu_ffn(h, w_in, w_out):
    gu = h @ w_in
    return (jax.nn.silu(gu[..., :FFN_DIM]) * gu[..., FFN_DIM:]) @ w_out

def setup_inputs(seed: int = 0) -> dict:
    key = jax.random.key(seed)
    ks = jax.random.split(key, 40)
    f32 = jnp.float32

    def nrm(k, shape, scale):
        return scale * jax.random.normal(k, shape, f32)

    def gain(k, shape):
        return 1.0 + 0.01 * jax.random.normal(k, shape, f32)

    dt0 = jnp.exp(jax.random.uniform(ks[17], (N_EVEN, 2, SSD_HEADS), f32,
                                     minval=math.log(1e-3), maxval=math.log(1e-1)))
    return {
        "x": nrm(ks[0], (BATCH, SEQ, D_MODEL), 1.0),
        "mem": nrm(ks[1], (BATCH, MEM_LEN, D_MODEL), 1.0),
        "mix_norm": gain(ks[2], (DEPTH, D_MODEL)),
        "ab_w_in": nrm(ks[3], (N_EVEN, D_MODEL, AB_PROJ), D_MODEL ** -0.5),
        "ab_w_out": nrm(ks[4], (N_EVEN, AB_OUT, D_MODEL), AB_OUT ** -0.5),
        "rw_mu": jax.random.uniform(ks[5], (N_EVEN, RW_PROJ), f32),
        "rw_w0": jax.random.uniform(ks[6], (N_EVEN, 2, RW_DIM), f32, minval=-6.5, maxval=-1.5),
        "rw_w2": nrm(ks[7], (N_EVEN, 2, RW_DECAY_RANK, RW_DIM), 0.1 * RW_DECAY_RANK ** -0.5),
        "rw_a0": nrm(ks[8], (N_EVEN, RW_DIM), 0.1),
        "rw_a2": nrm(ks[9], (N_EVEN, RW_A_RANK, RW_DIM), RW_A_RANK ** -0.5),
        "rw_g2": nrm(ks[10], (N_EVEN, RW_GATE_RANK, RW_DIM), RW_GATE_RANK ** -0.5),
        "rw_k_k": 0.85 + nrm(ks[11], (N_EVEN, RW_DIM), 0.05),
        "rw_k_a": 1.0 + nrm(ks[12], (N_EVEN, RW_DIM), 0.05),
        "rw_r_k": nrm(ks[13], (N_EVEN, RW_HEADS, RW_HEAD_DIM), 0.1),
        "rw_gn_w": gain(ks[14], (N_EVEN, RW_DIM)),
        "rw_gn_b": nrm(ks[15], (N_EVEN, RW_DIM), 0.01),
        "ssd_conv_w": nrm(ks[16], (N_EVEN, SSD_CONV, SSD_CONV_DIM), SSD_CONV ** -0.5),
        "ssd_conv_b": nrm(ks[18], (N_EVEN, SSD_CONV_DIM), 0.01),
        "ssd_dt_bias": dt0 + jnp.log(-jnp.expm1(-dt0)),
        "ssd_a_log": jnp.log(jax.random.uniform(ks[19], (N_EVEN, 2, SSD_HEADS), f32, minval=1.0, maxval=16.0)),
        "ssd_d": 1.0 + nrm(ks[20], (N_EVEN, SSD_HEADS), 0.1),
        "ssd_norm_w": gain(ks[21], (N_EVEN, SSD_DIM)),
        "hg_w_in": nrm(ks[22], (N_ODD, D_MODEL, HG_PROJ), D_MODEL ** -0.5),
        "hg_w_out": nrm(ks[23], (N_ODD, HG_VAL_WIDTH, D_MODEL), HG_VAL_WIDTH ** -0.5),
        "hg_norm_w": gain(ks[24], (N_ODD, HG_VAL_WIDTH)),
        "hg_lb": nrm(ks[25], (DEPTH, HG_KEY_WIDTH), 0.1),
        "xa_norm": gain(ks[26], (DEPTH, D_MODEL)),
        "mem_norm": gain(ks[27], (DEPTH, D_MODEL)),
        "xa_wq": nrm(ks[28], (DEPTH, D_MODEL, D_MODEL), D_MODEL ** -0.5),
        "xa_wkv": nrm(ks[29], (DEPTH, D_MODEL, 2 * D_MODEL), D_MODEL ** -0.5),
        "xa_wo": nrm(ks[30], (DEPTH, D_MODEL, D_MODEL), D_MODEL ** -0.5),
        "ffn_norm": gain(ks[31], (DEPTH, D_MODEL)),
        "ffn_w_in": nrm(ks[32], (DEPTH, D_MODEL, 2 * FFN_DIM), D_MODEL ** -0.5),
        "ffn_w_out": nrm(ks[33], (DEPTH, FFN_DIM, D_MODEL), FFN_DIM ** -0.5),
        "final_norm": gain(ks[34], (D_MODEL,)),
    }

def reference(x, mem, mix_norm, ab_w_in, ab_w_out, rw_mu, rw_w0, rw_w2, rw_a0, rw_a2, rw_g2,
              rw_k_k, rw_k_a, rw_r_k, rw_gn_w, rw_gn_b, ssd_conv_w, ssd_conv_b, ssd_dt_bias,
              ssd_a_log, ssd_d, ssd_norm_w, hg_w_in, hg_w_out, hg_norm_w, hg_lb, xa_norm,
              mem_norm, xa_wq, xa_wkv, xa_wo, ffn_norm, ffn_w_in, ffn_w_out, final_norm):
    lb_all = jax.nn.softmax(hg_lb.astype(jnp.float32), axis=0)
    lb_all = jnp.cumsum(lb_all, axis=0) - lb_all[0]
    for layer in range(DEPTH):
        h = rms_norm(x, mix_norm[layer])
        if layer % 2 == 0:
            e = layer // 2
            mixed = rwkv_ssd_mixer(h, ab_w_in[e], ab_w_out[e], rw_mu[e], rw_w0[e], rw_w2[e],
                                   rw_a0[e], rw_a2[e], rw_g2[e], rw_k_k[e], rw_k_a[e], rw_r_k[e],
                                   rw_gn_w[e], rw_gn_b[e], ssd_conv_w[e], ssd_conv_b[e],
                                   ssd_dt_bias[e], ssd_a_log[e], ssd_d[e], ssd_norm_w[e])
        else:
            o = layer // 2
            mixed = hgrn2_mixer(h, hg_w_in[o], hg_w_out[o], hg_norm_w[o], lb_all[layer])
        x = x + mixed
        x = x + memory_cross_attention(rms_norm(x, xa_norm[layer]), rms_norm(mem, mem_norm[layer]),
                                       xa_wq[layer], xa_wkv[layer], xa_wo[layer])
        x = x + swiglu_ffn(rms_norm(x, ffn_norm[layer]), ffn_w_in[layer], ffn_w_out[layer])
    return rms_norm(x, final_norm)


_drawn_inputs = setup_inputs


def setup_inputs(seed=0):
    import zlib

    import numpy as np

    out = dict(_drawn_inputs(seed))
    spreads = {}
    factors = {'mix_norm': 3.217,
     'rw_w2': 8.0,
     'rw_a0': 3.736,
     'rw_gn_w': 8.0,
     'rw_gn_b': 8.0,
     'ssd_conv_b': 4.553,
     'ssd_norm_w': 7.282,
     'hg_norm_w': 33.888,
     'xa_norm': 8.0,
     'mem_norm': 8.0,
     'ffn_norm': 5.91,
     'final_norm': 32.61,
     'ssd_d': 3.816}
    for name, (base, spread) in spreads.items():
        noise = np.random.default_rng([zlib.crc32(name.encode()), seed]).standard_normal(out[name].shape)
        drawn = base * np.exp(spread * noise) if base else spread * noise
        out[name] = jnp.asarray(drawn.astype(out[name].dtype))
    for name, factor in factors.items():
        out[name] = (out[name] * factor).astype(out[name].dtype)
    return out
```

```python
from contextlib import ExitStack

import numpy as np
import concourse.bass as bass
from concourse import mybir

F32 = mybir.dt.float32
U32 = mybir.dt.uint32
ALU = mybir.AluOpType
ACT = mybir.ActivationFunctionType
AXX = mybir.AxisListType.X

P = 128
D, T, MEM = 1024, 512, 256
KD = D // P
NC = T // P
HD = 64
RW_TILES = 14
XBC_TILES = 8
Z_TILES = 4
XS0, B0, C0, Z0, REV0 = 14, 18, 20, 22, 26
HEADS = 8
FFN = 2816
FT = FFN // P
DECAY_SCALE = float(np.exp(-0.5))
LEVELS = [1, 2, 4, 8, 16, 32, 64]
RW_VECS = ["w0f", "w0b", "a0", "kk", "ka", "rk", "gnw", "gnb"]


def column_layout():
    at, n = {}, 0
    for name, width in [("one", 1), ("eps", 1), ("gneps", 1), ("mix0", 8), ("mix1", 8), ("xa0", 8), ("xa1", 8),
                        ("mem0", 8), ("mem1", 8), ("ffn0", 8), ("ffn1", 8), ("final", 8), ("mu", 14),
                        ("taps", 32), ("rw", 4 * len(RW_VECS)), ("ssd_d", 4), ("ssd_w", 4), ("hgw", 8),
                        ("lb0", 8), ("lb1", 8), ("dtb", 2), ("alog", 2)]:
        at[name] = n
        n += width
    return at, n


COL, NCOLS = column_layout()
TAB = dict(ident=0, ones=128, blk=256, strict=384, incl=512, reset=640, up=1152, low=1152 + 7 * P)
NTAB = 1152 + 14 * P


class Steps:

    def __init__(self, sem, names):
        self.opened = names[0] == "^"
        self.sem, self.names, self.next = sem, list(names[self.opened:]), 0
        self.value = {n: j + 1 for j, n in enumerate(self.names)}
        assert len(self.value) == len(self.names), "step names repeat"

    def one(self, name):
        assert self.names[self.next % len(self.names)] == name, (self.names[self.next % len(self.names)], name)
        self.next += 1
        return 1

    def at(self, name, i=0):
        return i * len(self.names) + (self.value[name] + self.opened)

    def passes(self, i):
        assert self.opened
        return i * len(self.names) + 1


class Ring:

    def __init__(self, slots, sems):
        self.slots, self.sems, self.base = slots, sems, [0, 0]

    def load(self, sp, w, j, u):
        sp.dma_start(self.slots[u][:, 0:w.shape[2]], w[bass.ds(j, 1), :, :].rearrange("a p n -> (a p) n")
                     ).then_inc(self.sems[u], 16)

    def at(self, u, i):
        return i * 16 + (self.base[u] + 16)

    def used(self, n):
        self.base = [b + 16 * n for b in self.base]


def fori(engine, n0, n1):
    return engine.Fori(n0, n1)


def build_program(nc, dram, out_d, scratch_d):
    ctx = ExitStack()
    with ctx:
        def sb(name, words):
            return ctx.enter_context(nc.sbuf_tensor(name, [P, words], F32))[:, :]

        banks = [ctx.enter_context(nc.psum_tensor(f"bank{i}", [P, 512], F32))[:, :] for i in range(8)]
        xT = sb("xT", KD * T)
        hT = sb("hT", KD * T)
        proj = sb("proj", 40 * T)
        slots = [sb(f"wslot{u}", 22 * P) for u in range(2)]
        tab = sb("tab", NTAB)
        cols = sb("cols", NCOLS)
        memT = sb("memT", KD * MEM)
        work = sb("work", 11600)
        loads = ctx.enter_context(nc.semaphore("first_loads"))
        loads2 = ctx.enter_context(nc.semaphore("table_loads"))
        loads3 = ctx.enter_context(nc.semaphore("column_loads"))
        loads4 = ctx.enter_context(nc.semaphore("memory_loads"))
        loads5 = ctx.enter_context(nc.semaphore("low_rank_loads"))
        stored = ctx.enter_context(nc.semaphore("stored"))
        ring = Ring(slots, [ctx.enter_context(nc.semaphore(f"weights{u}_loaded")) for u in range(2)])

        x3 = xT.rearrange("p (n t) -> p n t", t=T)
        h3 = hT.rearrange("p (n t) -> p n t", t=T)
        p3 = proj.rearrange("p (n t) -> p n t", t=T)

        def table(name, width=P, at=0):
            return tab[:, TAB[name] + at:TAB[name] + at + width]

        ident, ones, blk = table("ident"), table("ones"), table("blk")

        def col(name, j=0, n=1):
            return cols[:, COL[name] + j:COL[name] + j + n]

        def chunk(ap, c):
            return ap[:, c * P:(c + 1) * P]

        def over_chunks(ap):
            return ap.unsqueeze(1).broadcast_to([P, NC, P])

        def by_chunk(ap):
            return ap.rearrange("p (c t) -> p c t", t=P)

        dirs = (lambda ap: ap, lambda ap: ap[:, ::-1])

        held = {n: ctx.enter_context(nc.semaphore(f"held_{n}")) for n in ("vec", "pool")}

        def hold(engine, name):
            engine.sem_inc(held[name], 1)

        def steps(scope, **named):
            return [Steps(scope.enter_context(nc.semaphore(n)), v) for n, v in named.items()]

        class Projection:

            def __init__(self, w, rhs, tiles, k=KD, n=T, token_major=False):
                self.w, self.rhs, self.tiles, self.k, self.n, self.tm = w, rhs, tiles, k, n, token_major

            def prefetch(self, sp):
                for u in range(2):
                    ring.load(sp, self.w, u, u)

            def load_rest(self, sp, pe_s, following):
                n = self.tiles // 2
                with fori(sp, 1, n) as i:
                    for u in range(2):
                        sp.wait_ge(pe_s.sem, pe_s.at(f"tile{u}", i - 1))
                        ring.load(sp, self.w, i * 2 + u, u)
                for u in range(2):
                    sp.wait_ge(pe_s.sem, pe_s.at(f"tile{u}", n - 1))
                    if following is not None:
                        ring.load(sp, following.w, u, u)

            def multiply(self, pe, pe_s, emptied):
                def one(i, first):
                    for u in range(2):
                        pe.wait_ge(ring.sems[u], ring.at(u, i))
                        if not first:
                            emptied(pe, u, i - 1)
                        if self.tm:
                            for m in range(MEM // P):
                                for k in range(self.k):
                                    ins = pe.matmul(banks[u][:, m * 256:(m + 1) * 256], self.rhs[:, k, m * P:(m + 1) * P],
                                                    slots[u][:, k * 256:(k + 1) * 256], start=k == 0, stop=k == self.k - 1)
                        else:
                            for k in range(self.k):
                                ins = pe.matmul(banks[u][:, 0:self.n], slots[u][:, k * P:(k + 1) * P],
                                                self.rhs[:, k, :], start=k == 0, stop=k == self.k - 1)
                        ins.then_inc(pe_s.sem, pe_s.one(f"tile{u}"))
                one(0, True)
                pe_s.next = 0
                with fori(pe, 1, self.tiles // 2) as i:
                    one(i, False)

        def project(name, pr, vector=None, scalar=None, following=None, reader="v"):
            with ExitStack() as scope:
                pe_s, v_s, a_s = steps(scope, **{name + "_tile": ["tile0", "tile1"], name + "_vec": ["v0", "v1"],
                                                 name + "_act": ["a0", "a1"]})
                emptied_by = v_s if reader == "v" else a_s
                with nc.Block() as block:
                    @block.sync
                    def _(sp):
                        pr.load_rest(sp, pe_s, following)

                    @block.tensor
                    def _(pe):
                        pr.multiply(pe, pe_s, lambda e, u, i: e.wait_ge(
                            emptied_by.sem, emptied_by.at(f"{reader}{u}", i)))

                    if scalar:
                        @block.scalar
                        def _(act):
                            with fori(act, 0, pr.tiles // 2) as i:
                                for u in range(2):
                                    act.wait_ge(pe_s.sem, pe_s.at(f"tile{u}", i))
                                    scalar(act, i, u, banks[u]).then_inc(a_s.sem, a_s.one(f"a{u}"))

                    if vector:
                        @block.vector
                        def _(dve):
                            with fori(dve, 0, pr.tiles // 2) as i:
                                for u in range(2):
                                    dve.wait_ge(pe_s.sem, pe_s.at(f"tile{u}", i))
                                    vector(dve, i, u, banks[u]).then_inc(v_s.sem, v_s.one(f"v{u}"))
                ring.used(pr.tiles // 2)

        def add_to_residual(name, w, rhs, k, following):
            def add(dve, i, u, bank):
                x = xT[:, bass.ds(i * (2 * T) + u * T, T)]
                return dve.tensor_tensor(x, bank, x, ALU.add)
            project(name, Projection(w, rhs, KD, k=k), vector=add, following=following)

        def rms_norm(name, src, dst, width, gain, following=None, store=None):
            root, inv = work[:, 0:width], work[:, 512:512 + width]
            with ExitStack() as scope:
                act_s, pe_s, v_s = steps(scope, **{
                    name + "_act": [f"square{k}" for k in range(KD)] + ["root"], name + "_pe": ["sum"],
                    name + "_vec": ["inverse"] + [f"out{k}" for k in range(KD)]})
                with nc.Block() as block:
                    @block.sync
                    def _(sp):
                        if following is not None:
                            following.prefetch(sp)
                        if store is not None:
                            for k in range(KD):
                                sp.wait_ge(v_s.sem, v_s.at(f"out{k}"))
                                sp.dma_start(store[:, k, :], dst[:, k, :]).then_inc(stored, 16)
                            sp.wait_ge(stored, 16 * KD)

                    @block.scalar
                    def _(act):
                        for k in range(KD):
                            act.activation(dst[:, k, :], src[:, k, :], ACT.Square).then_inc(act_s.sem, act_s.one(f"square{k}"))
                        act.wait_ge(pe_s.sem, pe_s.at("sum"))
                        act.activation(root, banks[0][:, 0:width], ACT.Sqrt, bias=col("eps"),
                                                  scale=1.0 / D).then_inc(act_s.sem, act_s.one("root"))

                    @block.tensor
                    def _(pe):
                        for k in range(KD):
                            pe.wait_ge(act_s.sem, act_s.at(f"square{k}"))
                            ins = pe.matmul(banks[0][:, 0:width], ones, dst[:, k, :], start=k == 0, stop=k == KD - 1)
                        ins.then_inc(pe_s.sem, pe_s.one("sum"))

                    @block.vector
                    def _(dve):
                        dve.wait_ge(act_s.sem, act_s.at("root"))
                        dve.reciprocal(inv, root).then_inc(v_s.sem, v_s.one("inverse"))
                        dve.wait_ge(v_s.sem, v_s.at("inverse"))
                        for k in range(KD):
                            dve.scalar_tensor_tensor(dst[:, k, :], src[:, k, :], col(gain, k), inv,
                                                              ALU.mult, ALU.mult).then_inc(v_s.sem, v_s.one(f"out{k}"))

        lora = work[:, 9552:11600]
        dtw = work[:, 9488:9552]
        with nc.Block() as block:
            @block.sync
            def _(sp):
                sp.dma_start(xT, dram["xT"]).then_inc(loads, 16)
                sp.dma_start(tab, dram["tab"]).then_inc(loads2, 16)
                sp.dma_start(cols, dram["cols"]).then_inc(loads3, 16)
                sp.dma_start(memT, dram["memT"]).then_inc(loads4, 16)
                sp.dma_start(work[:, 9488:11600], dram["lora"]).then_inc(loads5, 16)
                for s in (loads, loads2, loads3, loads4, loads5):
                    sp.wait_ge(s, 16)

        mem3 = memT.rearrange("p (n m) -> p n m", m=MEM)

        def rwkv_ssd_projection():
            pr = Projection(dram["ab_in"], h3, 26)
            raw = [work[:, u * 520:u * 520 + 514] for u in range(2)]
            t1 = [work[:, 1040 + u * 512:1552 + u * 512] for u in range(2)]
            t2 = [work[:, 2064 + u * 512:2576 + u * 512] for u in range(2)]
            rev = [work[:, 3088 + u * 512:3600 + u * 512] for u in range(2)]
            sil = [work[:, 8336 + u * 512:8848 + u * 512] for u in range(2)]
            dt_x, dt_m, dt, cum = (work[0:8, 4112 + 1024 * j:5136 + 1024 * j] for j in range(4))
            mu_half, mu_rest, decay_rate = work[:, 8300:8314], work[:, 8314:8328], work[0:8, 8330:8332]
            names = ["tile0", "tile1"]
            with ExitStack() as scope:
                pe_s, dtp_s = steps(scope, ab_tile=names, ab_dt_tile=["dt"])
                set_s, = steps(scope, ab_setup=["zero0", "zero1", "zero2", "zero3", "half", "rest"])
                act_s, = steps(scope, ab_raw=["raw0", "raw1"])
                v_s, = steps(scope, ab_taps=["^", "mid0", "left0", "right0", "mid1", "left1", "right1"])
                vc_s, = steps(scope, ab_conv=["^", "mid0", "left0", "right0", "mid1", "left1", "right1"])
                ac_s, = steps(scope, ab_silu=["raw0", "silu0", "raw1", "silu1"])
                g_s, = steps(scope, ab_reverse=["^", "fwd0", "rev0", "fwd1", "rev1"])
                az_s, = steps(scope, ab_z=["z0", "z1"])
                dta_s, = steps(scope, ab_dt_act=["rate", "exp", "log"])
                dtv_s, = steps(scope, ab_dt_vec=["x0", "x1", "minus", "negrate", "dt0", "dt1", "la0", "la1",
                                                 "cum0", "cum1"])
                nrw, nx, nz = RW_TILES // 2, XBC_TILES // 2, Z_TILES // 2
                with nc.Block() as block:
                    @block.sync
                    def _(sp):
                        pr.load_rest(sp, pe_s, None)
                        sp.wait_ge(dtv_s.sem, dtv_s.at("cum1"))
                        sp.dma_start(scratch_d.rearrange("(d h t) -> h d t", d=2, h=8),
                                     cum.rearrange("h (d t) -> h d t", d=2)).then_inc(stored_cum, 16)
                        sp.wait_ge(stored_cum, 16)

                    @block.tensor
                    def _(pe):
                        def one(i, wait_emptied):
                            for u in range(2):
                                pe.wait_ge(ring.sems[u], ring.at(u, i))
                                wait_emptied(u)
                                for k in range(KD):
                                    ins = pe.matmul(banks[u], slots[u][:, k * P:(k + 1) * P], h3[:, k, :],
                                                    start=k == 0, stop=k == KD - 1)
                                ins.then_inc(pe_s.sem, pe_s.one(f"tile{u}"))
                            pe_s.next = 0
                        one(0, lambda u: None)
                        with fori(pe, 1, nrw) as i:
                            one(i, lambda u: pe.wait_ge(act_s.sem, act_s.at(f"raw{u}", i - 1)))
                        one(nrw, lambda u: pe.wait_ge(act_s.sem, act_s.at(f"raw{u}", nrw - 1)))
                        with fori(pe, 1, nx) as i:
                            one(i + nrw, lambda u: pe.wait_ge(ac_s.sem, ac_s.at(f"raw{u}", i - 1)))
                        one(nrw + nx, lambda u: pe.wait_ge(ac_s.sem, ac_s.at(f"raw{u}", nx - 1)))
                        with fori(pe, 1, nz) as i:
                            one(i + (nrw + nx), lambda u: pe.wait_ge(az_s.sem, az_s.at(f"z{u}", i - 1)))
                        for k in range(KD):
                            ins = pe.matmul(banks[2][0:8, :], dtw[:, k * 8:(k + 1) * 8], h3[:, k, :],
                                            start=k == 0, stop=k == KD - 1)
                        ins.then_inc(dtp_s.sem, dtp_s.one("dt"))

                    @block.scalar
                    def _(act):
                        act.wait_ge(set_s.sem, set_s.at("zero3"))
                        with fori(act, 0, nrw) as i:
                            for u in range(2):
                                act.wait_ge(pe_s.sem, pe_s.at(f"tile{u}", i))
                                act.wait_ge(v_s.sem, v_s.passes(i))
                                act.activation(raw[u][:, 1:513], banks[u], ACT.Copy).then_inc(act_s.sem, act_s.one(f"raw{u}"))
                        act.wait_ge(v_s.sem, v_s.at("right1", nrw - 1))
                        with fori(act, 0, nx) as i:
                            for u in range(2):
                                act.wait_ge(pe_s.sem, pe_s.at(f"tile{u}", i + nrw))
                                act.wait_ge(vc_s.sem, vc_s.passes(i))
                                act.activation(raw[u][:, 1:513], banks[u], ACT.Copy).then_inc(ac_s.sem, ac_s.one(f"raw{u}"))
                                act.wait_ge(vc_s.sem, vc_s.at(f"right{u}", i))
                                act.wait_ge(g_s.sem, g_s.passes(i))
                                act.activation(sil[u], rev[u], ACT.Silu).then_inc(ac_s.sem, ac_s.one(f"silu{u}"))
                        with fori(act, 0, nz) as i:
                            for u in range(2):
                                act.wait_ge(pe_s.sem, pe_s.at(f"tile{u}", i + (nrw + nx)))
                                act.activation(proj[:, bass.ds(i * (2 * T) + (Z0 + u) * T, T)], banks[u],
                                                         ACT.Silu).then_inc(az_s.sem, az_s.one(f"z{u}"))
                        act.activation(decay_rate, cols[0:8, COL["alog"]:COL["alog"] + 2], ACT.Exp).then_inc(dta_s.sem, dta_s.one("rate"))
                        act.wait_ge(dtv_s.sem, dtv_s.at("minus"))
                        act.activation(dt_m, dt_m, ACT.Exp).then_inc(dta_s.sem, dta_s.one("exp"))
                        act.wait_ge(dta_s.sem, dta_s.at("exp"))
                        act.activation(dt_m, dt_m, ACT.Ln, bias=1.0).then_inc(dta_s.sem, dta_s.one("log"))

                    @block.vector
                    def _(dve):
                        dve.sem_inc(v_s.sem, 1)
                        dve.sem_inc(vc_s.sem, 1)
                        for u in range(2):
                            dve.memset(raw[u][:, 0:1], 0.0).then_inc(set_s.sem, set_s.one(f"zero{2 * u}"))
                            dve.memset(raw[u][:, 513:514], 0.0).then_inc(set_s.sem, set_s.one(f"zero{2 * u + 1}"))
                        dve.tensor_scalar(mu_half, col("mu", 0, 14), 0.5, None, ALU.mult).then_inc(set_s.sem, set_s.one("half"))
                        dve.tensor_scalar(mu_rest, col("mu", 0, 14), -1.0, 1.0, ALU.mult, ALU.add).then_inc(set_s.sem, set_s.one("rest"))
                        dve.wait_ge(set_s.sem, set_s.at("rest"))
                        with fori(dve, 0, nrw) as i:
                            for u in range(2):
                                j = i * 2 + u
                                half = mu_half[:, bass.ds(j, 1)]
                                dve.wait_ge(act_s.sem, act_s.at(f"raw{u}", i))
                                dve.tensor_scalar(t1[u], raw[u][:, 1:513], mu_rest[:, bass.ds(j, 1)], None,
                                                           ALU.mult).then_inc(v_s.sem, v_s.one(f"mid{u}"))
                                dve.wait_ge(v_s.sem, v_s.at(f"mid{u}", i))
                                dve.scalar_tensor_tensor(t2[u], raw[u][:, 0:512], half, t1[u],
                                                                  ALU.mult, ALU.add).then_inc(v_s.sem, v_s.one(f"left{u}"))
                                dve.wait_ge(v_s.sem, v_s.at(f"left{u}", i))
                                dve.scalar_tensor_tensor(proj[:, bass.ds(i * (2 * T) + u * T, T)],
                                                                  raw[u][:, 2:514], half, t2[u], ALU.mult, ALU.add).then_inc(v_s.sem, v_s.one(f"right{u}"))
                        dve.wait_ge(v_s.sem, v_s.at("right1", nrw - 1))
                        with fori(dve, 0, nx) as i:
                            for u in range(2):
                                def tap(n):
                                    return cols[:, bass.ds(i * 8 + (COL["taps"] + 4 * u + n), 1)]
                                dve.wait_ge(ac_s.sem, ac_s.at(f"raw{u}", i))
                                dve.tensor_scalar(t1[u], raw[u][:, 1:513], tap(1), tap(3), ALU.mult, ALU.add).then_inc(vc_s.sem, vc_s.one(f"mid{u}"))
                                dve.wait_ge(vc_s.sem, vc_s.at(f"mid{u}", i))
                                dve.scalar_tensor_tensor(t2[u], raw[u][:, 0:512], tap(0), t1[u],
                                                                   ALU.mult, ALU.add).then_inc(vc_s.sem, vc_s.one(f"left{u}"))
                                dve.wait_ge(vc_s.sem, vc_s.at(f"left{u}", i))
                                dve.scalar_tensor_tensor(rev[u], raw[u][:, 2:514], tap(2), t2[u],
                                                                   ALU.mult, ALU.add).then_inc(vc_s.sem, vc_s.one(f"right{u}"))
                        dve.wait_ge(dtp_s.sem, dtp_s.at("dt"))
                        for d in range(2):
                            dve.tensor_scalar(dt_x[:, d * T:(d + 1) * T], banks[2][0:8, :],
                                                         cols[0:8, COL["dtb"] + d:COL["dtb"] + d + 1], None, ALU.add).then_inc(dtv_s.sem, dtv_s.one(f"x{d}"))
                        dve.wait_ge(dtv_s.sem, dtv_s.at("x1"))
                        dve.scalar_tensor_tensor(dt_m, dt_x, -1.0, dt_x, ALU.mult, ALU.min).then_inc(dtv_s.sem, dtv_s.one("minus"))
                        dve.wait_ge(dta_s.sem, dta_s.at("rate"))
                        dve.tensor_scalar(decay_rate, decay_rate, -1.0, None, ALU.mult).then_inc(dtv_s.sem, dtv_s.one("negrate"))
                        dve.wait_ge(dta_s.sem, dta_s.at("log"))
                        for d in range(2):
                            dve.scalar_tensor_tensor(
                                dt[:, d * T:(d + 1) * T], dirs[d](dt_x[:, d * T:(d + 1) * T]), 0.0,
                                dirs[d](dt_m[:, d * T:(d + 1) * T]), ALU.max, ALU.add).then_inc(dtv_s.sem, dtv_s.one(f"dt{d}"))
                        dve.wait_ge(dtv_s.sem, dtv_s.at("dt1"))
                        for d in range(2):
                            dve.tensor_scalar(dt_x[:, d * T:(d + 1) * T], dt[:, d * T:(d + 1) * T],
                                                         decay_rate[:, d:d + 1], None, ALU.mult).then_inc(dtv_s.sem, dtv_s.one(f"la{d}"))
                        dve.wait_ge(dtv_s.sem, dtv_s.at("la1"))
                        for d in range(2):
                            dve.tensor_tensor_scan(cum[:, d * T:(d + 1) * T], tab[0:8, TAB["reset"]:TAB["reset"] + T],
                                                              dt_x[:, d * T:(d + 1) * T], 0.0, ALU.mult, ALU.add).then_inc(dtv_s.sem, dtv_s.one(f"cum{d}"))

                    @block.gpsimd
                    def _(pool):
                        pool.sem_inc(g_s.sem, 1)
                        with fori(pool, 0, nx) as i:
                            for u in range(2):
                                pool.wait_ge(ac_s.sem, ac_s.at(f"silu{u}", i))
                                for name, at, src in (("fwd", XS0, sil[u]), ("rev", REV0, sil[u][:, ::-1])):
                                    pool.tensor_copy(proj[:, bass.ds(i * (2 * T) + (at + u) * T, T)], src).then_inc(g_s.sem, g_s.one(f"{name}{u}"))
                ring.used(13)
            return dt, cum

        stored_cum = ctx.enter_context(nc.semaphore("cum_stored"))
        mixer0_out = Projection(dram["ab_out"], h3, KD)
        rms_norm("norm_mix0", x3, h3, T, "mix0", following=Projection(dram["ab_in"], h3, 26))
        dt_sb, cum_sb = rwkv_ssd_projection()

        def ssd():
            cumb = work[:, 0:2048]
            xs_st, b_st, c_st = work[:, 2048:3072], work[:, 3072:3584], work[:, 3584:4096]
            state = work[:, 4112:4368]
            o = 4368
            dt_tok, cum_tok, ecum = work[:, o:o + 64], work[:, o + 64:o + 128], work[:, o + 128:o + 192]
            cum16, dt16, ecum16, eend, wdiff, wexp = (work[:, o + 192 + 16 * j:o + 208 + 16 * j] for j in range(6))
            q = 34 * T
            dec = proj[:, q:q + 512]
            mix = proj[:, q + 512:q + 1024]
            sm, btok = proj[:, q + 1024:q + 1152], proj[:, q + 1152:q + 1280]
            xdt, xdtw = proj[:, q + 1280:q + 1536], proj[:, q + 1536:q + 1792]
            y1, y2 = proj[:, q + 1792:q + 2048], proj[:, q + 2048:q + 2304]
            tmp = proj[:, q + 2304:q + 2560]

            def h4(ap):
                return ap.rearrange("p (h w) -> p h w", h=4)

            def per_head(ap16, c, w):
                return ap16[:, 4 * c:4 * c + 4].unsqueeze(2).broadcast_to([P, 4, w])

            with ExitStack() as scope:
                pre_pe, pre_v, pre_a = steps(scope, ssd_pre_pe=["tok"], ssd_pre_vec=["dt_tok", "cum_tok", "mask"],
                                             ssd_pre_act=["ecum"])
                pe_s, a_s, v_s, g_s = steps(
                    scope,
                    ssd_pe=["^"] + [f"{s}{c}" for c in range(NC) for s in ("scores", "turned", "off", "add", "y", "back")],
                    ssd_act=["^", "xs", "b", "c", "eend", "wexp"] + [f"{s}{c}" for c in range(NC) for s in ("dec", "btok", "out")],
                    ssd_vec=["^", "zero", "wdiff"] + [f"{s}{c}" for c in range(NC) for s in
                                                 ("xdt", "xdtw", "sm", "cap", "mix", "y1", "hdecay", "hadd", "y2")],
                    ssd_pool=["cum16", "dt16", "ecum16"] + [f"dec{c}" for c in range(NC)])
                cumb_sem = scope.enter_context(nc.semaphore("cumb_loaded"))

                def passes():
                    return [(d, g) for d in range(2) for g in range(2)]

                def each_pass(engine, body):
                    with fori(engine, 0, 2) as d:
                        with fori(engine, 0, 2) as g:
                            body(d, g, d * 2 + g)

                with nc.Block() as block:
                    @block.sync
                    def _(sp):
                        def body(d, g, it):
                            sp.wait_ge(v_s.sem, v_s.passes(it))
                            sp.dma_start(cumb, scratch_d[bass.ds(d * (8 * T) + g * (4 * T), 4 * T)].partition_broadcast(P)
                                         ).then_inc(cumb_sem, 16)
                        each_pass(sp, body)

                    @block.tensor
                    def _(pe):
                        for d in range(2):
                            for c in range(NC):
                                w = d * T + c * P
                                k = (d * NC + c) * 8
                                pe.transpose(banks[0][:, k:k + 8], dt_sb[:, w:w + P], ident[0:8, 0:8])
                                ins = pe.transpose(banks[1][:, k:k + 8], cum_sb[:, w:w + P], ident[0:8, 0:8])
                        ins.then_inc(pre_pe.sem, pre_pe.one("tok"))
                        pe.sem_inc(pe_s.sem, 1)

                        def body(d, g, it):
                            pe.wait_ge(v_s.sem, v_s.passes(it))
                            pe.wait_ge(a_s.sem, a_s.at("c", it))
                            for c in range(NC):
                                if c:
                                    pe.wait_ge(v_s.sem, v_s.at(f"sm{c - 1}", it))
                                else:
                                    pe.wait_ge(pre_v.sem, pre_v.at("cum_tok"))
                                pe.matmul(banks[1][:, 0:P], chunk(b_st, c), chunk(c_st, c),
                                                    start=True, stop=True).then_inc(pe_s.sem, pe_s.one(f"scores{c}"))
                                if c:
                                    pe.wait_ge(v_s.sem, v_s.at(f"xdt{c - 1}", it))
                                    pe.wait_ge(a_s.sem, a_s.at(f"btok{c - 1}", it))
                                for j in range(2):
                                    pe.transpose(banks[2][:, j * P:(j + 1) * P], chunk(xs_st, NC * j + c), ident)
                                pe.transpose(banks[2][:, 2 * P:3 * P], chunk(b_st, c), ident).then_inc(pe_s.sem, pe_s.one(f"turned{c}"))
                                if c:
                                    pe.wait_ge(v_s.sem, v_s.at(f"hadd{c - 1}", it))
                                else:
                                    pe.wait_ge(v_s.sem, v_s.at("zero", it))
                                pe.matmul(banks[4][:, 0:256], chunk(c_st, c), state, start=True, stop=True).then_inc(pe_s.sem, pe_s.one(f"off{c}"))
                                pe.wait_ge(v_s.sem, v_s.at(f"xdtw{c}", it))
                                pe.wait_ge(a_s.sem, a_s.at(f"btok{c}", it))
                                pe.matmul(banks[5][:, 0:256], btok, xdtw, start=True, stop=True).then_inc(pe_s.sem, pe_s.one(f"add{c}"))
                                pe.wait_ge(v_s.sem, v_s.at(f"mix{c}", it))
                                if c:
                                    pe.wait_ge(v_s.sem, v_s.at(f"y2{c - 1}", it))
                                for h in range(4):
                                    ins = pe.matmul(banks[3][:, h * HD:(h + 1) * HD], chunk(mix, h),
                                                    xdt[:, h * HD:(h + 1) * HD], start=True, stop=True)
                                ins.then_inc(pe_s.sem, pe_s.one(f"y{c}"))
                                pe.wait_ge(v_s.sem, v_s.at(f"y2{c}", it))
                                if c:
                                    pe.wait_ge(a_s.sem, a_s.at(f"out{c - 1}", it))
                                for j in range(2):
                                    ins = pe.transpose(banks[6][:, j * P:(j + 1) * P], y2[:, j * P:(j + 1) * P], ident)
                                ins.then_inc(pe_s.sem, pe_s.one(f"back{c}"))
                        each_pass(pe, body)

                    @block.scalar
                    def _(act):
                        act.sem_inc(a_s.sem, 1)
                        act.wait_ge(pre_v.sem, pre_v.at("cum_tok"))
                        act.activation(ecum, cum_tok, ACT.Exp).then_inc(pre_a.sem, pre_a.one("ecum"))

                        def body(d, g, it):
                            act.wait_ge(pe_s.sem, pe_s.passes(it))
                            act.wait_ge(v_s.sem, v_s.passes(it))
                            base = d * (12 * T)
                            act.activation(xs_st, proj[:, bass.ds(base + g * (2 * T) + XS0 * T, 2 * T)], ACT.Copy).then_inc(a_s.sem, a_s.one("xs"))
                            act.activation(b_st, proj[:, bass.ds(base + g * T + B0 * T, T)], ACT.Copy).then_inc(a_s.sem, a_s.one("b"))
                            act.activation(c_st, proj[:, bass.ds(base + g * T + C0 * T, T)], ACT.Copy).then_inc(a_s.sem, a_s.one("c"))
                            act.wait_ge(cumb_sem, it * 16 + 16)
                            ends = cumb.rearrange("p (h c t) -> p c h t", h=4, t=P)[:, :, :, P - 1]
                            act.activation(eend.rearrange("p (c h) -> p c h", h=4), ends, ACT.Exp).then_inc(a_s.sem, a_s.one("eend"))
                            act.wait_ge(v_s.sem, v_s.at("wdiff", it))
                            act.activation(wexp, wdiff, ACT.Exp).then_inc(a_s.sem, a_s.one("wexp"))
                            for c in range(NC):
                                act.wait_ge(v_s.sem, v_s.at(f"cap{c}", it))
                                act.activation(dec, dec, ACT.Exp).then_inc(a_s.sem, a_s.one(f"dec{c}"))
                                act.wait_ge(pe_s.sem, pe_s.at(f"turned{c}", it))
                                if c:
                                    act.wait_ge(pe_s.sem, pe_s.at(f"add{c - 1}", it))
                                act.activation(btok, banks[2][:, 2 * P:3 * P], ACT.Copy).then_inc(a_s.sem, a_s.one(f"btok{c}"))
                                act.wait_ge(pe_s.sem, pe_s.at(f"back{c}", it))
                                act.activation(h3[:, bass.ds(d * 4 + g * 2, 2), c * P:(c + 1) * P],
                                                        banks[6][:, 0:256].rearrange("p (j t) -> p j t", t=P),
                                                        ACT.Copy).then_inc(a_s.sem, a_s.one(f"out{c}"))
                        each_pass(act, body)

                    @block.gpsimd
                    def _(pool):
                        def body(d, g, it):
                            pool.wait_ge(a_s.sem, a_s.passes(it))
                            pool.wait_ge(v_s.sem, v_s.passes(it))
                            pool.wait_ge(pre_a.sem, pre_a.at("ecum"))
                            for name, dst, src in (("cum16", cum16, cum_tok), ("dt16", dt16, dt_tok), ("ecum16", ecum16, ecum)):
                                pool.tensor_copy(dst.rearrange("p (c h) -> p c h", h=4),
                                                          src.rearrange("p (n h) -> p n h", h=8)[:, bass.ds(d * 4, 4), bass.ds(g * 4, 4)]).then_inc(g_s.sem, g_s.one(name))
                            pool.wait_ge(cumb_sem, it * 16 + 16)
                            pool.wait_ge(g_s.sem, g_s.at("cum16", it))
                            for c in range(NC):
                                if c:
                                    pool.wait_ge(v_s.sem, v_s.at(f"mix{c - 1}", it))
                                pool.tensor_tensor(h4(dec), h4(cumb)[:, :, c * P:(c + 1) * P],
                                                            per_head(cum16, c, P), ALU.subtract).then_inc(g_s.sem, g_s.one(f"dec{c}"))
                        each_pass(pool, body)

                    @block.vector
                    def _(dve):
                        dve.sem_inc(v_s.sem, 1)
                        dve.wait_ge(pre_pe.sem, pre_pe.at("tok"))
                        dve.tensor_copy(dt_tok, banks[0][:, 0:64]).then_inc(pre_v.sem, pre_v.one("dt_tok"))
                        dve.tensor_copy(cum_tok, banks[1][:, 0:64]).then_inc(pre_v.sem, pre_v.one("cum_tok"))

                        def body(d, g, it):
                            dve.wait_ge(pe_s.sem, pe_s.passes(it))
                            dve.memset(state, 0.0).then_inc(v_s.sem, v_s.one("zero"))
                            dve.wait_ge(g_s.sem, g_s.at("ecum16", it))
                            dve.wait_ge(cumb_sem, it * 16 + 16)
                            ends = cumb.rearrange("p (h c t) -> p c h t", h=4, t=P)[:, :, :, P - 1]
                            dve.tensor_tensor(wdiff.rearrange("p (c h) -> p c h", h=4), ends,
                                                       cum16.rearrange("p (c h) -> p c h", h=4), ALU.subtract).then_inc(v_s.sem, v_s.one("wdiff"))
                            for c in range(NC):
                                dve.wait_ge(pe_s.sem, pe_s.at(f"turned{c}", it))
                                if c:
                                    dve.wait_ge(pe_s.sem, pe_s.at(f"y{c - 1}", it))
                                dve.tensor_tensor(h4(xdt), h4(banks[2][:, 0:256]), per_head(dt16, c, HD), ALU.mult).then_inc(v_s.sem, v_s.one(f"xdt{c}"))
                                dve.wait_ge(a_s.sem, a_s.at("wexp", it))
                                dve.wait_ge(v_s.sem, v_s.at(f"xdt{c}", it))
                                dve.tensor_tensor(h4(xdtw), h4(xdt), per_head(wexp, c, HD), ALU.mult).then_inc(v_s.sem, v_s.one(f"xdtw{c}"))
                                dve.wait_ge(pe_s.sem, pe_s.at(f"scores{c}", it))
                                dve.tensor_tensor(sm, banks[1][:, 0:P], table("incl"), ALU.mult).then_inc(v_s.sem, v_s.one(f"sm{c}"))
                                dve.wait_ge(g_s.sem, g_s.at(f"dec{c}", it))
                                dve.tensor_scalar(dec, dec, 0.0, None, ALU.min).then_inc(v_s.sem, v_s.one(f"cap{c}"))
                                dve.wait_ge(a_s.sem, a_s.at(f"dec{c}", it))
                                dve.wait_ge(v_s.sem, v_s.at(f"sm{c}", it))
                                dve.tensor_tensor(h4(mix), h4(dec), sm.unsqueeze(1).broadcast_to([P, 4, P]), ALU.mult).then_inc(v_s.sem, v_s.one(f"mix{c}"))
                                dve.wait_ge(pe_s.sem, pe_s.at(f"off{c}", it))
                                dve.tensor_tensor(h4(y1), h4(banks[4][:, 0:256]), per_head(ecum16, c, HD), ALU.mult).then_inc(v_s.sem, v_s.one(f"y1{c}"))
                                dve.tensor_tensor(h4(tmp), h4(state), per_head(eend, c, HD), ALU.mult).then_inc(v_s.sem, v_s.one(f"hdecay{c}"))
                                dve.wait_ge(pe_s.sem, pe_s.at(f"add{c}", it))
                                dve.wait_ge(v_s.sem, v_s.at(f"hdecay{c}", it))
                                dve.tensor_tensor(state, banks[5][:, 0:256], tmp, ALU.add).then_inc(v_s.sem, v_s.one(f"hadd{c}"))
                                dve.wait_ge(pe_s.sem, pe_s.at(f"y{c}", it))
                                if c:
                                    dve.wait_ge(pe_s.sem, pe_s.at(f"back{c - 1}", it))
                                dve.tensor_tensor(y2, banks[3][:, 0:256], y1, ALU.add).then_inc(v_s.sem, v_s.one(f"y2{c}"))
                        each_pass(dve, body)

        def ssd_gate():
            both, skip, sq = work[:, 0:2048], work[:, 2048:4096], work[:, 4112:6160]
            root, inv = proj[:, 34 * T:36 * T], proj[:, 36 * T:38 * T]
            with ExitStack() as scope:
                v_s, a_s, pe_s = steps(
                    scope, gate_vec=["both"] + [f"skip{j}" for j in range(4)] + ["gated", "inverse"] + [f"out{j}" for j in range(4)],
                    gate_act=["square", "root0", "root1"], gate_pe=["sum0", "sum1"])
                with nc.Block() as block:
                    @block.vector
                    def _(dve):
                        dve.tensor_tensor(both.rearrange("p (j t) -> p j t", t=T), h3[:, 0:4, :], h3[:, 4:8, ::-1],
                                                   ALU.add).then_inc(v_s.sem, v_s.one("both"))
                        dve.wait_ge(v_s.sem, v_s.at("both"))
                        for j in range(4):
                            dve.scalar_tensor_tensor(skip[:, j * T:(j + 1) * T], p3[:, XS0 + j, :], col("ssd_d", j),
                                                              both[:, j * T:(j + 1) * T], ALU.mult, ALU.add).then_inc(v_s.sem, v_s.one(f"skip{j}"))
                        dve.wait_ge(v_s.sem, v_s.at("skip3"))
                        dve.tensor_tensor(hT[:, 4 * T:8 * T], skip, proj[:, Z0 * T:(Z0 + 4) * T], ALU.mult).then_inc(v_s.sem, v_s.one("gated"))
                        dve.wait_ge(a_s.sem, a_s.at("root1"))
                        dve.reciprocal(inv, root).then_inc(v_s.sem, v_s.one("inverse"))
                        dve.wait_ge(v_s.sem, v_s.at("inverse"))
                        for j in range(4):
                            dve.scalar_tensor_tensor(h3[:, 4 + j, :], h3[:, 4 + j, :], col("ssd_w", j),
                                                              inv[:, (j // 2) * T:(j // 2 + 1) * T], ALU.mult, ALU.mult).then_inc(v_s.sem, v_s.one(f"out{j}"))

                    @block.scalar
                    def _(act):
                        act.wait_ge(v_s.sem, v_s.at("gated"))
                        act.activation(sq, hT[:, 4 * T:8 * T], ACT.Square).then_inc(a_s.sem, a_s.one("square"))
                        for g in range(2):
                            act.wait_ge(pe_s.sem, pe_s.at(f"sum{g}"))
                            act.activation(root[:, g * T:(g + 1) * T], banks[g], ACT.Sqrt, bias=col("eps"),
                                                    scale=1.0 / 256).then_inc(a_s.sem, a_s.one(f"root{g}"))

                    @block.tensor
                    def _(pe):
                        pe.wait_ge(a_s.sem, a_s.at("square"))
                        for g in range(2):
                            for j in range(2):
                                ins = pe.matmul(banks[g], ones, sq[:, (2 * g + j) * T:(2 * g + j + 1) * T],
                                                start=j == 0, stop=j == 1)
                            ins.then_inc(pe_s.sem, pe_s.one(f"sum{g}"))

        ssd()
        ssd_gate()
        def rwkv():
            spans = {"r": [proj, XS0 * T, 40 * T], "w": [work, 0, 9488], "s0": [slots[0], KD * P, 22 * P],
                     "s1": [slots[1], KD * P, 22 * P]}

            def take(words, span="r"):
                s = spans[span]
                at = s[1]
                s[1] += words
                assert s[1] <= s[2], (span, s)
                return s[0][:, at:at + words]

            tanh_ad, gate_in = take(T), take(T)
            low, vec, r_st, v_st = take(T), take(8), take(T), take(T)
            a_t, g_t, sg0, sg1, kk, sq, km, b_t, rk, bonus = (take(T) for _ in range(10))
            ka1 = sq
            cum, cen, cex, pos, neg, prv = (take(T) for _ in range(6))
            kr = take(2 * NC * P).rearrange("p (c w t) -> p c w t", c=NC, w=2)
            b_i, k_i, v_r = take(T), take(T), take(T, "w")
            b_tok, k_tok, v_tok = take(T, "w"), take(T, "w"), take(T, "w")
            state, added, rhs, sa = (take(P, "w") for _ in range(4))
            mid, carry = take(4, "w"), take(4, "w")
            ac, be = [], []
            for h in range(2):
                ac.append(take(2 * NC * P, "w").rearrange("p (c w t) -> p c w t", c=NC, w=2))
                be.append(take(2 * NC * P, "w").rearrange("p (c w t) -> p c w t", c=NC, w=2))
            x_m = [take(T, "w"), take(T, "w")]
            x_t = [take(T, "w"), take(T, "s1")]
            y_m = [take(T, "s0"), take(T, "s0")]
            o_t = take(T, "s1")
            sg = [sg0, sg1]
            y_bank, z_bank, zt_bank = [4, 6], [3, 5], [7, 0]
            out_bank = 6
            nl = len(LEVELS) - 1
            heads = range(2)
            hs = [slice(h * HD, (h + 1) * HD) for h in heads]

            def vcol(name):
                return vec[:, RW_VECS.index(name):RW_VECS.index(name) + 1]

            def level_names(kinds):
                return [f"{k}{n}{h}_%d" for n in range(1, nl + 1) for group in (["y"], ["z", "zt"]) for h in heads
                        for k in group if k in kinds and not (k == "z" and n == nl)]

            def both_dirs(names):
                return [n % d for d in range(2) for n in names]

            pe_names = ["a", "w0", "w1", "g", "norm", "bonus"] + both_dirs(
                ["turn_b_%d", "turn_k_%d", "turn_v_%d"] + [f"{m}{h}{q}_%d" for m in ("ac", "be") for h in heads for q in range(2)]
                + [f"x{h}_%d" for h in heads] + level_names(["y", "z", "zt"])
                + [f"{s}{c}_%d" for c in range(NC) for s in ("rhs", "sa", "s", "o") if not (s == "s" and c == NC - 1)]
            ) + ["mean", "var"]
            act_names = ["^", "a", "w0", "w1", "g", "sq", "root"] + both_dirs(
                ["pos_%d", "neg_%d", "prv_%d", "mid_%d", "b_tok_%d", "k_tok_%d", "v_tok_%d"]
                + [f"x{h}_%d" for h in heads] + level_names(["y"]) + [f"{s}{c}_%d" for c in range(NC) for s in ("rhs", "sa")]
                + ["out_%d"]) + ["osq", "oroot"]
            act_names.remove("out_1")
            vec_names = ["^", "kk0", "ka", "km", "rk", "nmax", "ninv", "kk", "b", "bonus"] + both_dirs(
                ["cum_%d", "cen_%d", "cex_%d", "kkP_%d", "bI_%d", "carry_%d", "zero_%d"]
                + [f"{m}{h}{q}_%d" for m in ("ac", "be") for h in heads for q in range(2)]
                + [f"{s}{h}_%d" for h in heads for s in ("xa", "xt")] + level_names(["z", "zt"])
                + [f"{s}{c}_%d" for c in range(NC - 1) for s in ("add", "s")]
                + ["out_%d"]) + ["centre", "oinv", "on", "og", "ob", "res"]
            vec_names.remove("out_0")
            pool_names = ["^", "low", "vec", "r", "v"] + both_dirs(["v_%d", "rP_%d", "kI_%d"])
            with ExitStack() as scope:
                zero_s, pre_a, pe_s, a_s, v_s, g_s = steps(scope, rw_zero=["ac0", "be0", "ac1", "be1"],
                                                           rw_pre=["tanh", "ad", "gate"], rw_pe=pe_names, rw_act=act_names,
                                                   rw_vec=vec_names, rw_pool=pool_names)
                with nc.Block() as block:
                    @block.sync
                    def _(sp):
                        mixer0_out.prefetch(sp)

                    @block.gpsimd
                    def _(pool):
                        pool.sem_inc(g_s.sem, 1)
                        with fori(pool, 0, 4) as ct:
                            pool.wait_ge(v_s.sem, v_s.passes(ct))
                            pool.wait_ge(a_s.sem, a_s.passes(ct))
                            hold(pool, "pool")
                            pool.tensor_copy(low.rearrange("p (m c) -> p m c", m=4),
                                                      lora[:, 0:2048].rearrange("p (m c) -> p m c", m=4)[:, :, bass.ds(ct * P, P)]).then_inc(g_s.sem, g_s.one("low"))
                            pool.tensor_copy(vec, cols[:, bass.ds(ct * 8 + COL["rw"], 8)]).then_inc(g_s.sem, g_s.one("vec"))
                            pool.tensor_copy(r_st, proj[:, bass.ds(ct * T, T)]).then_inc(g_s.sem, g_s.one("r"))
                            pool.tensor_copy(v_st, proj[:, bass.ds(ct * T + 8 * T, T)]).then_inc(g_s.sem, g_s.one("v"))
                            for d in range(2):
                                if d:
                                    pool.wait_ge(pe_s.sem, pe_s.at("o3_0", ct))
                                else:
                                    pool.wait_ge(g_s.sem, g_s.at("v", ct))
                                hold(pool, "pool")
                                pool.tensor_copy(v_r, dirs[d](v_st)).then_inc(g_s.sem, g_s.one(f"v_{d}"))
                                pool.wait_ge(a_s.sem, a_s.at(f"neg_{d}", ct))
                                pool.tensor_tensor(kr[:, :, 1, :], by_chunk(dirs[d](r_st)), by_chunk(pos), ALU.mult).then_inc(g_s.sem, g_s.one(f"rP_{d}"))
                                pool.wait_ge(v_s.sem, v_s.at("b", ct))
                                pool.tensor_tensor(k_i, dirs[d](km), neg, ALU.mult).then_inc(g_s.sem, g_s.one(f"kI_{d}"))

                    @block.tensor
                    def _(pe):
                        pe.wait_ge(pre_a.sem, pre_a.at("gate"))
                        with fori(pe, 0, 4) as ct:
                            pe.wait_ge(a_s.sem, a_s.passes(ct))
                            pe.wait_ge(v_s.sem, v_s.passes(ct))
                            pe.wait_ge(g_s.sem, g_s.at("low", ct))
                            pe.matmul(banks[0], low[64:P, 2 * P:3 * P], tanh_ad[64:P, :], start=True, stop=True).then_inc(pe_s.sem, pe_s.one("a"))
                            for d in range(2):
                                pe.matmul(banks[1 + d], low[0:64, d * P:(d + 1) * P], tanh_ad[0:64, :],
                                                    start=True, stop=True).then_inc(pe_s.sem, pe_s.one(f"w{d}"))
                            pe.matmul(banks[3], low[:, 3 * P:4 * P], gate_in, start=True, stop=True).then_inc(pe_s.sem, pe_s.one("g"))
                            pe.wait_ge(a_s.sem, a_s.at("sq", ct))
                            pe.matmul(banks[4], blk, sq, start=True, stop=True).then_inc(pe_s.sem, pe_s.one("norm"))
                            pe.wait_ge(v_s.sem, v_s.at("rk", ct))
                            pe.matmul(banks[5], blk, rk, start=True, stop=True).then_inc(pe_s.sem, pe_s.one("bonus"))
                            for d in range(2):
                                for n, (src, s, name, before) in enumerate((
                                        (b_i, v_s, f"bI_{d}", (a_s, "a")), (k_i, g_s, f"kI_{d}", (a_s, "w0")),
                                        (v_r, g_s, f"v_{d}", (a_s, "w1")))):
                                    pe.wait_ge(s.sem, s.at(name, ct))
                                    pe.wait_ge(before[0].sem, before[0].at(before[1], ct))
                                    for c in range(NC):
                                        ins = pe.transpose(chunk(banks[n], c), chunk(src, c), ident)
                                    ins.then_inc(pe_s.sem, pe_s.one(("turn_b_%d", "turn_k_%d", "turn_v_%d")[n] % d))
                                pe.wait_ge(v_s.sem, v_s.at(f"kkP_{d}", ct))
                                pe.wait_ge(g_s.sem, g_s.at(f"rP_{d}", ct))
                                if d:
                                    pe.wait_ge(v_s.sem, v_s.at("bonus", ct))
                                for m, banks_of, src in (("ac", ((3, 4), (5, 6)), b_i), ("be", ((7, 0), (1, 2)), k_i)):
                                    for h in heads:
                                        for q in range(2):
                                            if m == "be":
                                                pe.wait_ge(a_s.sem, a_s.at(f"v_tok_{d}", ct))
                                            elif (h, q) == (1, 0):
                                                pe.wait_ge(v_s.sem, v_s.at("bonus", ct))
                                            elif d == 0:
                                                pe.wait_ge(a_s.sem, a_s.at("root" if q else "g", ct))
                                            elif (h, q) == (1, 1):
                                                pe.wait_ge(a_s.sem, a_s.at("out_0", ct))
                                            bank = banks[banks_of[h][q]].rearrange("p (c w) -> p c w", c=2)
                                            for e in range(2):
                                                c = 2 * q + e
                                                ins = pe.matmul(bank[:, e, :], chunk(src, c)[hs[h], :],
                                                                kr[hs[h], c, :, :], start=True, stop=True)
                                            ins.then_inc(pe_s.sem, pe_s.one(f"{m}{h}{q}_{d}"))
                                for h in heads:
                                    pe.wait_ge(v_s.sem, v_s.at(f"xt{h}_{d}", ct))
                                    for c in range(NC):
                                        ins = pe.transpose(chunk(banks[z_bank[h]], c), chunk(x_t[h], c), ident)
                                    ins.then_inc(pe_s.sem, pe_s.one(f"x{h}_{d}"))
                                for n in range(1, nl + 1):
                                    for h in heads:
                                        if n == 1:
                                            pe.wait_ge(a_s.sem, a_s.at(f"x{h}_{d}", ct))
                                        else:
                                            pe.wait_ge(v_s.sem, v_s.at(f"zt{n - 1}{h}_{d}", ct))
                                        for c in range(NC):
                                            ins = pe.matmul(chunk(banks[y_bank[h]], c), ac[h][:, c, 0, :], chunk(x_m[h], c),
                                                            start=True, stop=True)
                                        ins.then_inc(pe_s.sem, pe_s.one(f"y{n}{h}_{d}"))
                                    for h in heads:
                                        pe.wait_ge(a_s.sem, a_s.at(f"y{n}{h}_{d}", ct))
                                        if n < nl:
                                            for c in range(NC):
                                                ins = pe.matmul(chunk(banks[z_bank[h]], c), chunk(x_t[h], c), chunk(y_m[h], c),
                                                                start=True, stop=True)
                                            ins.then_inc(pe_s.sem, pe_s.one(f"z{n}{h}_{d}"))
                                        if n == 1:
                                            pe.wait_ge(v_s.sem, v_s.at(f"be11_{d}", ct))
                                        for c in range(NC):
                                            ins = pe.matmul(chunk(banks[zt_bank[h]], c), chunk(y_m[h], c), chunk(x_t[h], c),
                                                            start=True, stop=True)
                                        ins.then_inc(pe_s.sem, pe_s.one(f"zt{n}{h}_{d}"))
                                pe.wait_ge(v_s.sem, v_s.at(f"zt{nl}1_{d}", ct))
                                for c in range(NC):
                                    pe.wait_ge(v_s.sem, v_s.at(f"s{c - 1}_{d}" if c else f"zero_{d}", ct))
                                    pe.matmul(banks[1][:, 0:P], kr[:, c, 0, :], state, start=True, stop=False)
                                    for h in heads:
                                        ins = pe.matmul(banks[1][:, hs[h]], be[h][:, c, 0, :], chunk(v_tok, c)[:, hs[h]],
                                                        start=False, stop=h == 1)
                                    ins.then_inc(pe_s.sem, pe_s.one(f"rhs{c}_{d}"))
                                    pe.wait_ge(a_s.sem, a_s.at(f"rhs{c}_{d}", ct))
                                    for h in heads:
                                        ins = pe.matmul(banks[2][:, hs[h]], chunk(x_t[h], c), rhs[:, hs[h]], start=True, stop=True)
                                    ins.then_inc(pe_s.sem, pe_s.one(f"sa{c}_{d}"))
                                    pe.wait_ge(a_s.sem, a_s.at(f"sa{c}_{d}", ct))
                                    if c < NC - 1:
                                        pe.matmul(banks[4][:, 0:P], chunk(b_tok, c), sa, start=True, stop=False)
                                        pe.matmul(banks[4][:, 0:P], chunk(k_tok, c), chunk(v_tok, c),
                                                            start=False, stop=True).then_inc(pe_s.sem, pe_s.one(f"s{c}_{d}"))
                                    out = chunk(banks[out_bank], c)
                                    pe.matmul(out, state, kr[:, c, 1, :], start=True, stop=False)
                                    for h in heads:
                                        pe.matmul(out[hs[h], :], sa[:, hs[h]], ac[h][:, c, 1, :], start=False, stop=False)
                                        ins = pe.matmul(out[hs[h], :], chunk(v_tok, c)[:, hs[h]], be[h][:, c, 1, :],
                                                        start=False, stop=True)
                                    ins.then_inc(pe_s.sem, pe_s.one(f"o{c}_{d}"))
                            pe.wait_ge(v_s.sem, v_s.at("out_1", ct))
                            pe.matmul(banks[1], blk, o_t, start=True, stop=True).then_inc(pe_s.sem, pe_s.one("mean"))
                            pe.wait_ge(a_s.sem, a_s.at("osq", ct))
                            pe.matmul(banks[2], blk, sq, start=True, stop=True).then_inc(pe_s.sem, pe_s.one("var"))

                    @block.scalar
                    def _(act):
                        act.activation(tanh_ad[0:64, :], p3[0:64, 12, :], ACT.Tanh).then_inc(pre_a.sem, pre_a.one("tanh"))
                        act.activation(tanh_ad[64:P, :], p3[64:P, 12, :], ACT.Copy).then_inc(pre_a.sem, pre_a.one("ad"))
                        act.activation(gate_in, p3[:, 13, :], ACT.Sigmoid).then_inc(pre_a.sem, pre_a.one("gate"))
                        act.sem_inc(a_s.sem, 1)
                        with fori(act, 0, 4) as ct:
                            act.wait_ge(v_s.sem, v_s.passes(ct))
                            act.wait_ge(g_s.sem, g_s.at("vec", ct))
                            for name, bank, dst, bias in (("a", 0, a_t, "a0"), ("w0", 1, sg0, "w0f"), ("w1", 2, sg1, "w0b")):
                                act.wait_ge(pe_s.sem, pe_s.at(name, ct))
                                act.activation(dst, banks[bank], ACT.Sigmoid, bias=vcol(bias)).then_inc(a_s.sem, a_s.one(name))
                            act.wait_ge(pe_s.sem, pe_s.at("g", ct))
                            act.activation(g_t, banks[3], ACT.Copy).then_inc(a_s.sem, a_s.one("g"))
                            act.wait_ge(v_s.sem, v_s.at("km", ct))
                            act.activation(sq, kk, ACT.Square).then_inc(a_s.sem, a_s.one("sq"))
                            act.wait_ge(pe_s.sem, pe_s.at("norm", ct))
                            act.activation(sq, banks[4], ACT.Sqrt).then_inc(a_s.sem, a_s.one("root"))
                            for d in range(2):
                                act.wait_ge(v_s.sem, v_s.at(f"cex_{d}", ct))
                                act.activation(pos, cen, ACT.Exp, scale=-DECAY_SCALE).then_inc(a_s.sem, a_s.one(f"pos_{d}"))
                                act.activation(neg, cen, ACT.Exp, scale=DECAY_SCALE).then_inc(a_s.sem, a_s.one(f"neg_{d}"))
                                act.activation(prv, cex, ACT.Exp, scale=-DECAY_SCALE).then_inc(a_s.sem, a_s.one(f"prv_{d}"))
                                act.activation(mid, by_chunk(cum)[:, :, HD - 1], ACT.Exp, scale=-DECAY_SCALE).then_inc(a_s.sem, a_s.one(f"mid_{d}"))
                                for n, (name, dst, turned) in enumerate((("b_tok", b_tok, "turn_b"), ("k_tok", k_tok, "turn_k"),
                                                                         ("v_tok", v_tok, "turn_v"))):
                                    act.wait_ge(pe_s.sem, pe_s.at(f"{turned}_{d}", ct))
                                    act.activation(dst, banks[n], ACT.Copy).then_inc(a_s.sem, a_s.one(f"{name}_{d}"))
                                for h in heads:
                                    act.wait_ge(pe_s.sem, pe_s.at(f"x{h}_{d}", ct))
                                    act.activation(x_m[h], banks[z_bank[h]], ACT.Copy).then_inc(a_s.sem, a_s.one(f"x{h}_{d}"))
                                for n in range(1, nl + 1):
                                    for h in heads:
                                        act.wait_ge(pe_s.sem, pe_s.at(f"y{n}{h}_{d}", ct))
                                        act.activation(y_m[h], banks[y_bank[h]], ACT.Copy).then_inc(a_s.sem, a_s.one(f"y{n}{h}_{d}"))
                                for c in range(NC):
                                    act.wait_ge(pe_s.sem, pe_s.at(f"rhs{c}_{d}", ct))
                                    act.activation(rhs, banks[1][:, 0:P], ACT.Copy).then_inc(a_s.sem, a_s.one(f"rhs{c}_{d}"))
                                    act.wait_ge(pe_s.sem, pe_s.at(f"sa{c}_{d}", ct))
                                    if c:
                                        act.wait_ge(pe_s.sem, pe_s.at(f"o{c - 1}_{d}", ct))
                                    act.activation(sa, banks[2][:, 0:P], ACT.Copy).then_inc(a_s.sem, a_s.one(f"sa{c}_{d}"))
                                if d == 0:
                                    act.wait_ge(pe_s.sem, pe_s.at("o3_0", ct))
                                    act.activation(o_t, banks[out_bank], ACT.Copy).then_inc(a_s.sem, a_s.one("out_0"))
                            act.wait_ge(v_s.sem, v_s.at("centre", ct))
                            act.activation(sq, o_t, ACT.Square).then_inc(a_s.sem, a_s.one("osq"))
                            act.wait_ge(pe_s.sem, pe_s.at("var", ct))
                            act.activation(sq, banks[2], ACT.Sqrt, bias=col("gneps"), scale=1.0 / HD).then_inc(a_s.sem, a_s.one("oroot"))

                    @block.vector
                    def _(dve):
                        dve.sem_inc(v_s.sem, 1)
                        for h in heads:
                            dve.memset(ac[h], 0.0).then_inc(zero_s.sem, zero_s.one(f"ac{h}"))
                            dve.memset(be[h], 0.0).then_inc(zero_s.sem, zero_s.one(f"be{h}"))
                        dve.wait_ge(zero_s.sem, zero_s.at("be1"))
                        causal = table("strict", 2 * P).bitcast(U32)
                        with fori(dve, 0, 4) as ct:
                            k_in = proj[:, bass.ds(ct * T + 4 * T, T)]
                            dve.wait_ge(a_s.sem, a_s.passes(ct))
                            dve.wait_ge(g_s.sem, g_s.at("v", ct))
                            dve.tensor_scalar(kk, k_in, vcol("kk"), None, ALU.mult).then_inc(v_s.sem, v_s.one("kk0"))
                            dve.wait_ge(a_s.sem, a_s.at("a", ct))
                            dve.tensor_scalar(ka1, a_t, vcol("ka"), vcol("ka"), ALU.mult, ALU.subtract).then_inc(v_s.sem, v_s.one("ka"))
                            dve.wait_ge(v_s.sem, v_s.at("ka", ct))
                            dve.scalar_tensor_tensor(km, ka1, 1.0, k_in, ALU.add, ALU.mult).then_inc(v_s.sem, v_s.one("km"))
                            dve.wait_ge(v_s.sem, v_s.at("km", ct))
                            dve.scalar_tensor_tensor(rk, r_st, vcol("rk"), km, ALU.mult, ALU.mult).then_inc(v_s.sem, v_s.one("rk"))
                            dve.wait_ge(a_s.sem, a_s.at("root", ct))
                            dve.tensor_scalar(sq, sq, 1e-12, None, ALU.max).then_inc(v_s.sem, v_s.one("nmax"))
                            dve.wait_ge(v_s.sem, v_s.at("nmax", ct))
                            dve.reciprocal(sq, sq).then_inc(v_s.sem, v_s.one("ninv"))
                            dve.wait_ge(v_s.sem, v_s.at("ninv", ct))
                            dve.tensor_tensor(kk, kk, sq, ALU.mult).then_inc(v_s.sem, v_s.one("kk"))
                            dve.wait_ge(v_s.sem, v_s.at("kk", ct))
                            dve.tensor_tensor(b_t, kk, a_t, ALU.mult).then_inc(v_s.sem, v_s.one("b"))
                            dve.wait_ge(pe_s.sem, pe_s.at("bonus", ct))
                            dve.tensor_tensor(bonus, banks[5], v_st, ALU.mult).then_inc(v_s.sem, v_s.one("bonus"))
                            for d in range(2):
                                dve.tensor_tensor_scan(cum, table("reset", T), dirs[d](sg[d]), 0.0, ALU.mult, ALU.add).then_inc(v_s.sem, v_s.one(f"cum_{d}"))
                                dve.wait_ge(v_s.sem, v_s.at(f"cum_{d}", ct))
                                dve.tensor_tensor(by_chunk(cen), by_chunk(cum),
                                                           by_chunk(cum)[:, :, HD - 1:HD].broadcast_to([P, NC, P]), ALU.subtract).then_inc(v_s.sem, v_s.one(f"cen_{d}"))
                                dve.wait_ge(v_s.sem, v_s.at(f"cen_{d}", ct))
                                dve.tensor_tensor(cex, cen, dirs[d](sg[d]), ALU.subtract).then_inc(v_s.sem, v_s.one(f"cex_{d}"))
                                dve.wait_ge(a_s.sem, a_s.at(f"mid_{d}", ct))
                                if d:
                                    dve.wait_ge(pe_s.sem, pe_s.at("o3_0", ct))
                                dve.scalar_tensor_tensor(kr[:, :, 0, :], by_chunk(dirs[d](kk)), -1.0, by_chunk(prv),
                                                                  ALU.mult, ALU.mult).then_inc(v_s.sem, v_s.one(f"kkP_{d}"))
                                dve.tensor_tensor(b_i, dirs[d](b_t), neg, ALU.mult).then_inc(v_s.sem, v_s.one(f"bI_{d}"))
                                dve.tensor_tensor(carry[:, 0:3], by_chunk(pos)[:, 0:3, P - 1], mid[:, 1:4], ALU.mult).then_inc(v_s.sem, v_s.one(f"carry_{d}"))
                                dve.memset(state, 0.0).then_inc(v_s.sem, v_s.one(f"zero_{d}"))
                                for m, dst, bks in (("ac", ac, ((3, 4), (5, 6))), ("be", be, ((7, 0), (1, 2)))):
                                    for h in heads:
                                        for q in range(2):
                                            dve.wait_ge(pe_s.sem, pe_s.at(f"{m}{h}{q}_{d}", ct))
                                            hold(dve, "vec")
                                            dve.copy_predicated(
                                                dst[h][:, 2 * q:2 * q + 2, :, :].rearrange("p c w t -> p c (w t)"),
                                                causal.unsqueeze(1).broadcast_to([P, 2, 2 * P]),
                                                banks[bks[h][q]].rearrange("p (c w) -> p c w", c=2)).then_inc(v_s.sem, v_s.one(f"{m}{h}{q}_{d}"))
                                for h in heads:
                                    dve.wait_ge(v_s.sem, v_s.at(f"be11_{d}", ct))
                                    dve.tensor_tensor(by_chunk(x_t[h]), ac[h][:, :, 0, :],
                                                               over_chunks(table("up")), ALU.mult).then_inc(v_s.sem, v_s.one(f"xa{h}_{d}"))
                                    dve.wait_ge(v_s.sem, v_s.at(f"xa{h}_{d}", ct))
                                    dve.tensor_tensor(by_chunk(x_t[h]), by_chunk(x_t[h]), over_chunks(ident), ALU.add).then_inc(v_s.sem, v_s.one(f"xt{h}_{d}"))
                                for n in range(1, nl + 1):
                                    for h in heads:
                                        if n < nl:
                                            dve.wait_ge(pe_s.sem, pe_s.at(f"zt{n}{h}_{d}", ct))
                                            hold(dve, "vec")
                                            dve.copy_predicated(by_chunk(x_m[h]), over_chunks(table("low", P, n * P).bitcast(U32)),
                                                                         by_chunk(banks[z_bank[h]])).then_inc(v_s.sem, v_s.one(f"z{n}{h}_{d}"))
                                        dve.wait_ge(pe_s.sem, pe_s.at(f"zt{n}{h}_{d}", ct))
                                        hold(dve, "vec")
                                        dve.copy_predicated(by_chunk(x_t[h]), over_chunks(table("up", P, n * P).bitcast(U32)),
                                                                     by_chunk(banks[zt_bank[h]])).then_inc(v_s.sem, v_s.one(f"zt{n}{h}_{d}"))
                                for c in range(NC - 1):
                                    dve.wait_ge(pe_s.sem, pe_s.at(f"s{c}_{d}", ct))
                                    dve.tensor_tensor(added, banks[4][:, 0:P], state, ALU.add).then_inc(v_s.sem, v_s.one(f"add{c}_{d}"))
                                    dve.wait_ge(v_s.sem, v_s.at(f"add{c}_{d}", ct))
                                    dve.wait_ge(pe_s.sem, pe_s.at(f"o{c}_{d}", ct))
                                    dve.scalar_tensor_tensor(state, added, carry[:, c:c + 1], blk, ALU.mult, ALU.mult).then_inc(v_s.sem, v_s.one(f"s{c}_{d}"))
                                if d:
                                    dve.wait_ge(pe_s.sem, pe_s.at("o3_1", ct))
                                    dve.tensor_tensor(o_t, banks[out_bank][:, ::-1], o_t, ALU.add).then_inc(v_s.sem, v_s.one("out_1"))
                            dve.wait_ge(pe_s.sem, pe_s.at("mean", ct))
                            dve.scalar_tensor_tensor(o_t, banks[1], -1.0 / HD, o_t, ALU.mult, ALU.add).then_inc(v_s.sem, v_s.one("centre"))
                            dve.wait_ge(a_s.sem, a_s.at("oroot", ct))
                            dve.reciprocal(sq, sq).then_inc(v_s.sem, v_s.one("oinv"))
                            dve.wait_ge(v_s.sem, v_s.at("oinv", ct))
                            dve.tensor_tensor(o_t, o_t, sq, ALU.mult).then_inc(v_s.sem, v_s.one("on"))
                            dve.wait_ge(v_s.sem, v_s.at("on", ct))
                            dve.tensor_scalar(o_t, o_t, vcol("gnw"), vcol("gnb"), ALU.mult, ALU.add).then_inc(v_s.sem, v_s.one("og"))
                            dve.wait_ge(v_s.sem, v_s.at("og", ct))
                            dve.tensor_tensor(o_t, o_t, bonus, ALU.add).then_inc(v_s.sem, v_s.one("ob"))
                            dve.wait_ge(v_s.sem, v_s.at("ob", ct))
                            dve.tensor_tensor(hT[:, bass.ds(ct * T, T)], o_t, g_t, ALU.mult).then_inc(v_s.sem, v_s.one("res"))

        rwkv()
        add_to_residual("mix0_out", dram["ab_out"], h3, KD, None)

        def cross_attention(n):
            kT, vt, memn = work[:, 1024:3072], work[:, 3072:5120], work[:, 5120:7168]
            k3 = kT.rearrange("p (n m) -> p n m", m=MEM)
            v3 = vt.rearrange("p (b d) -> p b d", b=2)
            memn3 = memn.rearrange("p (n m) -> p n m", m=MEM)
            wk = Projection(dram[f"wk{n}"], memn3, KD, n=MEM)
            wv = Projection(dram[f"wv{n}"], memn3, 4, token_major=True)
            wq = Projection(dram[f"wq{n}"], h3, KD)
            wo = Projection(dram[f"wo{n}"], h3, KD)
            rms_norm(f"norm_mem{n}", mem3, memn3, MEM, f"mem{n}", following=wk)
            project(f"keys{n}", wk, vector=lambda dve, i, u, bank: dve.tensor_copy(
                kT[:, bass.ds(i * (2 * MEM) + u * MEM, MEM)], bank[:, 0:MEM]), following=wv)
            project(f"values{n}", wv, vector=lambda dve, i, u, bank: dve.tensor_copy(
                v3[:, :, bass.ds(i * 512 + u * 256, 256)], bank.rearrange("p (b d) -> p b d", b=2)))
            rms_norm(f"norm_xa{n}", x3, h3, T, f"xa{n}", following=wq)
            project(f"queries{n}", wq, scalar=lambda act, i, u, bank: act.activation(
                proj[:, bass.ds(i * (2 * T) + u * T, T)], bank, ACT.Copy, scale=1.0 / 16), reader="a")

            o = KD * T
            q_h, k_h, v_h = proj[:, o:o + 1024], proj[:, o + 1024:o + 1536], proj[:, o + 1536:o + 2048]
            prob = proj[:, o + 2048:o + 3072].rearrange("p (c m) -> p c m", c=NC)
            prob_t = proj[:, o + 3072:o + 4096].rearrange("p (b t) -> p b t", b=2)
            top, total = proj[:, o + 4096:o + 4100], proj[:, o + 4104:o + 4108]
            with ExitStack() as scope:
                pe_s, a_s, v_s, g_s = steps(
                    scope, **{f"xa{n}_pe": ["^", "s0", "s1", "turn0", "turn1", "o0", "o1"],
                              f"xa{n}_act": ["^"] + [f"exp{c}" for c in range(NC)] + ["p0", "o0", "o1"],
                              f"xa{n}_vec": ["^", "top0", "top1", "minus", "total", "prob", "p1"],
                              f"xa{n}_pool": ["^", "q", "k", "v"]})
                with nc.Block() as block:
                    @block.sync
                    def _(sp):
                        wo.prefetch(sp)

                    @block.gpsimd
                    def _(pool):
                        pool.sem_inc(g_s.sem, 1)
                        with fori(pool, 0, 4) as h:
                            pool.wait_ge(pe_s.sem, pe_s.passes(h))
                            hold(pool, "pool")
                            pool.tensor_copy(q_h, proj[:, bass.ds(h * (2 * T), 2 * T)]).then_inc(g_s.sem, g_s.one("q"))
                            pool.tensor_copy(k_h, kT[:, bass.ds(h * (2 * MEM), 2 * MEM)]).then_inc(g_s.sem, g_s.one("k"))
                            pool.tensor_copy(v_h.rearrange("p (b d) -> p b d", b=2), v3[:, :, bass.ds(h * 256, 256)]).then_inc(g_s.sem, g_s.one("v"))

                    @block.tensor
                    def _(pe):
                        pe.sem_inc(pe_s.sem, 1)
                        with fori(pe, 0, 4) as h:
                            pe.wait_ge(g_s.sem, g_s.at("k", h))
                            pe.wait_ge(a_s.sem, a_s.passes(h))
                            pe.wait_ge(v_s.sem, v_s.passes(h))
                            for c in range(NC):
                                for k in range(2):
                                    ins = pe.matmul(banks[c // 2][:, (c % 2) * MEM:(c % 2 + 1) * MEM],
                                                    q_h[:, k * T + c * P:k * T + (c + 1) * P], k_h[:, k * MEM:(k + 1) * MEM],
                                                    start=k == 0, stop=k == 1)
                                if c % 2:
                                    ins.then_inc(pe_s.sem, pe_s.one(f"s{c // 2}"))
                            pe.wait_ge(v_s.sem, v_s.at("prob", h))
                            for b in range(2):
                                for c in range(NC):
                                    ins = pe.transpose(chunk(banks[2 + b], c), prob[:, c, b * P:(b + 1) * P], ident)
                                ins.then_inc(pe_s.sem, pe_s.one(f"turn{b}"))
                            pe.wait_ge(g_s.sem, g_s.at("v", h))
                            pe.wait_ge(a_s.sem, a_s.at("p0", h))
                            pe.wait_ge(v_s.sem, v_s.at("p1", h))
                            for d in range(2):
                                for b in range(2):
                                    ins = pe.matmul(banks[4 + d], v_h[:, b * 256 + d * P:b * 256 + (d + 1) * P],
                                                    prob_t[:, b, :], start=b == 0, stop=b == 1)
                                ins.then_inc(pe_s.sem, pe_s.one(f"o{d}"))

                    @block.vector
                    def _(dve):
                        dve.sem_inc(v_s.sem, 1)
                        with fori(dve, 0, 4) as h:
                            dve.wait_ge(a_s.sem, a_s.passes(h))
                            for b in range(2):
                                dve.wait_ge(pe_s.sem, pe_s.at(f"s{b}", h))
                                dve.tensor_reduce(top[:, 2 * b:2 * b + 2], banks[b].rearrange("p (c m) -> p c m", c=2),
                                                           AXX, ALU.max).then_inc(v_s.sem, v_s.one(f"top{b}"))
                            dve.wait_ge(v_s.sem, v_s.at("top1", h))
                            dve.tensor_scalar(top, top, -1.0, None, ALU.mult).then_inc(v_s.sem, v_s.one("minus"))
                            dve.wait_ge(a_s.sem, a_s.at("exp3", h))
                            dve.reciprocal(total, total).then_inc(v_s.sem, v_s.one("total"))
                            dve.wait_ge(v_s.sem, v_s.at("total", h))
                            dve.tensor_tensor(prob, prob, total.unsqueeze(2).broadcast_to([P, NC, MEM]), ALU.mult).then_inc(v_s.sem, v_s.one("prob"))
                            dve.wait_ge(pe_s.sem, pe_s.at("turn1", h))
                            dve.tensor_copy(prob_t[:, 1, :], banks[3]).then_inc(v_s.sem, v_s.one("p1"))

                    @block.scalar
                    def _(act):
                        act.sem_inc(a_s.sem, 1)
                        with fori(act, 0, 4) as h:
                            act.wait_ge(pe_s.sem, pe_s.passes(h))
                            act.wait_ge(v_s.sem, v_s.at("minus", h))
                            for c in range(NC):
                                act.activation(prob[:, c, :], banks[c // 2][:, (c % 2) * MEM:(c % 2 + 1) * MEM],
                                                        ACT.Exp, bias=top[:, c:c + 1], accum_out=total[:, c:c + 1]).then_inc(a_s.sem, a_s.one(f"exp{c}"))
                            act.wait_ge(pe_s.sem, pe_s.at("turn0", h))
                            act.activation(prob_t[:, 0, :], banks[2], ACT.Copy).then_inc(a_s.sem, a_s.one("p0"))
                            for d in range(2):
                                act.wait_ge(pe_s.sem, pe_s.at(f"o{d}", h))
                                act.activation(hT[:, bass.ds(h * (2 * T) + d * T, T)], banks[4 + d], ACT.Copy).then_inc(a_s.sem, a_s.one(f"o{d}"))
            add_to_residual(f"xa_out{n}", dram[f"wo{n}"], h3, KD, None)

        def swiglu(n):
            w_in = Projection(dram[f"f_in{n}"], h3, 2 * FT)
            a3 = proj[:, 0:FT * T].rearrange("p (n t) -> p n t", t=T)
            w_out = Projection(dram[f"f_out{n}"], a3, KD, k=FT)
            silu = work[:, 1024:1536]
            rms_norm(f"norm_ffn{n}", x3, h3, T, f"ffn{n}", following=w_in)
            with ExitStack() as scope:
                pe_s, a_s, v_s = steps(scope, **{f"ffn{n}_tile": ["tile0", "tile1"], f"ffn{n}_act": ["silu"],
                                                 f"ffn{n}_vec": ["^", "gated"]})
                with nc.Block() as block:
                    @block.sync
                    def _(sp):
                        w_in.load_rest(sp, pe_s, w_out)

                    @block.tensor
                    def _(pe):
                        w_in.multiply(pe, pe_s, lambda e, u, i: e.wait_ge(v_s.sem, v_s.at("gated", i)) if u else e.wait_ge(a_s.sem, a_s.at("silu", i)))

                    @block.scalar
                    def _(act):
                        with fori(act, 0, FT) as i:
                            act.wait_ge(pe_s.sem, pe_s.at("tile0", i))
                            act.wait_ge(v_s.sem, v_s.passes(i))
                            act.activation(silu, banks[0], ACT.Silu).then_inc(a_s.sem, a_s.one("silu"))

                    @block.vector
                    def _(dve):
                        dve.sem_inc(v_s.sem, 1)
                        with fori(dve, 0, FT) as i:
                            dve.wait_ge(a_s.sem, a_s.at("silu", i))
                            dve.wait_ge(pe_s.sem, pe_s.at("tile1", i))
                            dve.tensor_tensor(proj[:, bass.ds(i * T, T)], silu, banks[1], ALU.mult).then_inc(v_s.sem, v_s.one("gated"))
                ring.used(FT)
            add_to_residual(f"ffn_out{n}", dram[f"f_out{n}"], a3, FT, None)

        def hgrn_projection():
            pr = Projection(dram["hg_in"], h3, 5 * HEADS)
            funcs = [(4, ACT.Copy), (8, ACT.Sigmoid), (4, ACT.Copy), (4, ACT.Silu)]
            with ExitStack() as scope:
                pe_s, a_s = steps(scope, hg_tile=["tile0", "tile1"], hg_emptied=["a0", "a1"])
                with nc.Block() as block:
                    @block.sync
                    def _(sp):
                        pr.load_rest(sp, pe_s, None)

                    @block.tensor
                    def _(pe):
                        pr.multiply(pe, pe_s, lambda e, u, i: e.wait_ge(a_s.sem, a_s.at(f"a{u}", i)))

                    @block.scalar
                    def _(act):
                        done = 0
                        for passes, func in funcs:
                            with fori(act, done, done + passes) as i:
                                for u in range(2):
                                    act.wait_ge(pe_s.sem, pe_s.at(f"tile{u}", i))
                                    act.activation(proj[:, bass.ds(i * (2 * T) + u * T, T)], banks[u], func).then_inc(a_s.sem, a_s.one(f"a{u}"))
                            done += passes
                ring.used(5 * HEADS // 2)

        def hgrn():
            nl = len(LEVELS)
            low_b, rest_b = work[:, 0:8], work[:, 8:16]
            base = 1024

            def take(words):
                nonlocal base
                base += words
                return work[:, base - words:base]

            q_st, g_st, i_st, f0 = take(T), take(T), take(T), take(T)
            i_b, q_d = take(T), [q_st, take(T)]
            i_d = [i_st, i_b]
            qp = [take(T), take(T)]
            ks = [take(T), take(T)]
            tot = [take(T), take(T)]
            att = [take(T), take(T)]
            k_tok, v_tok = take(T), take(T)
            states = take(3 * P)
            tot2 = [take(256), take(256)]
            o_t, sq = [slots[u][:, KD * P:KD * P + T] for u in range(2)]
            mid_b = [slots[u][:, KD * P + T:KD * P + 2 * T] for u in range(2)]
            inv = slots[0][:, KD * P + 2 * T:KD * P + 3 * T]
            m_bank = [[0, 1], [2, 3]]

            def both(names):
                return [n % d for d in range(2) for n in names]

            lvl = [f"{k}{n}_{d}" for n in range(nl) for d in range(2) for k in ("m",)]
            with ExitStack() as scope:
                pre_v, pre_a = steps(scope, hg_pre_vec=["top", "d0", "d1", "sum", "inv", "low", "rest"], hg_pre_act=["e0", "e1"])
                pe_s, a_s, v_s, g_s = steps(
                    scope,
                    hg_pe=["diag_0", "diag_1"] + [f"m{n}_{d}" for n in range(nl) for d in range(2)]
                    + both(["turn_v_%d", "turn_k_%d", "add_%d", "o_%d"]) + ["sum"],
                    hg_act=["^", "q", "i"] + both(["v_tok_%d", "k_tok_%d"] ) + ["o", "osq", "root"],
                    hg_vec=["^"] + [f"{k}_{d}" for d in range(2) for k in ("gate", "tot", "ks", "qp")] + ["diag_0", "diag_1"]
                    + [f"{k}{n}_{d}" for n in range(nl) for d in range(2) for k in ("m", "q", "k", "t")]
                    + [f"{k}_{d}" for d in range(2) for k in ("st0", "st1", "st2")] + ["o", "inv", "norm", "out"],
                    hg_pool=["^", "q_1", "i_1", "g"])
                with nc.Block() as block:
                    @block.sync
                    def _(sp):
                        Projection(dram["hg_out"], h3, KD).prefetch(sp)

                    @block.gpsimd
                    def _(pool):
                        pool.sem_inc(g_s.sem, 1)
                        with fori(pool, 0, HEADS) as h:
                            pool.wait_ge(v_s.sem, v_s.passes(h))
                            pool.wait_ge(a_s.sem, a_s.at("q", h))
                            hold(pool, "pool")
                            pool.tensor_copy(q_d[1], q_st[:, ::-1]).then_inc(g_s.sem, g_s.one("q_1"))
                            pool.wait_ge(a_s.sem, a_s.at("i", h))
                            hold(pool, "pool")
                            pool.tensor_copy(i_b, i_st[:, ::-1]).then_inc(g_s.sem, g_s.one("i_1"))
                            pool.tensor_copy(g_st, proj[:, bass.ds(h * T + 32 * T, T)]).then_inc(g_s.sem, g_s.one("g"))

                    @block.scalar
                    def _(act):
                        act.wait_ge(pre_v.sem, pre_v.at("d1"))
                        act.activation(low_b, low_b, ACT.Exp).then_inc(pre_a.sem, pre_a.one("e0"))
                        act.activation(rest_b, rest_b, ACT.Exp).then_inc(pre_a.sem, pre_a.one("e1"))
                        act.sem_inc(a_s.sem, 1)
                        with fori(act, 0, HEADS) as h:
                            act.wait_ge(v_s.sem, v_s.passes(h))
                            act.activation(q_st, proj[:, bass.ds(h * T, T)], ACT.Copy).then_inc(a_s.sem, a_s.one("q"))
                            act.activation(i_st, proj[:, bass.ds(h * T + 24 * T, T)], ACT.Copy).then_inc(a_s.sem, a_s.one("i"))
                            for d in range(2):
                                act.wait_ge(pe_s.sem, pe_s.at(f"turn_v_{d}", h))
                                if d:
                                    act.wait_ge(pe_s.sem, pe_s.at("o_0", h))
                                act.activation(v_tok, banks[4], ACT.Copy).then_inc(a_s.sem, a_s.one(f"v_tok_{d}"))
                                act.wait_ge(pe_s.sem, pe_s.at(f"turn_k_{d}", h))
                                act.activation(k_tok, banks[5], ACT.Copy).then_inc(a_s.sem, a_s.one(f"k_tok_{d}"))
                                if d == 0:
                                    pass
                            act.wait_ge(pe_s.sem, pe_s.at("o_0", h))
                            act.activation(o_t, banks[7], ACT.Copy).then_inc(a_s.sem, a_s.one("o"))
                            act.wait_ge(v_s.sem, v_s.at("o", h))
                            act.activation(sq, o_t, ACT.Square).then_inc(a_s.sem, a_s.one("osq"))
                            act.wait_ge(pe_s.sem, pe_s.at("sum", h))
                            act.activation(sq, banks[5], ACT.Sqrt, bias=col("eps"), scale=1.0 / P).then_inc(a_s.sem, a_s.one("root"))

                    @block.tensor
                    def _(pe):
                        with fori(pe, 0, HEADS) as h:
                            pe.wait_ge(a_s.sem, a_s.passes(h))
                            pe.wait_ge(v_s.sem, v_s.passes(h))
                            pe.wait_ge(a_s.sem, a_s.at("i", h))
                            for d in range(2):
                                pe.wait_ge(v_s.sem, v_s.at(f"ks_{d}", h))
                                if d:
                                    pe.wait_ge(g_s.sem, g_s.at("q_1", h))
                                for c in range(NC):
                                    ins = pe.matmul(chunk(banks[d], c), chunk(ks[d], c), chunk(q_d[d], c), start=True, stop=True)
                                ins.then_inc(pe_s.sem, pe_s.one(f"diag_{d}"))
                            for n in range(nl):
                                for d in range(2):
                                    if n == 0:
                                        pe.wait_ge(v_s.sem, v_s.at(f"qp_{d}", h))
                                    else:
                                        pe.wait_ge(v_s.sem, v_s.at(f"k{n - 1}_{d}", h))
                                    for c in range(NC):
                                        ins = pe.matmul(chunk(banks[m_bank[n % 2 == 0][d]], c), chunk(ks[d], c), chunk(qp[d], c),
                                                        start=True, stop=True)
                                    ins.then_inc(pe_s.sem, pe_s.one(f"m{n}_{d}"))
                            for d in range(2):
                                if d:
                                    pe.wait_ge(g_s.sem, g_s.at("i_1", h))
                                    pe.wait_ge(a_s.sem, a_s.at("k_tok_0", h))
                                for c in range(NC):
                                    ins = pe.transpose(chunk(banks[4], c), chunk(i_d[d], c), ident)
                                ins.then_inc(pe_s.sem, pe_s.one(f"turn_v_{d}"))
                                pe.wait_ge(v_s.sem, v_s.at(f"k{nl - 1}_{d}", h))
                                for c in range(NC):
                                    ins = pe.transpose(chunk(banks[5], c), chunk(ks[d], c), ident)
                                ins.then_inc(pe_s.sem, pe_s.one(f"turn_k_{d}"))
                                pe.wait_ge(a_s.sem, a_s.at(f"k_tok_{d}", h))
                                if d:
                                    pe.wait_ge(v_s.sem, v_s.at("st2_0", h))
                                for c in range(NC - 1):
                                    ins = pe.matmul(chunk(banks[6], c), chunk(k_tok, c), chunk(v_tok, c), start=True, stop=True)
                                ins.then_inc(pe_s.sem, pe_s.one(f"add_{d}"))
                                pe.wait_ge(v_s.sem, v_s.at(f"st2_{d}", h))
                                for c in range(NC):
                                    out = chunk(banks[7 if d == 0 else 4], c)
                                    ins = pe.matmul(out, chunk(v_tok, c), chunk(att[d], c), start=True, stop=c == 0)
                                    if c:
                                        ins = pe.matmul(out, chunk(states, c - 1), chunk(qp[d], c), start=False, stop=True)
                                ins.then_inc(pe_s.sem, pe_s.one(f"o_{d}"))
                            pe.wait_ge(a_s.sem, a_s.at("osq", h))
                            pe.matmul(banks[5], ones, sq, start=True, stop=True).then_inc(pe_s.sem, pe_s.one("sum"))

                    @block.vector
                    def _(dve):
                        l0, l1 = col("lb0", 0, 8), col("lb1", 0, 8)
                        dve.tensor_tensor(inv[:, 0:8], l0, l1, ALU.max).then_inc(pre_v.sem, pre_v.one("top"))
                        dve.wait_ge(pre_v.sem, pre_v.at("top"))
                        dve.tensor_tensor(rest_b, l0, inv[:, 0:8], ALU.subtract).then_inc(pre_v.sem, pre_v.one("d0"))
                        dve.tensor_tensor(low_b, l1, inv[:, 0:8], ALU.subtract).then_inc(pre_v.sem, pre_v.one("d1"))
                        dve.wait_ge(pre_a.sem, pre_a.at("e1"))
                        dve.tensor_tensor(rest_b, low_b, rest_b, ALU.add).then_inc(pre_v.sem, pre_v.one("sum"))
                        dve.wait_ge(pre_v.sem, pre_v.at("sum"))
                        dve.reciprocal(rest_b, rest_b).then_inc(pre_v.sem, pre_v.one("inv"))
                        dve.wait_ge(pre_v.sem, pre_v.at("inv"))
                        dve.tensor_tensor(low_b, low_b, rest_b, ALU.mult).then_inc(pre_v.sem, pre_v.one("low"))
                        dve.wait_ge(pre_v.sem, pre_v.at("low"))
                        dve.tensor_scalar(rest_b, low_b, -1.0, 1.0, ALU.mult, ALU.add).then_inc(pre_v.sem, pre_v.one("rest"))
                        dve.wait_ge(pre_v.sem, pre_v.at("rest"))
                        dve.sem_inc(v_s.sem, 1)
                        with fori(dve, 0, HEADS) as h:
                            dve.wait_ge(a_s.sem, a_s.passes(h))
                            for d in range(2):
                                if d:
                                    dve.wait_ge(v_s.sem, v_s.at("ks_0", h))
                                dve.tensor_scalar(f0, proj[:, bass.ds(h * T + (8 + 8 * d) * T, T)], rest_b[:, bass.ds(h, 1)],
                                                           low_b[:, bass.ds(h, 1)], ALU.mult, ALU.add).then_inc(v_s.sem, v_s.one(f"gate_{d}"))
                                dve.wait_ge(v_s.sem, v_s.at(f"gate_{d}", h))
                                dve.tensor_copy(tot[d], dirs[d](f0)).then_inc(v_s.sem, v_s.one(f"tot_{d}"))
                                dve.tensor_scalar(ks[d], dirs[d](f0), -1.0, 1.0, ALU.mult, ALU.add).then_inc(v_s.sem, v_s.one(f"ks_{d}"))
                                if d:
                                    dve.wait_ge(g_s.sem, g_s.at("q_1", h))
                                else:
                                    dve.wait_ge(a_s.sem, a_s.at("q", h))
                                dve.wait_ge(v_s.sem, v_s.at(f"tot_{d}", h))
                                dve.tensor_tensor(qp[d], q_d[d], tot[d], ALU.mult).then_inc(v_s.sem, v_s.one(f"qp_{d}"))
                            for d in range(2):
                                dve.wait_ge(pe_s.sem, pe_s.at(f"diag_{d}", h))
                                dve.tensor_tensor(by_chunk(att[d]), by_chunk(banks[d]), over_chunks(ident), ALU.mult).then_inc(v_s.sem, v_s.one(f"diag_{d}"))
                            for n, b in enumerate(LEVELS):
                                pairs = T // (2 * b)
                                for d in range(2):
                                    dve.wait_ge(pe_s.sem, pe_s.at(f"m{n}_{d}", h))
                                    dve.wait_ge(v_s.sem, v_s.at(f"m{n - 1}_{d}" if n else f"diag_{d}", h))
                                    hold(dve, "vec")
                                    dve.copy_predicated(by_chunk(att[d]), over_chunks(table("up", P, n * P).bitcast(U32)),
                                                                 by_chunk(banks[m_bank[n % 2 == 0][d]])).then_inc(v_s.sem, v_s.one(f"m{n}_{d}"))
                                    now = (tot, tot2, mid_b)
                                    t_in = tot[d] if n % 2 == 0 else tot2[d]
                                    t_out = tot2[d] if n % 2 == 0 else tot[d]
                                    t_in = t_in[:, 0:2 * pairs].rearrange("p (n two) -> p n two", two=2)
                                    q4 = qp[d].rearrange("p (n two b) -> p n two b", two=2, b=b)[:, :, 1, :]
                                    k4 = ks[d].rearrange("p (n two b) -> p n two b", two=2, b=b)[:, :, 0, :]
                                    if n:
                                        dve.wait_ge(v_s.sem, v_s.at(f"t{n - 1}_{d}", h))
                                    dve.tensor_tensor(q4, q4, t_in[:, :, 0:1].broadcast_to([P, pairs, b]), ALU.mult).then_inc(v_s.sem, v_s.one(f"q{n}_{d}"))
                                    dve.tensor_tensor(k4, k4, t_in[:, :, 1:2].broadcast_to([P, pairs, b]), ALU.mult).then_inc(v_s.sem, v_s.one(f"k{n}_{d}"))
                                    dve.tensor_tensor(t_out[:, 0:pairs], t_in[:, :, 0], t_in[:, :, 1], ALU.mult).then_inc(v_s.sem, v_s.one(f"t{n}_{d}"))
                            for d in range(2):
                                whole = tot2[d] if nl % 2 else tot[d]
                                dve.wait_ge(pe_s.sem, pe_s.at(f"add_{d}", h))
                                if d:
                                    dve.wait_ge(pe_s.sem, pe_s.at("o_0", h))
                                dve.tensor_copy(chunk(states, 0), chunk(banks[6], 0)).then_inc(v_s.sem, v_s.one(f"st0_{d}"))
                                for c in (1, 2):
                                    dve.wait_ge(v_s.sem, v_s.at(f"st{c - 1}_{d}", h))
                                    dve.scalar_tensor_tensor(chunk(states, c), chunk(states, c - 1), whole[:, c:c + 1],
                                                                      chunk(banks[6], c), ALU.mult, ALU.add).then_inc(v_s.sem, v_s.one(f"st{c}_{d}"))
                            dve.wait_ge(a_s.sem, a_s.at("o", h))
                            dve.wait_ge(pe_s.sem, pe_s.at("o_1", h))
                            dve.tensor_tensor(o_t, banks[4][:, ::-1], o_t, ALU.add).then_inc(v_s.sem, v_s.one("o"))
                            dve.wait_ge(a_s.sem, a_s.at("root", h))
                            dve.reciprocal(inv, sq).then_inc(v_s.sem, v_s.one("inv"))
                            dve.wait_ge(v_s.sem, v_s.at("inv", h))
                            dve.scalar_tensor_tensor(o_t, o_t, cols[:, bass.ds(h + COL["hgw"], 1)], inv,
                                                              ALU.mult, ALU.mult).then_inc(v_s.sem, v_s.one("norm"))
                            dve.wait_ge(v_s.sem, v_s.at("norm", h))
                            dve.wait_ge(g_s.sem, g_s.at("g", h))
                            dve.tensor_tensor(hT[:, bass.ds(h * T, T)], o_t, g_st, ALU.mult).then_inc(v_s.sem, v_s.one("out"))

        cross_attention(0)
        swiglu(0)
        rms_norm("norm_mix1", x3, h3, T, "mix1", following=Projection(dram["hg_in"], h3, 5 * HEADS))
        hgrn_projection()
        hgrn()
        add_to_residual("mix1_out", dram["hg_out"], h3, KD, None)
        cross_attention(1)
        swiglu(1)
        rms_norm("norm_final", x3, h3, T, "final", store=out_d)


def tiles(w, width=P):
    k, n = w.shape
    return np.ascontiguousarray(w.reshape(k // P, P, n // width, width).transpose(2, 1, 0, 3).reshape(n // width, P, -1))


def channels(v):
    return v.reshape(-1, P).T


def kernel(**inputs):
    import concourse.bacc as bacc
    from concourse.bass_utils import run_bass_kernel_spmd as run

    a = {k: np.asarray(v) for k, v in inputs.items()}
    f = np.float32
    ab = a["ab_w_in"][0]
    z0 = RW_TILES * P
    order = np.concatenate([ab[:, :z0], ab[:, z0 + 512:z0 + 1536], ab[:, z0:z0 + 512]], axis=1)
    dtw = ab[:, z0 + 1536:].reshape(KD, P, 8).transpose(1, 0, 2).reshape(P, 64)
    zero = np.zeros((64, 512), f)
    lora = np.concatenate([
        dtw,
        np.concatenate([a["rw_w2"][0, 0], zero]).reshape(P, 512), np.concatenate([a["rw_w2"][0, 1], zero]),
        np.concatenate([zero, a["rw_a2"][0]]), a["rw_g2"][0]], axis=1)

    tri = np.arange(P)
    up, low = tri[:, None] < tri[None, :], tri[:, None] > tri[None, :]
    eye = np.eye(P, dtype=f)
    head = (tri[:, None] // HD == tri[None, :] // HD).astype(f)
    levels = [((tri[:, None] // b) % 2 == 0) & (tri[None, :] // b == tri[:, None] // b + 1) for b in LEVELS]
    reset = np.ones((P, T), f)
    reset[:, ::P] = 0.0
    tab = np.concatenate([eye, np.ones((P, P), f), head, up.astype(f), (up | (eye > 0)).astype(f), reset] + [m.astype(f) for m in levels]
                         + [m.T.astype(f) for m in levels], axis=1)

    cols = np.zeros((P, NCOLS), f)

    def put(name, block):
        cols[0:block.shape[0], COL[name]:COL[name] + block.shape[1]] = block

    put("one", np.ones((P, 1), f))
    put("eps", np.full((P, 1), 1e-6, f))
    put("gneps", np.full((P, 1), 64e-5, f))
    for n in range(2):
        put(f"mix{n}", channels(a["mix_norm"][n]))
        put(f"xa{n}", channels(a["xa_norm"][n]))
        put(f"mem{n}", channels(a["mem_norm"][n]))
        put(f"ffn{n}", channels(a["ffn_norm"][n]))
        put(f"lb{n}", channels(a["hg_lb"][n]))
    put("final", channels(a["final_norm"]))
    put("mu", channels(a["rw_mu"][0]))
    taps = [channels(v) for v in (*a["ssd_conv_w"][0], a["ssd_conv_b"][0])]
    put("taps", np.stack(taps, axis=2).reshape(P, 32))
    vecs = [a["rw_w0"][0, 0], a["rw_w0"][0, 1], a["rw_a0"][0], a["rw_k_k"][0], a["rw_k_a"][0],
            a["rw_r_k"][0].reshape(-1), a["rw_gn_w"][0], a["rw_gn_b"][0]]
    put("rw", np.stack([channels(v) for v in vecs], axis=2).reshape(P, -1))
    put("ssd_d", channels(np.repeat(a["ssd_d"][0], HD)))
    put("ssd_w", channels(a["ssd_norm_w"][0]))
    put("hgw", channels(a["hg_norm_w"][0]))
    put("dtb", a["ssd_dt_bias"][0].T)
    put("alog", a["ssd_a_log"][0].T)

    arrays = {
        "xT": np.ascontiguousarray(a["x"][0].T.reshape(KD, P, T).transpose(1, 0, 2).reshape(P, -1)),
        "memT": np.ascontiguousarray(a["mem"][0].T.reshape(KD, P, MEM).transpose(1, 0, 2).reshape(P, -1)),
        "tab": tab, "cols": cols, "lora": np.ascontiguousarray(lora),
        "ab_in": tiles(order), "ab_out": tiles(a["ab_w_out"][0]),
        "hg_in": tiles(a["hg_w_in"][0]), "hg_out": tiles(a["hg_w_out"][0]),
    }
    for n in range(2):
        arrays[f"wq{n}"] = tiles(a["xa_wq"][n])
        arrays[f"wk{n}"] = tiles(a["xa_wkv"][n][:, :D])
        arrays[f"wv{n}"] = tiles(a["xa_wkv"][n][:, D:], 256)
        arrays[f"wo{n}"] = tiles(a["xa_wo"][n])
        w = a["ffn_w_in"][n]
        arrays[f"f_in{n}"] = tiles(np.ascontiguousarray(w.reshape(D, 2, FT, P).transpose(0, 2, 1, 3)).reshape(D, 2 * FFN))
        arrays[f"f_out{n}"] = tiles(a["ffn_w_out"][n])

    nc = bacc.Bacc("TRN2", target_bir_lowering=False, num_devices=1)
    dram = {k: nc.dram_tensor("in_" + k, v.shape, F32, kind="ExternalInput").ap() for k, v in arrays.items()}
    out_d = nc.dram_tensor("out_yT", (P, KD, T), F32, kind="ExternalOutput").ap()
    scratch_d = nc.dram_tensor("scratch_cum", (2 * 8 * T,), F32, kind="Internal").ap()
    build_program(nc, dram, out_d, scratch_d)
    r = run(nc, [{"in_" + k: v for k, v in arrays.items()}], core_ids=[0])
    y = r.results[0]["out_yT"]
    return np.ascontiguousarray(y.transpose(1, 0, 2).reshape(D, T).T.reshape(1, T, D))
```

```python
from contextlib import ExitStack

import numpy as np
import concourse.bass as bass
from concourse import mybir

F32 = mybir.dt.float32
F32R = mybir.dt.float32r
U32 = mybir.dt.uint32
ALU = mybir.AluOpType
ACT = mybir.ActivationFunctionType
AXX = mybir.AxisListType.X

P = 128
D, T, MEM = 1024, 512, 256
KD = D // P
NC = T // P
HD = 64
RW_TILES = 14
XBC_TILES = 8
Z_TILES = 4
XS0, B0, C0, Z0, REV0 = 14, 18, 20, 22, 26
HEADS = 8
FFN = 2816
FT = FFN // P
PART = FT // 2 * P
DECAY_SCALE = float(np.exp(-0.5))
RW_WORDS = 14700
LEVELS = [1, 2, 4, 8, 16, 32, 64]
RW_VECS = ["w0f", "w0b", "a0", "kk", "ka", "rk", "gnw", "gnb"]


def column_layout():
    at, n = {}, 0
    for name, width in [("one", 1), ("eps", 1), ("gneps", 1), ("mix0", 8), ("mix1", 8), ("xa0", 8), ("xa1", 8),
                        ("mem0", 8), ("mem1", 8), ("ffn0", 8), ("ffn1", 8), ("final", 8), ("mu", 14),
                        ("taps", 32), ("rw", 4 * len(RW_VECS)), ("ssd_d", 4), ("ssd_w", 4), ("hgw", 8),
                        ("lb0", 8), ("lb1", 8), ("dtb", 2), ("alog", 2)]:
        at[name] = n
        n += width
    return at, n


COL, NCOLS = column_layout()
TAB = dict(ident=0, ones=128, blk=256, strict=384, incl=512, reset=640, up=1152, low=1152 + 7 * P)
NTAB = 1152 + 14 * P


class Steps:

    def __init__(self, sem, names):
        self.opened = names[0] == "^"
        self.sem, self.names, self.next = sem, list(names[self.opened:]), 0
        self.value = {n: j + 1 for j, n in enumerate(self.names)}
        assert len(self.value) == len(self.names), "step names repeat"

    def one(self, name):
        assert self.names[self.next % len(self.names)] == name, (self.names[self.next % len(self.names)], name)
        self.next += 1
        return 1

    def at(self, name, i=0):
        return i * len(self.names) + (self.value[name] + self.opened)

    def passes(self, i):
        assert self.opened
        return i * len(self.names) + 1


class Ring:

    def __init__(self, slots, sems):
        self.slots, self.sems, self.base = slots, sems, [0, 0]

    def load(self, sp, w, j, u):
        sp.dma_start(self.slots[u][:, 0:w.shape[2]], w[bass.ds(j, 1), :, :].rearrange("a p n -> (a p) n")
                     ).then_inc(self.sems[u], 16)

    def prefetch(self, sp, w):
        for u in range(2):
            self.load(sp, w, u, u)

    def at(self, u, n):
        return n * 16 + (self.base[u] + 16)

    def used(self, u, n):
        self.base[u] += 16 * n


class Halves:

    def __init__(self, hi, lo, n):
        self.hi_flat, self.lo_flat = hi, lo
        self.hi, self.lo = (t.rearrange("p (n t) -> p n t", t=n) for t in (hi, lo))


def fori(engine, n0, n1):
    return engine.Fori(n0, n1)


def build_program(nc, dram, out_d, scratch_d):
    ctx = ExitStack()
    with ctx:
        def sb(name, words):
            return ctx.enter_context(nc.sbuf_tensor(name, [P, words], F32))[:, :]

        banks = [ctx.enter_context(nc.psum_tensor(f"bank{i}", [P, 512], F32))[:, :] for i in range(8)]
        xT = sb("xT", KD * T)
        slots = [sb(f"wslot{u}", PART) for u in range(2)]
        tab = sb("tab", NTAB)
        cols = sb("cols", NCOLS)
        memT = sb("memT", KD * MEM)
        x_squares = sb("x_squares", T)
        mem_inv = sb("mem_inv", MEM)
        loads = ctx.enter_context(nc.semaphore("first_loads"))
        loads2 = ctx.enter_context(nc.semaphore("table_loads"))
        loads3 = ctx.enter_context(nc.semaphore("column_loads"))
        loads4 = ctx.enter_context(nc.semaphore("memory_loads"))
        loads6 = ctx.enter_context(nc.semaphore("first_table_loads"))
        loads5 = ctx.enter_context(nc.semaphore("low_rank_loads"))
        stored = ctx.enter_context(nc.semaphore("stored"))
        ring = Ring(slots, [ctx.enter_context(nc.semaphore(f"weights{u}_loaded")) for u in range(2)])

        x3 = xT.rearrange("p (n t) -> p n t", t=T)
        mem3 = memT.rearrange("p (n m) -> p n m", m=MEM)

        def table(name, width=P, at=0):
            return tab[:, TAB[name] + at:TAB[name] + at + width]

        ident, ones, blk = table("ident"), table("ones"), table("blk")

        def col(name, j=0, n=1):
            return cols[:, COL[name] + j:COL[name] + j + n]

        def chunk(ap, c):
            return ap[:, c * P:(c + 1) * P]

        def over_chunks(ap):
            return ap.unsqueeze(1).broadcast_to([P, NC, P])

        def by_chunk(ap):
            return ap.rearrange("p (c t) -> p c t", t=P)

        dirs = (lambda ap: ap, lambda ap: ap[:, ::-1])

        held = {n: ctx.enter_context(nc.semaphore(f"held_{n}")) for n in ("vec", "pool")}

        def hold(engine, name):
            engine.sem_inc(held[name], 1)

        taken = []

        def clear_semaphores():
            with nc.Block() as block:
                @block.gpsimd
                def _(pool):
                    for s in taken:
                        pool.sem_clear(s)
            for s in taken:
                nc.release_semaphore(s)
            taken.clear()

        def steps(**named):
            sems = {n: nc.alloc_semaphore(name=n) for n in named}
            taken.extend(sems.values())
            return [Steps(sems[n], v) for n, v in named.items()]

        def area(scope, name, words):
            return scope.enter_context(nc.sbuf_tensor(name, [P, words], F32))[:, :]

        def halves(scope, name, tiles, n=T):
            return Halves(*(scope.enter_context(nc.sbuf_tensor(f"{name}_{part}", [P, tiles * n], F32R))[:, :]
                            for part in ("hi", "lo")), n)

        def as_f32(ap):
            return ap.bitcast(F32)

        class Projection:

            def __init__(self, scope, name, w, rhs, tiles, k=KD, n=T, cuts=1, token_major=False, extra=0):
                self.name, self.w, self.rhs, self.k, self.n, self.cuts, self.tm = name, w, rhs, k, n, cuts, token_major
                self.passes, self.parts, self.extra = tiles // 2, 2 * cuts, extra
                words = w.shape[2]
                self.words = words
                self.wt = [halves(scope, f"{name}_w{u}", 1, words) for u in range(2)]
                each = range(self.parts)
                self.pe_s, self.hi_s, self.lo_s = steps(**{
                    name + "_tile": [f"tile{p}" for p in each], name + "_hi": [f"hi{p}" for p in each],
                    name + "_lo": [f"lo{p}" for p in each]})
                self.ready = None

            def load(self, sp, i, p):
                ring.load(sp, self.w, i * self.parts + p, p % 2)

            def sync(self, sp, following):
                def one(i, last):
                    for p in range(self.parts):
                        sp.wait_ge(self.lo_s.sem, self.lo_s.at(f"lo{p}", i))
                        if p + 2 < self.parts:
                            self.load(sp, i, p + 2)
                        elif not last:
                            self.load(sp, i + 1, p + 2 - self.parts)
                        elif p % 2 < self.extra:
                            ring.load(sp, self.w, self.passes * self.parts + p % 2, p % 2)
                        elif following is not None:
                            ring.load(sp, following, p % 2, p % 2)
                with fori(sp, 0, self.passes - 1) as i:
                    one(i, False)
                one(self.passes - 1, True)

            def split_hi(self, act, i, p):
                u = p % 2
                act.wait_ge(ring.sems[u], ring.at(u, i * self.cuts + p // 2))
                act.activation(self.wt[u].hi_flat, slots[u][:, 0:self.words], ACT.Copy).then_inc(
                    self.hi_s.sem, self.hi_s.one(f"hi{p}"))

            def split_lo(self, dve, i, p):
                u = p % 2
                dve.wait_ge(self.hi_s.sem, self.hi_s.at(f"hi{p}", i))
                dve.tensor_tensor(self.wt[u].lo_flat, slots[u][:, 0:self.words], as_f32(self.wt[u].hi_flat),
                                  ALU.subtract).then_inc(self.lo_s.sem, self.lo_s.one(f"lo{p}"))

            def in_turns(self, engine, split, segments):
                def one(i, last, function):
                    for p in range(self.parts):
                        within = p + 2 < self.parts
                        if within or not last:
                            engine.wait_ge(self.pe_s.sem, self.pe_s.at(f"tile{p}", i))
                            if within:
                                split(engine, i, p + 2)
                            else:
                                split(engine, i + 1, p + 2 - self.parts)
                        if function and p % self.cuts == self.cuts - 1:
                            engine.wait_ge(self.pe_s.sem, self.pe_s.at(f"tile{p}", i))
                            function(i, p // self.cuts)
                done = 0
                for count, function in segments:
                    end = done + count
                    stop = min(end, self.passes - 1)
                    if stop > done:
                        with fori(engine, done, stop) as i:
                            one(i, False, function)
                    if end == self.passes:
                        one(end - 1, True, function)
                    done = end
                assert done == self.passes

            def first_hi(self, act):
                for p in range(2):
                    self.split_hi(act, 0, p)

            def first_lo(self, dve):
                for p in range(2):
                    self.split_lo(dve, 0, p)

            def scalar(self, act, *segments):
                self.in_turns(act, self.split_hi, segments or [(self.passes, None)])

            def vector(self, dve, *segments):
                self.in_turns(dve, self.split_lo, segments or [(self.passes, None)])

            def products(self, pe, p, bank, ready=None):
                w, r, k0 = self.wt[p % 2], self.rhs, p % self.cuts * self.k
                first, last = p % self.cuts == 0, p % self.cuts == self.cuts - 1
                for k in range(self.k):
                    if ready:
                        ready(pe, k)
                    for n, (wp, rp) in enumerate(((w.hi_flat, r.hi), (w.lo_flat, r.hi), (w.hi_flat, r.lo))):
                        start, stop = first and k == 0 and n == 0, last and k == self.k - 1 and n == 2
                        if self.tm:
                            for m in range(MEM // P):
                                ins = pe.matmul(banks[2 * bank + m][:, 0:256], rp[:, k0 + k, m * P:(m + 1) * P],
                                                wp[:, k * 256:(k + 1) * 256], start=start, stop=stop)
                        else:
                            ins = pe.matmul(banks[bank][:, 0:self.n], wp[:, k * P:(k + 1) * P], rp[:, k0 + k, :],
                                            start=start, stop=stop)
                return ins

            def tensor(self, pe, *segments):
                def one(i, emptied):
                    for p in range(self.parts):
                        pe.wait_ge(self.lo_s.sem, self.lo_s.at(f"lo{p}", i))
                        if emptied and p % self.cuts == 0:
                            emptied(p // self.cuts, i - 1)
                        ready = self.ready if emptied is None and p == 0 else None
                        self.products(pe, p, p // self.cuts, ready).then_inc(self.pe_s.sem, self.pe_s.one(f"tile{p}"))
                one(0, None)
                done = 1
                for count, emptied in segments:
                    with fori(pe, done, done + count) as i:
                        one(i, emptied)
                    done += count
                assert done == self.passes, (self.name, done)

            def end(self):
                for u in range(2):
                    ring.used(u, self.passes * self.cuts + (u < self.extra))

        class SplitSource:

            def __init__(self, scope, name, src, rhs):
                self.src, self.rhs = src, rhs
                self.a_s, self.v_s = steps(**{name + "_src_hi": [f"hi{k}" for k in range(KD)],
                                                     name + "_src_lo": [f"lo{k}" for k in range(KD)]})

            def scalar(self, act):
                for k in range(KD):
                    act.activation(self.rhs.hi[:, k, :], self.src[:, k, :], ACT.Copy).then_inc(
                        self.a_s.sem, self.a_s.one(f"hi{k}"))

            def vector(self, dve):
                for k in range(KD):
                    dve.wait_ge(self.a_s.sem, self.a_s.at(f"hi{k}"))
                    dve.tensor_tensor(self.rhs.lo[:, k, :], self.src[:, k, :], as_f32(self.rhs.hi[:, k, :]),
                                      ALU.subtract).then_inc(self.v_s.sem, self.v_s.one(f"lo{k}"))

            def tensor(self, pe):
                pass

            def gpsimd(self, pool):
                pass

            def ready(self, pe, k):
                pe.wait_ge(self.v_s.sem, self.v_s.at(f"lo{k}"))

        class NormSource:

            def __init__(self, scope, name, src, rhs, gain, width=T, room=None, squares=None, keep=None, kept=None):
                self.squares, self.kept = squares, kept
                self.src, self.rhs, self.gain, self.width = src, rhs, gain, width
                room = area(scope, name + "_norm", 5 * width) if room is None else room
                self.tmp = [room[:, j * width:(j + 1) * width] for j in range(4)]
                self.inv = keep if keep is not None else kept if kept is not None else room[:, 4 * width:5 * width]
                ks = range(KD)
                squared = [] if squares is not None or kept is not None else list(ks)
                vec = [f"square{k}" for k in squared if k % 2] + ([] if kept is not None else ["inverse"])
                for k in ks:
                    vec += [f"out{k}"] + ([f"lo{k - 1}"] if k % 2 else [])
                self.a_s, self.v_s, self.pe_s, self.g_s = steps(**{
                    name + "_norm_act": [f"square{k}" for k in squared if k % 2 == 0]
                    + ([] if kept is not None else ["root"]) + [f"hi{k}" for k in ks],
                    name + "_norm_vec": vec, name + "_norm_pe": [f"sum{k}" for k in squared or [KD - 1]],
                    name + "_norm_pool": [f"lo{k}" for k in ks if k % 2]})
                self.squared = squared

            def scalar(self, act):
                a_s, pe_s, v_s = self.a_s, self.pe_s, self.v_s
                for k in self.squared[::2]:
                    if k >= 4:
                        act.wait_ge(pe_s.sem, pe_s.at(f"sum{k - 4}"))
                    act.activation(self.tmp[k % 4], self.src[:, k, :], ACT.Square).then_inc(a_s.sem, a_s.one(f"square{k}"))
                if self.kept is None:
                    act.wait_ge(pe_s.sem, pe_s.at(f"sum{KD - 1}"))
                    act.activation(self.inv, banks[7][:, 0:self.width], ACT.Sqrt, bias=col("eps"),
                                   scale=1.0 / D).then_inc(a_s.sem, a_s.one("root"))
                for k in range(KD):
                    act.wait_ge(v_s.sem, v_s.at(f"out{k}"))
                    act.activation(self.rhs.hi[:, k, :], self.tmp[k % 4], ACT.Copy).then_inc(a_s.sem, a_s.one(f"hi{k}"))

            def tensor(self, pe):
                a_s, pe_s, v_s = self.a_s, self.pe_s, self.v_s
                if self.squares is not None:
                    pe.matmul(banks[7][:, 0:self.width], ones, self.squares, start=True, stop=True
                              ).then_inc(pe_s.sem, pe_s.one(f"sum{KD - 1}"))
                for k in self.squared:
                    if k % 2:
                        pe.wait_ge(v_s.sem, v_s.at(f"square{k}"))
                    else:
                        pe.wait_ge(a_s.sem, a_s.at(f"square{k}"))
                    pe.matmul(banks[7][:, 0:self.width], ones, self.tmp[k % 4], start=k == 0,
                              stop=k == KD - 1).then_inc(pe_s.sem, pe_s.one(f"sum{k}"))

            def lo(self, engine, k, done):
                engine.wait_ge(self.a_s.sem, self.a_s.at(f"hi{k}"))
                engine.tensor_tensor(self.rhs.lo[:, k, :], self.tmp[k % 4], as_f32(self.rhs.hi[:, k, :]),
                                     ALU.subtract).then_inc(done.sem, done.one(f"lo{k}"))

            def vector(self, dve):
                a_s, pe_s, v_s, g_s = self.a_s, self.pe_s, self.v_s, self.g_s
                for k in self.squared[1::2]:
                    if k >= 4:
                        dve.wait_ge(pe_s.sem, pe_s.at(f"sum{k - 4}"))
                    dve.tensor_tensor(self.tmp[k % 4], self.src[:, k, :], self.src[:, k, :], ALU.mult).then_inc(
                        v_s.sem, v_s.one(f"square{k}"))
                if self.kept is None:
                    dve.wait_ge(a_s.sem, a_s.at("root"))
                    dve.reciprocal(self.inv, self.inv).then_inc(v_s.sem, v_s.one("inverse"))
                    dve.wait_ge(v_s.sem, v_s.at("inverse"))
                for k in range(KD):
                    if k >= 4:
                        s = g_s if k % 2 else v_s
                        dve.wait_ge(s.sem, s.at(f"lo{k - 4}"))
                    dve.scalar_tensor_tensor(self.tmp[k % 4], self.src[:, k, :], col(self.gain, k), self.inv,
                                             ALU.mult, ALU.mult).then_inc(v_s.sem, v_s.one(f"out{k}"))
                    if k % 2:
                        self.lo(dve, k - 1, v_s)

            def gpsimd(self, pool):
                for k in range(1, KD, 2):
                    self.lo(pool, k, self.g_s)

            def ready(self, pe, k):
                s = self.g_s if k % 2 else self.v_s
                pe.wait_ge(s.sem, s.at(f"lo{k}"))

        def project(name, pr, source=None, vector=None, scalar=None, following=None, reader="v"):
            with ExitStack() as scope:
                v_s, a_s = steps(**{name + "_vec": ["v0", "v1"], name + "_act": ["a0", "a1"]})
                emptied_by = v_s if reader == "v" else a_s
                if source:
                    pr.ready = source.ready
                with nc.Block() as block:
                    @block.sync
                    def _(sp):
                        pr.sync(sp, following)

                    @block.tensor
                    def _(pe):
                        if source:
                            source.tensor(pe)
                        pr.tensor(pe, (pr.passes - 1, lambda u, i: pe.wait_ge(emptied_by.sem, emptied_by.at(f"{reader}{u}", i))))

                    @block.scalar
                    def _(act):
                        pr.first_hi(act)
                        if source:
                            source.scalar(act)
                        pr.scalar(act, (pr.passes, scalar and (
                            lambda i, u: scalar(act, i, u).then_inc(a_s.sem, a_s.one(f"a{u}")))))

                    @block.vector
                    def _(dve):
                        pr.first_lo(dve)
                        if source:
                            source.vector(dve)
                        pr.vector(dve, (pr.passes, vector and (
                            lambda i, u: vector(dve, i, u).then_inc(v_s.sem, v_s.one(f"v{u}")))))

                    @block.gpsimd
                    def _(pool):
                        if source:
                            source.gpsimd(pool)
                pr.end()

        def add_to_residual(scope, name, w, rhs, following, source=None, **shape):
            pr = Projection(scope, name, w, rhs, KD, **shape)
            square = [area(scope, f"{name}_square{u}", T) for u in range(2)]
            zero_s, v_s, a_s = steps(**{name + "_zero": ["zero"], name + "_vec": ["x0", "sum0", "x1", "sum1"],
                                        name + "_act": ["square0", "square1"]})
            if source:
                pr.ready = source.ready

            def tile(i, u):
                return xT[:, bass.ds(i * (2 * T) + u * T, T)]

            with nc.Block() as block:
                @block.sync
                def _(sp):
                    pr.sync(sp, following)

                @block.tensor
                def _(pe):
                    pr.tensor(pe, (pr.passes - 1, lambda u, i: pe.wait_ge(v_s.sem, v_s.at(f"x{u}", i))))

                @block.scalar
                def _(act):
                    pr.first_hi(act)
                    if source:
                        source.scalar(act)

                    def squared(i, u):
                        act.wait_ge(v_s.sem, v_s.at(f"x{u}", i))
                        act.activation(square[u], tile(i, u), ACT.Square).then_inc(a_s.sem, a_s.one(f"square{u}"))
                    pr.scalar(act, (pr.passes, squared))

                @block.vector
                def _(dve):
                    dve.memset(x_squares, 0.0).then_inc(zero_s.sem, zero_s.one("zero"))
                    pr.first_lo(dve)
                    if source:
                        source.vector(dve)
                    dve.wait_ge(zero_s.sem, zero_s.at("zero"))

                    def add(i, u):
                        dve.tensor_tensor(tile(i, u), banks[u], tile(i, u), ALU.add).then_inc(v_s.sem, v_s.one(f"x{u}"))
                        dve.wait_ge(a_s.sem, a_s.at(f"square{u}", i))
                        dve.tensor_tensor(x_squares, square[u], x_squares, ALU.add).then_inc(v_s.sem, v_s.one(f"sum{u}"))
                    pr.vector(dve, (pr.passes, add))
            pr.end()

        mixer0 = ctx.enter_context(ExitStack())
        proj = area(mixer0, "proj0", REV0 * T + 8 * T)
        p3 = proj.rearrange("p (n t) -> p n t", t=T)
        lora = area(mixer0, "lora", 4 * T)
        dt_cum = area(mixer0, "dt_cum", 4 * T)
        with nc.Block() as block:
            @block.sync
            def _(sp):
                sp.dma_start(xT, dram["xT"]).then_inc(loads, 16)
                sp.dma_start(cols, dram["cols"]).then_inc(loads3, 16)
                sp.dma_start(tab[:, 0:2 * P], dram["tab"][:, 0:2 * P]).then_inc(loads6, 16)
                ring.prefetch(sp, dram["ab_in"])
                sp.dma_start(tab[:, 2 * P:NTAB], dram["tab"][:, 2 * P:NTAB]).then_inc(loads2, 16)
                sp.dma_start(lora, dram["lora"]).then_inc(loads5, 16)
                sp.dma_start(memT, dram["memT"]).then_inc(loads4, 16)
                for s in (loads, loads3, loads6):
                    sp.wait_ge(s, 16)

        def rwkv_ssd_projection(outer):
            work = area(outer, "ab_work", 5160)
            raw = [work[:, u * 520:u * 520 + 514] for u in range(2)]
            t1, t2, conv, sil = ([work[:, 1040 + j * 1024 + u * 512:1552 + j * 1024 + u * 512] for u in range(2)]
                                 for j in range(4))
            mu_half, mu_rest, decay_rate = work[:, 5136:5136 + 14], proj[:, 33 * T:33 * T + 14], work[0:8, 5152:5154]
            dt_x, dt_m, dt, cum = work[0:8, 1040:2064], work[0:8, 2064:3088], dt_cum[0:8, 0:1024], dt_cum[0:8, 1024:2048]
            rhs = halves(outer, "ab_h", KD)
            pr = Projection(outer, "ab_in", dram["ab_in"], rhs, 26, extra=1)
            source = NormSource(outer, "ab_in", x3, rhs, "mix0", room=work[:, 0:5 * T])
            pr.ready = source.ready
            with ExitStack() as scope:
                pe_s = pr.pe_s
                dtp_s, dth_s, dtl_s = steps(ab_dt_tile=["dt"], ab_dt_hi=["hi"], ab_dt_lo=["lo"])
                set_s, = steps(ab_setup=["zero0", "zero1", "zero2", "zero3", "half", "rest"])
                act_s, = steps(ab_raw=["raw0", "raw1"])
                v_s, = steps(ab_taps=["^", "mid0", "left0", "right0", "mid1", "left1", "right1"])
                vc_s, = steps(ab_conv=["^", "mid0", "left0", "right0", "mid1", "left1", "right1"])
                ac_s, = steps(ab_silu=["raw0", "silu0", "raw1", "silu1"])
                g_s, = steps(ab_reverse=["^", "fwd0", "rev0", "fwd1", "rev1"])
                az_s, = steps(ab_z=["z0", "z1"])
                dta_s, = steps(ab_dt_act=["rate", "exp", "log"])
                dtv_s, = steps(ab_dt_vec=["x0", "x1", "minus", "negrate", "dt0", "dt1", "la0", "la1",
                                                 "cum0", "cum1"])
                nrw, nx, nz = RW_TILES // 2, XBC_TILES // 2, Z_TILES // 2
                with nc.Block() as block:
                    @block.sync
                    def _(sp):
                        pr.sync(sp, None)
                        sp.wait_ge(dtv_s.sem, dtv_s.at("cum1"))
                        sp.dma_start(scratch_d.rearrange("(d h t) -> h d t", d=2, h=8),
                                     cum.rearrange("h (d t) -> h d t", d=2)).then_inc(stored_cum, 16)
                        for s in (stored_cum, loads2, loads4, loads5):
                            sp.wait_ge(s, 16)

                    @block.tensor
                    def _(pe):
                        source.tensor(pe)
                        def after(sem, name):
                            return lambda u, i: pe.wait_ge(sem.sem, sem.at(f"{name}{u}", i))

                        pr.tensor(pe, (nrw, after(act_s, "raw")),
                                  (nx, lambda u, i: pe.wait_ge(ac_s.sem, ac_s.at(f"raw{u}", i - nrw))),
                                  (nz - 1, lambda u, i: pe.wait_ge(az_s.sem, az_s.at(f"z{u}", i - (nrw + nx)))))
                        pe.wait_ge(dtl_s.sem, dtl_s.at("lo"))
                        ins = pr.products(pe, 0, 2)
                        ins.then_inc(dtp_s.sem, dtp_s.one("dt"))

                    @block.scalar
                    def _(act):
                        pr.first_hi(act)
                        source.scalar(act)
                        act.wait_ge(set_s.sem, set_s.at("zero3"))

                        def rwkv_tile(i, u):
                            act.wait_ge(v_s.sem, v_s.passes(i))
                            act.activation(raw[u][:, 1:513], banks[u], ACT.Copy).then_inc(act_s.sem, act_s.one(f"raw{u}"))

                        def conv_tile(i, u):
                            i = i - nrw
                            act.wait_ge(v_s.sem, v_s.at("right1", nrw - 1))
                            act.wait_ge(vc_s.sem, vc_s.passes(i))
                            act.activation(raw[u][:, 1:513], banks[u], ACT.Copy).then_inc(ac_s.sem, ac_s.one(f"raw{u}"))
                            act.wait_ge(vc_s.sem, vc_s.at(f"right{u}", i))
                            act.wait_ge(g_s.sem, g_s.passes(i))
                            act.activation(sil[u], conv[u], ACT.Silu).then_inc(ac_s.sem, ac_s.one(f"silu{u}"))

                        def z_tile(i, u):
                            act.activation(proj[:, bass.ds(i * (2 * T) + (Z0 + u - 2 * (nrw + nx)) * T, T)], banks[u],
                                           ACT.Silu).then_inc(az_s.sem, az_s.one(f"z{u}"))

                        pr.scalar(act, (nrw, rwkv_tile), (nx, conv_tile), (nz, z_tile))
                        act.wait_ge(ring.sems[0], ring.at(0, pr.passes))
                        act.activation(pr.wt[0].hi_flat, slots[0][:, 0:pr.words], ACT.Copy).then_inc(dth_s.sem, dth_s.one("hi"))
                        act.activation(decay_rate, cols[0:8, COL["alog"]:COL["alog"] + 2], ACT.Exp).then_inc(dta_s.sem, dta_s.one("rate"))
                        act.wait_ge(dtv_s.sem, dtv_s.at("minus"))
                        act.activation(dt_m, dt_m, ACT.Exp).then_inc(dta_s.sem, dta_s.one("exp"))
                        act.wait_ge(dta_s.sem, dta_s.at("exp"))
                        act.activation(dt_m, dt_m, ACT.Ln, bias=1.0).then_inc(dta_s.sem, dta_s.one("log"))

                    @block.vector
                    def _(dve):
                        dve.sem_inc(v_s.sem, 1)
                        dve.sem_inc(vc_s.sem, 1)
                        pr.first_lo(dve)
                        source.vector(dve)
                        dve.wait_ge(source.g_s.sem, source.g_s.at(f"lo{KD - 1}"))
                        dve.wait_ge(source.v_s.sem, source.v_s.at(f"lo{KD - 2}"))
                        for u in range(2):
                            dve.memset(raw[u][:, 0:1], 0.0).then_inc(set_s.sem, set_s.one(f"zero{2 * u}"))
                            dve.memset(raw[u][:, 513:514], 0.0).then_inc(set_s.sem, set_s.one(f"zero{2 * u + 1}"))
                        dve.tensor_scalar(mu_half, col("mu", 0, 14), 0.5, None, ALU.mult).then_inc(set_s.sem, set_s.one("half"))
                        dve.tensor_scalar(mu_rest, col("mu", 0, 14), -1.0, 1.0, ALU.mult, ALU.add).then_inc(set_s.sem, set_s.one("rest"))
                        dve.wait_ge(set_s.sem, set_s.at("rest"))
                        def rwkv_tile(i, u):
                            j = i * 2 + u
                            half = mu_half[:, bass.ds(j, 1)]
                            dve.wait_ge(act_s.sem, act_s.at(f"raw{u}", i))
                            dve.tensor_scalar(t1[u], raw[u][:, 1:513], mu_rest[:, bass.ds(j, 1)], None,
                                              ALU.mult).then_inc(v_s.sem, v_s.one(f"mid{u}"))
                            dve.wait_ge(v_s.sem, v_s.at(f"mid{u}", i))
                            dve.scalar_tensor_tensor(t2[u], raw[u][:, 0:512], half, t1[u],
                                                     ALU.mult, ALU.add).then_inc(v_s.sem, v_s.one(f"left{u}"))
                            dve.wait_ge(v_s.sem, v_s.at(f"left{u}", i))
                            dve.scalar_tensor_tensor(proj[:, bass.ds(i * (2 * T) + u * T, T)],
                                                     raw[u][:, 2:514], half, t2[u], ALU.mult, ALU.add).then_inc(v_s.sem, v_s.one(f"right{u}"))

                        def conv_tile(i, u):
                            def tap(n):
                                return cols[:, bass.ds(i * 8 + (COL["taps"] + 4 * u + n - 8 * nrw), 1)]
                            i0 = i - nrw
                            dve.wait_ge(v_s.sem, v_s.at("right1", nrw - 1))
                            dve.wait_ge(ac_s.sem, ac_s.at(f"raw{u}", i0))
                            dve.tensor_scalar(t1[u], raw[u][:, 1:513], tap(1), tap(3), ALU.mult, ALU.add).then_inc(vc_s.sem, vc_s.one(f"mid{u}"))
                            dve.wait_ge(vc_s.sem, vc_s.at(f"mid{u}", i0))
                            dve.scalar_tensor_tensor(t2[u], raw[u][:, 0:512], tap(0), t1[u],
                                                     ALU.mult, ALU.add).then_inc(vc_s.sem, vc_s.one(f"left{u}"))
                            dve.wait_ge(vc_s.sem, vc_s.at(f"left{u}", i0))
                            dve.scalar_tensor_tensor(conv[u], raw[u][:, 2:514], tap(2), t2[u],
                                                     ALU.mult, ALU.add).then_inc(vc_s.sem, vc_s.one(f"right{u}"))

                        pr.vector(dve, (nrw, rwkv_tile), (nx, conv_tile), (nz, None))
                        dve.wait_ge(dth_s.sem, dth_s.at("hi"))
                        dve.tensor_tensor(pr.wt[0].lo_flat, slots[0][:, 0:pr.words], as_f32(pr.wt[0].hi_flat),
                                          ALU.subtract).then_inc(dtl_s.sem, dtl_s.one("lo"))
                        dve.wait_ge(dtp_s.sem, dtp_s.at("dt"))
                        for d in range(2):
                            dve.tensor_scalar(dt_x[:, d * T:(d + 1) * T], banks[2][0:8, :],
                                                         cols[0:8, COL["dtb"] + d:COL["dtb"] + d + 1], None, ALU.add).then_inc(dtv_s.sem, dtv_s.one(f"x{d}"))
                        dve.wait_ge(dtv_s.sem, dtv_s.at("x1"))
                        dve.scalar_tensor_tensor(dt_m, dt_x, -1.0, dt_x, ALU.mult, ALU.min).then_inc(dtv_s.sem, dtv_s.one("minus"))
                        dve.wait_ge(dta_s.sem, dta_s.at("rate"))
                        dve.tensor_scalar(decay_rate, decay_rate, -1.0, None, ALU.mult).then_inc(dtv_s.sem, dtv_s.one("negrate"))
                        dve.wait_ge(dta_s.sem, dta_s.at("log"))
                        for d in range(2):
                            dve.scalar_tensor_tensor(
                                dt[:, d * T:(d + 1) * T], dirs[d](dt_x[:, d * T:(d + 1) * T]), 0.0,
                                dirs[d](dt_m[:, d * T:(d + 1) * T]), ALU.max, ALU.add).then_inc(dtv_s.sem, dtv_s.one(f"dt{d}"))
                        dve.wait_ge(dtv_s.sem, dtv_s.at("dt1"))
                        for d in range(2):
                            dve.tensor_scalar(dt_x[:, d * T:(d + 1) * T], dt[:, d * T:(d + 1) * T],
                                                         decay_rate[:, d:d + 1], None, ALU.mult).then_inc(dtv_s.sem, dtv_s.one(f"la{d}"))
                        dve.wait_ge(dtv_s.sem, dtv_s.at("la1"))
                        dve.wait_ge(loads2, 16)
                        for d in range(2):
                            dve.tensor_tensor_scan(cum[:, d * T:(d + 1) * T], tab[0:8, TAB["reset"]:TAB["reset"] + T],
                                                              dt_x[:, d * T:(d + 1) * T], 0.0, ALU.mult, ALU.add).then_inc(dtv_s.sem, dtv_s.one(f"cum{d}"))

                    @block.gpsimd
                    def _(pool):
                        pool.sem_inc(g_s.sem, 1)
                        source.gpsimd(pool)
                        with fori(pool, 0, nx) as i:
                            for u in range(2):
                                pool.wait_ge(ac_s.sem, ac_s.at(f"silu{u}", i))
                                for name, at, src in (("fwd", XS0, sil[u]), ("rev", REV0, sil[u][:, ::-1])):
                                    pool.tensor_copy(proj[:, bass.ds(i * (2 * T) + (at + u) * T, T)], src).then_inc(g_s.sem, g_s.one(f"{name}{u}"))
                pr.end()
            return dt, cum

        stored_cum = ctx.enter_context(nc.semaphore("cum_stored"))
        with ExitStack() as inner:
            dt_sb, cum_sb = rwkv_ssd_projection(inner)
        hT = area(mixer0, "hT0", KD * T)
        h3 = hT.rearrange("p (n t) -> p n t", t=T)

        def ssd(outer):
            work, room = area(outer, "ssd_work", 4656), area(outer, "ssd_room", 9 * T)
            cumb = work[:, 0:2048]
            xs_st, b_st, c_st = work[:, 2048:3072], work[:, 3072:3584], work[:, 3584:4096]
            state = work[:, 4112:4368]
            o = 4368
            dt_tok, cum_tok, ecum = work[:, o:o + 64], work[:, o + 64:o + 128], work[:, o + 128:o + 192]
            cum16, dt16, ecum16, eend, wdiff, wexp = (work[:, o + 192 + 16 * j:o + 208 + 16 * j] for j in range(6))
            used = [0]

            def take(n):
                used[0] += n
                return room[:, used[0] - n:used[0]]

            dec, mix = [take(T), take(T)], [take(T), take(T)]
            sm, btok = [take(P), take(P)], [take(P), take(P)]
            xdt, xdtw, y2 = [take(256), take(256)], [take(256), take(256)], [take(256), take(256)]
            y1, tmp = take(256), take(256)
            score_bank, turn_bank, y_bank, off_bank, add_bank, back_bank = [0, 1], [2, 7], 3, 4, 5, 6

            def h4(ap):
                return ap.rearrange("p (h w) -> p h w", h=4)

            def per_head(ap16, c, w):
                return ap16[:, 4 * c:4 * c + 4].unsqueeze(2).broadcast_to([P, 4, w])

            pre_pe, pre_v, pre_a = steps(ssd_pre_pe=["tok"], ssd_pre_vec=["dt_tok", "cum_tok"], ssd_pre_act=["ecum"])

            def each_chunk(names):
                return [f"{n}{c}" for c in range(NC) for n in names]

            s_act, s_vec, s_pool = steps(ssd_S_act=["xs", "b", "c", "eend", "wexp"], ssd_S_vec=["zero", "wdiff"],
                                         ssd_S_pool=["cum16", "dt16", "ecum16"])
            f_pe, f_act, f_vec, f_pool = steps(
                ssd_F_pe=each_chunk(["scores", "turned"]), ssd_F_act=each_chunk(["dec", "btok"]),
                ssd_F_vec=each_chunk(["cap", "sm", "xdt", "xdtw", "mix"]), ssd_F_pool=each_chunk(["dec"]))
            b_pe, b_act, b_vec = steps(
                ssd_B_pe=["^"] + each_chunk(["off", "add", "y", "back"]), ssd_B_act=["^"] + each_chunk(["out"]),
                ssd_B_vec=["^"] + each_chunk(["y1", "hdecay", "hadd", "y2"]))
            cumb_sem = ctx.enter_context(nc.semaphore("cumb_loaded"))

            def each_pass(engine, stage, front, back):
                with fori(engine, 0, 2) as d:
                    with fori(engine, 0, 2) as g:
                        it = d * 2 + g
                        stage(d, g, it)
                        front(0, it)
                        for c in range(NC):
                            if c + 1 < NC:
                                front(c + 1, it)
                            back(c, d, g, it)

            with nc.Block() as block:
                @block.sync
                def _(sp):
                    with fori(sp, 0, 2) as d:
                        with fori(sp, 0, 2) as g:
                            sp.wait_ge(b_vec.sem, b_vec.passes(d * 2 + g))
                            sp.dma_start(cumb, scratch_d[bass.ds(d * (8 * T) + g * (4 * T), 4 * T)].partition_broadcast(P)
                                         ).then_inc(cumb_sem, 16)

                @block.tensor
                def _(pe):
                    for d in range(2):
                        for c in range(NC):
                            w = d * T + c * P
                            k = (d * NC + c) * 8
                            pe.transpose(banks[0][:, k:k + 8], dt_sb[:, w:w + P], ident[0:8, 0:8])
                            ins = pe.transpose(banks[1][:, k:k + 8], cum_sb[:, w:w + P], ident[0:8, 0:8])
                    ins.then_inc(pre_pe.sem, pre_pe.one("tok"))
                    pe.wait_ge(pre_v.sem, pre_v.at("cum_tok"))
                    pe.sem_inc(b_pe.sem, 1)

                    def stage(d, g, it):
                        pe.wait_ge(b_vec.sem, b_vec.passes(it))
                        pe.wait_ge(s_act.sem, s_act.at("c", it))

                    def front(c, it):
                        u = c % 2
                        if c >= 2:
                            pe.wait_ge(f_vec.sem, f_vec.at(f"sm{c - 2}", it))
                        pe.matmul(banks[score_bank[u]][:, 0:P], chunk(b_st, c), chunk(c_st, c), start=True, stop=True
                                  ).then_inc(f_pe.sem, f_pe.one(f"scores{c}"))
                        if c >= 2:
                            pe.wait_ge(f_vec.sem, f_vec.at(f"xdt{c - 2}", it))
                            pe.wait_ge(f_act.sem, f_act.at(f"btok{c - 2}", it))
                        bank = banks[turn_bank[u]]
                        for j in range(2):
                            pe.transpose(chunk(bank, j), chunk(xs_st, NC * j + c), ident)
                        pe.transpose(chunk(bank, 2), chunk(b_st, c), ident).then_inc(f_pe.sem, f_pe.one(f"turned{c}"))

                    def back(c, d, g, it):
                        u = c % 2
                        if c:
                            pe.wait_ge(b_vec.sem, b_vec.at(f"hadd{c - 1}", it))
                        else:
                            pe.wait_ge(s_vec.sem, s_vec.at("zero", it))
                        pe.matmul(banks[off_bank][:, 0:256], chunk(c_st, c), state, start=True, stop=True).then_inc(b_pe.sem, b_pe.one(f"off{c}"))
                        pe.wait_ge(f_vec.sem, f_vec.at(f"xdtw{c}", it))
                        pe.wait_ge(f_act.sem, f_act.at(f"btok{c}", it))
                        pe.matmul(banks[add_bank][:, 0:256], btok[u], xdtw[u], start=True, stop=True).then_inc(b_pe.sem, b_pe.one(f"add{c}"))
                        pe.wait_ge(f_vec.sem, f_vec.at(f"mix{c}", it))
                        if c:
                            pe.wait_ge(b_vec.sem, b_vec.at(f"y2{c - 1}", it))
                        for h in range(4):
                            ins = pe.matmul(banks[y_bank][:, h * HD:(h + 1) * HD], chunk(mix[u], h),
                                            xdt[u][:, h * HD:(h + 1) * HD], start=True, stop=True)
                        ins.then_inc(b_pe.sem, b_pe.one(f"y{c}"))
                        pe.wait_ge(b_vec.sem, b_vec.at(f"y2{c}", it))
                        if c:
                            pe.wait_ge(b_act.sem, b_act.at(f"out{c - 1}", it))
                        else:
                            pe.wait_ge(b_act.sem, b_act.passes(it))
                        for j in range(2):
                            ins = pe.transpose(chunk(banks[back_bank], j), chunk(y2[u], j), ident)
                        ins.then_inc(b_pe.sem, b_pe.one(f"back{c}"))
                    each_pass(pe, stage, front, back)

                @block.scalar
                def _(act):
                    act.sem_inc(b_act.sem, 1)
                    act.wait_ge(pre_v.sem, pre_v.at("cum_tok"))
                    act.activation(ecum, cum_tok, ACT.Exp).then_inc(pre_a.sem, pre_a.one("ecum"))

                    def stage(d, g, it):
                        act.wait_ge(b_pe.sem, b_pe.passes(it))
                        act.wait_ge(b_vec.sem, b_vec.passes(it))
                        base = d * (12 * T)
                        act.activation(xs_st, proj[:, bass.ds(base + g * (2 * T) + XS0 * T, 2 * T)], ACT.Copy).then_inc(s_act.sem, s_act.one("xs"))
                        act.activation(b_st, proj[:, bass.ds(base + g * T + B0 * T, T)], ACT.Copy).then_inc(s_act.sem, s_act.one("b"))
                        act.activation(c_st, proj[:, bass.ds(base + g * T + C0 * T, T)], ACT.Copy).then_inc(s_act.sem, s_act.one("c"))
                        act.wait_ge(cumb_sem, it * 16 + 16)
                        ends = cumb.rearrange("p (h c t) -> p c h t", h=4, t=P)[:, :, :, P - 1]
                        act.activation(eend.rearrange("p (c h) -> p c h", h=4), ends, ACT.Exp).then_inc(s_act.sem, s_act.one("eend"))
                        act.wait_ge(s_vec.sem, s_vec.at("wdiff", it))
                        act.activation(wexp, wdiff, ACT.Exp).then_inc(s_act.sem, s_act.one("wexp"))

                    def front(c, it):
                        u = c % 2
                        act.wait_ge(f_vec.sem, f_vec.at(f"cap{c}", it))
                        act.activation(dec[u], dec[u], ACT.Exp).then_inc(f_act.sem, f_act.one(f"dec{c}"))
                        act.wait_ge(f_vec.sem, f_vec.at(f"xdt{c}", it))
                        if c >= 2:
                            act.wait_ge(b_pe.sem, b_pe.at(f"add{c - 2}", it))
                        act.activation(btok[u], chunk(banks[turn_bank[u]], 2), ACT.Copy).then_inc(f_act.sem, f_act.one(f"btok{c}"))

                    def back(c, d, g, it):
                        act.wait_ge(b_pe.sem, b_pe.at(f"back{c}", it))
                        act.activation(h3[:, bass.ds(d * 4 + g * 2, 2), c * P:(c + 1) * P],
                                       banks[back_bank][:, 0:256].rearrange("p (j t) -> p j t", t=P),
                                       ACT.Copy).then_inc(b_act.sem, b_act.one(f"out{c}"))
                    each_pass(act, stage, front, back)

                @block.gpsimd
                def _(pool):
                    def stage(d, g, it):
                        pool.wait_ge(b_vec.sem, b_vec.passes(it))
                        pool.wait_ge(pre_a.sem, pre_a.at("ecum"))
                        hold(pool, "pool")
                        for name, dst, src in (("cum16", cum16, cum_tok), ("dt16", dt16, dt_tok), ("ecum16", ecum16, ecum)):
                            pool.tensor_copy(dst.rearrange("p (c h) -> p c h", h=4),
                                             src.rearrange("p (n h) -> p n h", h=8)[:, bass.ds(d * 4, 4), bass.ds(g * 4, 4)]
                                             ).then_inc(s_pool.sem, s_pool.one(name))
                        pool.wait_ge(cumb_sem, it * 16 + 16)
                        pool.wait_ge(s_pool.sem, s_pool.at("cum16", it))

                    def front(c, it):
                        if c >= 2:
                            pool.wait_ge(f_vec.sem, f_vec.at(f"mix{c - 2}", it))
                        pool.tensor_tensor(h4(dec[c % 2]), h4(cumb)[:, :, c * P:(c + 1) * P], per_head(cum16, c, P),
                                           ALU.subtract).then_inc(f_pool.sem, f_pool.one(f"dec{c}"))

                    def back(c, d, g, it):
                        pass
                    each_pass(pool, stage, front, back)

                @block.vector
                def _(dve):
                    dve.sem_inc(b_vec.sem, 1)
                    dve.wait_ge(pre_pe.sem, pre_pe.at("tok"))
                    dve.tensor_copy(dt_tok, banks[0][:, 0:64]).then_inc(pre_v.sem, pre_v.one("dt_tok"))
                    dve.tensor_copy(cum_tok, banks[1][:, 0:64]).then_inc(pre_v.sem, pre_v.one("cum_tok"))

                    def stage(d, g, it):
                        dve.wait_ge(b_pe.sem, b_pe.passes(it))
                        dve.memset(state, 0.0).then_inc(s_vec.sem, s_vec.one("zero"))
                        dve.wait_ge(s_pool.sem, s_pool.at("ecum16", it))
                        dve.wait_ge(cumb_sem, it * 16 + 16)
                        ends = cumb.rearrange("p (h c t) -> p c h t", h=4, t=P)[:, :, :, P - 1]
                        dve.tensor_tensor(wdiff.rearrange("p (c h) -> p c h", h=4), ends,
                                          cum16.rearrange("p (c h) -> p c h", h=4), ALU.subtract).then_inc(s_vec.sem, s_vec.one("wdiff"))

                    def front(c, it):
                        u = c % 2
                        dve.wait_ge(f_pool.sem, f_pool.at(f"dec{c}", it))
                        dve.tensor_scalar(dec[u], dec[u], 0.0, None, ALU.min).then_inc(f_vec.sem, f_vec.one(f"cap{c}"))
                        dve.wait_ge(f_pe.sem, f_pe.at(f"scores{c}", it))
                        if c >= 2:
                            dve.wait_ge(f_vec.sem, f_vec.at(f"mix{c - 2}", it))
                        dve.tensor_tensor(sm[u], banks[score_bank[u]][:, 0:P], table("incl"), ALU.mult).then_inc(f_vec.sem, f_vec.one(f"sm{c}"))
                        dve.wait_ge(f_pe.sem, f_pe.at(f"turned{c}", it))
                        if c >= 2:
                            dve.wait_ge(b_pe.sem, b_pe.at(f"y{c - 2}", it))
                        dve.tensor_tensor(h4(xdt[u]), h4(banks[turn_bank[u]][:, 0:256]), per_head(dt16, c, HD), ALU.mult).then_inc(f_vec.sem, f_vec.one(f"xdt{c}"))
                        dve.wait_ge(s_act.sem, s_act.at("wexp", it))
                        dve.wait_ge(f_vec.sem, f_vec.at(f"xdt{c}", it))
                        dve.tensor_tensor(h4(xdtw[u]), h4(xdt[u]), per_head(wexp, c, HD), ALU.mult).then_inc(f_vec.sem, f_vec.one(f"xdtw{c}"))
                        dve.wait_ge(f_act.sem, f_act.at(f"dec{c}", it))
                        dve.tensor_tensor(h4(mix[u]), h4(dec[u]), sm[u].unsqueeze(1).broadcast_to([P, 4, P]), ALU.mult).then_inc(f_vec.sem, f_vec.one(f"mix{c}"))

                    def back(c, d, g, it):
                        u = c % 2
                        dve.wait_ge(b_pe.sem, b_pe.at(f"off{c}", it))
                        if c:
                            dve.wait_ge(b_vec.sem, b_vec.at(f"y2{c - 1}", it))
                        dve.tensor_tensor(h4(y1), h4(banks[off_bank][:, 0:256]), per_head(ecum16, c, HD), ALU.mult).then_inc(b_vec.sem, b_vec.one(f"y1{c}"))
                        dve.tensor_tensor(h4(tmp), h4(state), per_head(eend, c, HD), ALU.mult).then_inc(b_vec.sem, b_vec.one(f"hdecay{c}"))
                        dve.wait_ge(b_pe.sem, b_pe.at(f"add{c}", it))
                        dve.wait_ge(b_vec.sem, b_vec.at(f"hdecay{c}", it))
                        dve.tensor_tensor(state, banks[add_bank][:, 0:256], tmp, ALU.add).then_inc(b_vec.sem, b_vec.one(f"hadd{c}"))
                        dve.wait_ge(b_pe.sem, b_pe.at(f"y{c}", it))
                        if c >= 2:
                            dve.wait_ge(b_pe.sem, b_pe.at(f"back{c - 2}", it))
                        dve.tensor_tensor(y2[u], banks[y_bank][:, 0:256], y1, ALU.add).then_inc(b_vec.sem, b_vec.one(f"y2{c}"))
                    each_pass(dve, stage, front, back)

        def ssd_gate(outer):
            both, skip, sq = (area(outer, "gate_" + n, 4 * T) for n in ("both", "skip", "square"))
            root, inv = (area(outer, "gate_" + n, 2 * T) for n in ("root", "inverse"))
            with ExitStack() as scope:
                v_s, a_s, pe_s = steps(
                    gate_vec=["both"] + [f"skip{j}" for j in range(4)] + ["gated", "inverse"] + [f"out{j}" for j in range(4)],
                    gate_act=["square", "root0", "root1"], gate_pe=["sum0", "sum1"])
                with nc.Block() as block:
                    @block.vector
                    def _(dve):
                        dve.tensor_tensor(both.rearrange("p (j t) -> p j t", t=T), h3[:, 0:4, :], h3[:, 4:8, ::-1],
                                                   ALU.add).then_inc(v_s.sem, v_s.one("both"))
                        dve.wait_ge(v_s.sem, v_s.at("both"))
                        for j in range(4):
                            dve.scalar_tensor_tensor(skip[:, j * T:(j + 1) * T], p3[:, XS0 + j, :], col("ssd_d", j),
                                                              both[:, j * T:(j + 1) * T], ALU.mult, ALU.add).then_inc(v_s.sem, v_s.one(f"skip{j}"))
                        dve.wait_ge(v_s.sem, v_s.at("skip3"))
                        dve.tensor_tensor(hT[:, 4 * T:8 * T], skip, proj[:, Z0 * T:(Z0 + 4) * T], ALU.mult).then_inc(v_s.sem, v_s.one("gated"))
                        dve.wait_ge(a_s.sem, a_s.at("root1"))
                        dve.reciprocal(inv, root).then_inc(v_s.sem, v_s.one("inverse"))
                        dve.wait_ge(v_s.sem, v_s.at("inverse"))
                        for j in range(4):
                            dve.scalar_tensor_tensor(h3[:, 4 + j, :], h3[:, 4 + j, :], col("ssd_w", j),
                                                              inv[:, (j // 2) * T:(j // 2 + 1) * T], ALU.mult, ALU.mult).then_inc(v_s.sem, v_s.one(f"out{j}"))

                    @block.scalar
                    def _(act):
                        act.wait_ge(v_s.sem, v_s.at("gated"))
                        act.activation(sq, hT[:, 4 * T:8 * T], ACT.Square).then_inc(a_s.sem, a_s.one("square"))
                        for g in range(2):
                            act.wait_ge(pe_s.sem, pe_s.at(f"sum{g}"))
                            act.activation(root[:, g * T:(g + 1) * T], banks[g], ACT.Sqrt, bias=col("eps"),
                                                    scale=1.0 / 256).then_inc(a_s.sem, a_s.one(f"root{g}"))

                    @block.tensor
                    def _(pe):
                        pe.wait_ge(a_s.sem, a_s.at("square"))
                        for g in range(2):
                            for j in range(2):
                                ins = pe.matmul(banks[g], ones, sq[:, (2 * g + j) * T:(2 * g + j + 1) * T],
                                                start=j == 0, stop=j == 1)
                            ins.then_inc(pe_s.sem, pe_s.one(f"sum{g}"))

        with ExitStack() as inner:
            ssd(inner)
        with ExitStack() as inner:
            ssd_gate(inner)

        def rwkv(outer):
            spans = [[xT, 0, 8 * T], [proj, XS0 * T, REV0 * T + 8 * T], [dt_cum, 0, 4 * T],
                     [area(outer, "rw_work", RW_WORDS), 0, RW_WORDS]]

            def take(words):
                for s in spans:
                    if s[1] + words <= s[2]:
                        s[1] += words
                        return s[0][:, s[1] - words:s[1]]
                raise ValueError("no room")

            r_st, v_st, a_t, sg0, sg1, kk, km, b_t = (take(T) for _ in range(8))
            assert spans[0][1] == spans[0][2]
            sg, ka1 = [sg0, sg1], b_t
            low, sq, rk = take(T), take(T), take(T)
            cum, cen, cex, pos, neg, prv = (take(T) for _ in range(6))
            b_i, k_i, v_r = take(T), take(T), take(T)
            x_m = [take(T), take(T)]
            y_m = [take(T), take(T)]
            o_t, osq = take(T), take(T)
            def chunks_of_pairs():
                return take(2 * NC * P).rearrange("p (c w t) -> p c w t", c=NC, w=2)

            kr = [chunks_of_pairs() for _ in range(2)]
            ac = [[chunks_of_pairs() for h in range(2)] for d in range(2)]
            be = [[chunks_of_pairs() for h in range(2)] for d in range(2)]
            x_t = [[take(T), take(T)] for d in range(2)]
            b_tok, k_tok, v_tok = ([take(T) for d in range(2)] for _ in range(3))
            state, added, rhs, sa = (take(P) for _ in range(4))
            vec, mid, carry = take(8), take(4), [take(4), take(4)]
            tanh_ad, gate_in = p3[:, 12, :], p3[:, 13, :]
            y_bank, z_bank, zt_bank = [4, 6], [3, 5], [7, 0]
            turn_bank = [3, 4, 5]
            score_bank = {("ac", 0, 0): 6, ("ac", 0, 1): 7, ("ac", 1, 0): 0, ("ac", 1, 1): 3,
                          ("be", 0, 0): 4, ("be", 0, 1): 5, ("be", 1, 0): 6, ("be", 1, 1): 7}
            nl = len(LEVELS) - 1
            heads = range(2)
            hs = [slice(h * HD, (h + 1) * HD) for h in heads]
            slot_list = ([("turn", n) for n in range(3)]
                         + [("score", m, h, q) for m in ("ac", "be") for h in heads for q in range(2)]
                         + [("x", h) for h in heads]
                         + [(kind, n, h) for n in range(1, nl + 1) for kind in ("y", "z") for h in heads])
            chain_at = {0: 11, 1: 3}
            chain_end = 4 * NC

            def vcol(name):
                return vec[:, RW_VECS.index(name):RW_VECS.index(name) + 1]

            def tile_col(name, ct):
                return cols[:, bass.ds(ct * 8 + (COL["rw"] + RW_VECS.index(name)), 1)]

            def tile_of(ap, ct, first=0):
                return ap[:, bass.ds(ct * T + first * T, T)]

            def level_names(kinds):
                return [f"{k}{n}{h}_%d" for n in range(1, nl + 1) for group in (["y"], ["z", "zt"]) for h in heads
                        for k in group if k in kinds and not (k == "z" and n == nl)]

            def both_dirs(names):
                return [n % d for d in range(2) for n in names]

            scores = [f"{m}{h}{q}_%d" for m in ("ac", "be") for h in heads for q in range(2)]
            masked = scores[:3] + ["xa0_%d", "xt0_%d"] + scores[3:5] + ["xa1_%d", "xt1_%d"] + scores[5:]
            with ExitStack() as scope:
                zero_s, pre_a = steps(rw_zero=[f"{m}{d}{h}" for m in ("ac", "be") for d in range(2) for h in heads],
                                      rw_pre=["tanh", "gate"])
                i_pe, i_act, i_vec = steps(
                    rw_I_pe=both_dirs(["turn0_%d", "turn1_%d", "turn2_%d"] + scores + ["x0_%d", "x1_%d"]
                                             + level_names(["y", "z", "zt"])),
                    rw_I_act=both_dirs(["tok0_%d", "tok1_%d", "tok2_%d", "x0_%d", "x1_%d"] + level_names(["y"])),
                    rw_I_vec=both_dirs(masked + level_names(["z", "zt"])))
                chain = ["%s%d" % (s, c) for c in range(NC) for s in ("rhs", "sa", "s", "o") if not (s == "s" and c == NC - 1)]
                c_pe, c_act, c_vec = steps(
                    rw_C_pe=["^"] + both_dirs([n + "_%d" for n in chain]),
                    rw_C_act=[f"{s}{c}_0" for c in range(NC) for s in ("rhs", "sa")] + ["out_0"]
                    + [f"{s}{c}_1" for c in range(NC) for s in ("rhs", "sa")],
                    rw_C_vec=both_dirs(["zero_%d"] + [f"{s}{c}_%d" for c in range(NC - 1) for s in ("add", "s")]) + ["out_1"])
                e_act, e_vec, e_pool = steps(
                    rw_E_act=both_dirs(["pos_%d", "neg_%d", "prv_%d", "mid_%d"]),
                    rw_E_vec=both_dirs(["cum_%d", "cen_%d", "cex_%d", "kkP_%d", "bI_%d", "carry_%d"]),
                    rw_E_pool=both_dirs(["v_%d", "rP_%d", "kI_%d"]))
                p_pe, p_act, p_vec, p_pool = steps(
                    rw_P_pe=["a", "w0", "w1", "g", "norm", "bonus"], rw_P_act=["a", "w0", "w1", "g", "sq", "root"],
                    rw_P_vec=["kk0", "ka", "km", "rk", "nmax", "ninv", "kk", "b", "bonus"],
                    rw_P_pool=["low", "vec", "r", "v"])
                f_pe, f_act, f_vec = steps(
                    rw_F_pe=["mean", "var"], rw_F_act=["^", "osq", "oroot"],
                    rw_F_vec=["^", "centre", "oinv", "on", "og", "ob", "res"])

                def wait_chain(engine, ct, d, before):
                    if d:
                        engine.wait_ge(c_pe.sem, c_pe.passes(ct))
                    elif before is not None:
                        engine.wait_ge(c_pe.sem, c_pe.at("o3_0", before))

                def run(engine, slot_I, prep, chain_step, elementwise, finish):
                    slots_of_unit = range(len(slot_list))
                    for t in slots_of_unit:
                        prep(t, 0, None)
                    for t in slots_of_unit:
                        elementwise(t, 0, 0, None)
                    for t in slots_of_unit:
                        slot_I(t, 0, 0, None)
                        elementwise(t, 0, 1, None)
                    with fori(engine, 0, 3) as ct:
                        for t in slots_of_unit:
                            slot_I(t, ct, 1, None)
                            prep(t, ct + 1, ct)
                            chain_step(t - chain_at[0], ct, 0)
                            elementwise(t, ct + 1, 0, ct)
                        for t in slots_of_unit:
                            slot_I(t, ct + 1, 0, ct)
                            chain_step(t - chain_at[1], ct, 1)
                            finish(t, ct)
                            elementwise(t, ct + 1, 1, ct)
                    for t in slots_of_unit:
                        slot_I(t, 3, 1, None)
                        chain_step(t - chain_at[0], 3, 0)
                    for j in range(chain_end + 1):
                        chain_step(j, 3, 1)
                    for t in slots_of_unit:
                        finish(t, 3)

                with nc.Block() as block:
                    @block.sync
                    def _(sp):
                        ring.prefetch(sp, dram["ab_out"])
                        sp.wait_ge(e_vec.sem, e_vec.at("carry_1", 3))
                        sp.wait_ge(e_pool.sem, e_pool.at("kI_1", 3))
                        sp.dma_start(xT, dram["xT"]).then_inc(loads, 16)
                        sp.wait_ge(loads, 32)

                    @block.gpsimd
                    def _(pool):
                        def prep(t, ct, before):
                            if t != 0:
                                return
                            if before is not None:
                                pool.wait_ge(p_vec.sem, p_vec.at("bonus", before))
                                pool.wait_ge(p_pe.sem, p_pe.at("g", before))
                                pool.wait_ge(p_act.sem, p_act.at("w1", before))
                                pool.wait_ge(e_pool.sem, e_pool.at("kI_1", before))
                                hold(pool, "pool")
                            pool.tensor_copy(low.rearrange("p (m c) -> p m c", m=4),
                                             lora.rearrange("p (m c) -> p m c", m=4)[:, :, bass.ds(ct * P, P)]
                                             ).then_inc(p_pool.sem, p_pool.one("low"))
                            pool.tensor_copy(vec, cols[:, bass.ds(ct * 8 + COL["rw"], 8)]).then_inc(p_pool.sem, p_pool.one("vec"))
                            pool.tensor_copy(r_st, tile_of(proj, ct)).then_inc(p_pool.sem, p_pool.one("r"))
                            pool.tensor_copy(v_st, tile_of(proj, ct, 8)).then_inc(p_pool.sem, p_pool.one("v"))

                        def elementwise(t, ct, d, before):
                            if t != 0:
                                return
                            pool.wait_ge(p_pool.sem, p_pool.at("v", ct))
                            if d:
                                pool.wait_ge(i_pe.sem, i_pe.at("be11_0", ct))
                            elif before is not None:
                                pool.wait_ge(i_pe.sem, i_pe.at("be11_1", before))
                            hold(pool, "pool")
                            pool.tensor_copy(v_r, dirs[d](v_st)).then_inc(e_pool.sem, e_pool.one(f"v_{d}"))
                            pool.wait_ge(e_act.sem, e_act.at(f"neg_{d}", ct))
                            wait_chain(pool, ct, d, before)
                            pool.tensor_tensor(kr[d][:, :, 1, :], by_chunk(dirs[d](r_st)), by_chunk(pos), ALU.mult
                                               ).then_inc(e_pool.sem, e_pool.one(f"rP_{d}"))
                            pool.wait_ge(p_vec.sem, p_vec.at("b", ct))
                            pool.tensor_tensor(k_i, dirs[d](km), neg, ALU.mult).then_inc(e_pool.sem, e_pool.one(f"kI_{d}"))

                        def nothing(t, *unit):
                            pass

                        run(pool, nothing, prep, nothing, elementwise, nothing)

                    @block.tensor
                    def _(pe):
                        pe.wait_ge(pre_a.sem, pre_a.at("gate"))
                        pe.sem_inc(c_pe.sem, 1)

                        def prep(t, ct, before):
                            if t == 4:
                                pe.wait_ge(p_pool.sem, p_pool.at("low", ct))
                                if before is not None:
                                    pe.wait_ge(f_act.sem, f_act.passes(before))
                                    pe.wait_ge(f_vec.sem, f_vec.passes(before))
                                pe.matmul(banks[1], low[64:P, 2 * P:3 * P], tanh_ad[64:P, :], start=True, stop=True
                                          ).then_inc(p_pe.sem, p_pe.one("a"))
                                pe.matmul(banks[2], low[0:64, 0:P], tanh_ad[0:64, :], start=True, stop=True
                                          ).then_inc(p_pe.sem, p_pe.one("w0"))
                            if t == 5:
                                pe.wait_ge(p_act.sem, p_act.at("a", ct))
                                pe.matmul(banks[1], low[0:64, P:2 * P], tanh_ad[0:64, :], start=True, stop=True
                                          ).then_inc(p_pe.sem, p_pe.one("w1"))
                            if t == 6:
                                pe.wait_ge(p_act.sem, p_act.at("w0", ct))
                                pe.matmul(banks[2], low[:, 3 * P:4 * P], gate_in, start=True, stop=True
                                          ).then_inc(p_pe.sem, p_pe.one("g"))
                            if t == 8:
                                pe.wait_ge(p_act.sem, p_act.at("sq", ct))
                                pe.matmul(banks[1], blk, sq, start=True, stop=True).then_inc(p_pe.sem, p_pe.one("norm"))
                                pe.wait_ge(p_vec.sem, p_vec.at("rk", ct))
                                pe.matmul(banks[2], blk, rk, start=True, stop=True).then_inc(p_pe.sem, p_pe.one("bonus"))

                        def slot_I(t, ct, d, before):
                            kind, *which = slot_list[t]
                            prev = ("_0", ct) if d else ("_1", before)
                            if kind == "turn":
                                n, = which
                                src = (b_i, k_i, v_r)[n]
                                s, name = ((e_vec, "bI"), (e_pool, "kI"), (e_pool, "v"))[n]
                                pe.wait_ge(s.sem, s.at(f"{name}_{d}", ct))
                                if prev[1] is not None:
                                    s, name = ((i_vec, f"z{nl - 1}0"), (i_act, f"y{nl}0"), (i_vec, f"z{nl - 1}1"))[n]
                                    pe.wait_ge(s.sem, s.at(name + prev[0], prev[1]))
                                for c in range(NC):
                                    ins = pe.transpose(chunk(banks[turn_bank[n]], c), chunk(src, c), ident)
                                ins.then_inc(i_pe.sem, i_pe.one(f"turn{n}_{d}"))
                            if kind == "score":
                                m, h, q = which
                                if which == ["ac", 0, 0]:
                                    pe.wait_ge(e_vec.sem, e_vec.at(f"kkP_{d}", ct))
                                    pe.wait_ge(e_pool.sem, e_pool.at(f"rP_{d}", ct))
                                before_in_bank = {("ac", 0, 0): (i_act, f"y{nl}1"), ("ac", 0, 1): (i_vec, f"zt{nl}0"),
                                                  ("ac", 1, 0): (i_vec, f"zt{nl}1")}
                                now_in_bank = {("ac", 1, 1): (i_act, "tok0"), ("be", 0, 0): (i_act, "tok1"),
                                               ("be", 0, 1): (i_act, "tok2"), ("be", 1, 0): (i_vec, "ac00"),
                                               ("be", 1, 1): (i_vec, "ac01")}
                                if (m, h, q) in now_in_bank:
                                    s, name = now_in_bank[m, h, q]
                                    pe.wait_ge(s.sem, s.at(f"{name}_{d}", ct))
                                elif prev[1] is not None:
                                    s, name = before_in_bank[m, h, q]
                                    pe.wait_ge(s.sem, s.at(name + prev[0], prev[1]))
                                bank = banks[score_bank[m, h, q]].rearrange("p (c w) -> p c w", c=2)
                                for e in range(2):
                                    c = 2 * q + e
                                    ins = pe.matmul(bank[:, e, :], chunk(b_i if m == "ac" else k_i, c)[hs[h], :],
                                                    kr[d][hs[h], c, :, :], start=True, stop=True)
                                ins.then_inc(i_pe.sem, i_pe.one(f"{m}{h}{q}_{d}"))
                            if kind == "x":
                                h, = which
                                pe.wait_ge(i_vec.sem, i_vec.at(f"xt{h}_{d}", ct))
                                pe.wait_ge(i_vec.sem, i_vec.at(("ac11_%d", "be01_%d")[h] % d, ct))
                                for c in range(NC):
                                    ins = pe.transpose(chunk(banks[z_bank[h]], c), chunk(x_t[d][h], c), ident)
                                ins.then_inc(i_pe.sem, i_pe.one(f"x{h}_{d}"))
                            if kind == "y":
                                n, h = which
                                if n == 1:
                                    pe.wait_ge(i_act.sem, i_act.at(f"x{h}_{d}", ct))
                                    pe.wait_ge(i_vec.sem, i_vec.at(f"be11_{d}", ct))
                                else:
                                    pe.wait_ge(i_vec.sem, i_vec.at(f"zt{n - 1}{h}_{d}", ct))
                                for c in range(NC):
                                    ins = pe.matmul(chunk(banks[y_bank[h]], c), ac[d][h][:, c, 0, :], chunk(x_m[h], c),
                                                    start=True, stop=True)
                                ins.then_inc(i_pe.sem, i_pe.one(f"y{n}{h}_{d}"))
                            if kind == "z":
                                n, h = which
                                pe.wait_ge(i_act.sem, i_act.at(f"y{n}{h}_{d}", ct))
                                if n < nl:
                                    for c in range(NC):
                                        ins = pe.matmul(chunk(banks[z_bank[h]], c), chunk(x_t[d][h], c), chunk(y_m[h], c),
                                                        start=True, stop=True)
                                    ins.then_inc(i_pe.sem, i_pe.one(f"z{n}{h}_{d}"))
                                for c in range(NC):
                                    ins = pe.matmul(chunk(banks[zt_bank[h]], c), chunk(y_m[h], c), chunk(x_t[d][h], c),
                                                    start=True, stop=True)
                                ins.then_inc(i_pe.sem, i_pe.one(f"zt{n}{h}_{d}"))

                        def chain_step(j, ct, d):
                            if not 0 <= j < chain_end:
                                return
                            c, kind = j // 4, ("rhs", "sa", "s", "o")[j % 4]
                            if kind == "rhs":
                                pe.wait_ge(c_vec.sem, c_vec.at(f"s{c - 1}_{d}" if c else f"zero_{d}", ct))
                                if c == 0:
                                    pe.wait_ge(i_vec.sem, i_vec.at(f"zt{nl}1_{d}", ct))
                                    if d == 0 and not (isinstance(ct, int) and ct == 3):
                                        pe.wait_ge(p_act.sem, p_act.at("root", ct + 1))
                                        pe.wait_ge(p_vec.sem, p_vec.at("bonus", ct + 1))
                                    elif d == 0:
                                        pe.wait_ge(f_act.sem, f_act.passes(ct))
                                    else:
                                        pe.wait_ge(c_act.sem, c_act.at("out_0", ct))
                                pe.matmul(banks[1][:, 0:P], kr[d][:, c, 0, :], state, start=True, stop=False)
                                for h in heads:
                                    ins = pe.matmul(banks[1][:, hs[h]], be[d][h][:, c, 0, :], chunk(v_tok[d], c)[:, hs[h]],
                                                    start=False, stop=h == 1)
                                ins.then_inc(c_pe.sem, c_pe.one(f"rhs{c}_{d}"))
                            if kind == "sa":
                                pe.wait_ge(c_act.sem, c_act.at(f"rhs{c}_{d}", ct))
                                for h in heads:
                                    ins = pe.matmul(banks[1][:, P + h * HD:P + (h + 1) * HD], chunk(x_t[d][h], c), rhs[:, hs[h]],
                                                    start=True, stop=True)
                                ins.then_inc(c_pe.sem, c_pe.one(f"sa{c}_{d}"))
                            if kind == "s" and c < NC - 1:
                                pe.wait_ge(c_act.sem, c_act.at(f"sa{c}_{d}", ct))
                                pe.matmul(banks[1][:, 2 * P:3 * P], chunk(b_tok[d], c), sa, start=True, stop=False)
                                pe.matmul(banks[1][:, 2 * P:3 * P], chunk(k_tok[d], c), chunk(v_tok[d], c),
                                          start=False, stop=True).then_inc(c_pe.sem, c_pe.one(f"s{c}_{d}"))
                            if kind == "o":
                                pe.wait_ge(c_act.sem, c_act.at(f"sa{c}_{d}", ct))
                                out = chunk(banks[2], c)
                                pe.matmul(out, state, kr[d][:, c, 1, :], start=True, stop=False)
                                for h in heads:
                                    pe.matmul(out[hs[h], :], sa[:, hs[h]], ac[d][h][:, c, 1, :], start=False, stop=False)
                                    ins = pe.matmul(out[hs[h], :], chunk(v_tok[d], c)[:, hs[h]], be[d][h][:, c, 1, :],
                                                    start=False, stop=True)
                                ins.then_inc(c_pe.sem, c_pe.one(f"o{c}_{d}"))

                        def finish(t, ct):
                            if t == 20:
                                pe.wait_ge(c_vec.sem, c_vec.at("out_1", ct))
                                pe.matmul(banks[1], blk, o_t, start=True, stop=True).then_inc(f_pe.sem, f_pe.one("mean"))
                            if t == 23:
                                pe.wait_ge(f_act.sem, f_act.at("osq", ct))
                                pe.matmul(banks[2], blk, osq, start=True, stop=True).then_inc(f_pe.sem, f_pe.one("var"))

                        def nothing(t, *unit):
                            pass

                        run(pe, slot_I, prep, chain_step, nothing, finish)

                    @block.scalar
                    def _(act):
                        act.activation(tanh_ad[0:64, :], tanh_ad[0:64, :], ACT.Tanh).then_inc(pre_a.sem, pre_a.one("tanh"))
                        act.activation(gate_in, gate_in, ACT.Sigmoid).then_inc(pre_a.sem, pre_a.one("gate"))
                        act.sem_inc(f_act.sem, 1)

                        def prep(t, ct, before):
                            if t == 4:
                                act.wait_ge(p_pool.sem, p_pool.at("vec", ct))
                                if before is not None:
                                    act.wait_ge(e_vec.sem, e_vec.at("carry_1", before))
                                    act.wait_ge(p_vec.sem, p_vec.at("bonus", before))
                                for name, bank, dst, bias in (("a", 1, a_t, "a0"), ("w0", 2, sg0, "w0f")):
                                    act.wait_ge(p_pe.sem, p_pe.at(name, ct))
                                    act.activation(dst, banks[bank], ACT.Sigmoid, bias=vcol(bias)).then_inc(p_act.sem, p_act.one(name))
                            if t == 5:
                                act.wait_ge(p_pe.sem, p_pe.at("w1", ct))
                                act.activation(sg1, banks[1], ACT.Sigmoid, bias=vcol("w0b")).then_inc(p_act.sem, p_act.one("w1"))
                            if t == 7:
                                act.wait_ge(p_pe.sem, p_pe.at("g", ct))
                                act.wait_ge(p_vec.sem, p_vec.at("km", ct))
                                act.activation(tile_of(proj, ct, 4), banks[2], ACT.Copy).then_inc(p_act.sem, p_act.one("g"))
                                act.activation(sq, kk, ACT.Square).then_inc(p_act.sem, p_act.one("sq"))
                            if t == 8:
                                act.wait_ge(p_pe.sem, p_pe.at("norm", ct))
                                act.activation(sq, banks[1], ACT.Sqrt).then_inc(p_act.sem, p_act.one("root"))

                        def slot_I(t, ct, d, before):
                            kind, *which = slot_list[t]
                            if kind == "turn":
                                n, = which
                                if n == 0:
                                    wait_chain(act, ct, d, before)
                                act.wait_ge(i_pe.sem, i_pe.at(f"turn{n}_{d}", ct))
                                act.activation((b_tok, k_tok, v_tok)[n][d], banks[turn_bank[n]], ACT.Copy
                                               ).then_inc(i_act.sem, i_act.one(f"tok{n}_{d}"))
                            if kind == "x":
                                h, = which
                                act.wait_ge(i_pe.sem, i_pe.at(f"x{h}_{d}", ct))
                                act.activation(x_m[h], banks[z_bank[h]], ACT.Copy).then_inc(i_act.sem, i_act.one(f"x{h}_{d}"))
                            if kind == "y":
                                n, h = which
                                act.wait_ge(i_pe.sem, i_pe.at(f"y{n}{h}_{d}", ct))
                                act.activation(y_m[h], banks[y_bank[h]], ACT.Copy).then_inc(i_act.sem, i_act.one(f"y{n}{h}_{d}"))

                        def chain_step(j, ct, d):
                            if 0 <= j < chain_end and j % 4 < 2:
                                c, kind = j // 4, ("rhs", "sa")[j % 4]
                                act.wait_ge(c_pe.sem, c_pe.at(f"{kind}{c}_{d}", ct))
                                if kind == "rhs":
                                    act.activation(rhs, banks[1][:, 0:P], ACT.Copy).then_inc(c_act.sem, c_act.one(f"rhs{c}_{d}"))
                                else:
                                    act.activation(sa, banks[1][:, P:2 * P], ACT.Copy).then_inc(c_act.sem, c_act.one(f"sa{c}_{d}"))
                            if j == chain_end and d == 0:
                                act.wait_ge(c_pe.sem, c_pe.at("o3_0", ct))
                                act.wait_ge(f_vec.sem, f_vec.passes(ct))
                                act.activation(o_t, banks[2], ACT.Copy).then_inc(c_act.sem, c_act.one("out_0"))

                        def elementwise(t, ct, d, before):
                            if t != 14:
                                return
                            if d:
                                act.wait_ge(e_vec.sem, e_vec.at("carry_0", ct))
                                act.wait_ge(e_pool.sem, e_pool.at("kI_0", ct))
                            elif before is not None:
                                act.wait_ge(e_vec.sem, e_vec.at("carry_1", before))
                                act.wait_ge(e_pool.sem, e_pool.at("kI_1", before))
                            act.wait_ge(e_vec.sem, e_vec.at(f"cex_{d}", ct))
                            act.activation(pos, cen, ACT.Exp, scale=-DECAY_SCALE).then_inc(e_act.sem, e_act.one(f"pos_{d}"))
                            act.activation(neg, cen, ACT.Exp, scale=DECAY_SCALE).then_inc(e_act.sem, e_act.one(f"neg_{d}"))
                            act.activation(prv, cex, ACT.Exp, scale=-DECAY_SCALE).then_inc(e_act.sem, e_act.one(f"prv_{d}"))
                            act.activation(mid, by_chunk(cum)[:, :, HD - 1], ACT.Exp, scale=-DECAY_SCALE
                                           ).then_inc(e_act.sem, e_act.one(f"mid_{d}"))

                        def finish(t, ct):
                            if t == 21:
                                act.wait_ge(f_vec.sem, f_vec.at("centre", ct))
                                act.activation(osq, o_t, ACT.Square).then_inc(f_act.sem, f_act.one("osq"))
                            if t == 24:
                                act.wait_ge(f_pe.sem, f_pe.at("var", ct))
                                act.activation(osq, banks[2], ACT.Sqrt, bias=col("gneps"), scale=1.0 / HD
                                               ).then_inc(f_act.sem, f_act.one("oroot"))

                        run(act, slot_I, prep, chain_step, elementwise, finish)

                    @block.vector
                    def _(dve):
                        dve.sem_inc(f_vec.sem, 1)
                        causal = table("strict", 2 * P).bitcast(U32)

                        def prep(t, ct, before):
                            k_in = tile_of(proj, ct, 4)
                            if t == 4:
                                dve.wait_ge(p_pool.sem, p_pool.at("v", ct))
                                if before is not None:
                                    dve.wait_ge(e_vec.sem, e_vec.at("carry_1", before))
                                dve.tensor_scalar(kk, k_in, vcol("kk"), None, ALU.mult).then_inc(p_vec.sem, p_vec.one("kk0"))
                            if t == 5:
                                dve.wait_ge(p_act.sem, p_act.at("a", ct))
                                dve.tensor_scalar(ka1, a_t, vcol("ka"), vcol("ka"), ALU.mult, ALU.subtract).then_inc(p_vec.sem, p_vec.one("ka"))
                                dve.wait_ge(p_vec.sem, p_vec.at("ka", ct))
                                if before is not None:
                                    dve.wait_ge(e_pool.sem, e_pool.at("kI_1", before))
                                dve.scalar_tensor_tensor(km, ka1, 1.0, k_in, ALU.add, ALU.mult).then_inc(p_vec.sem, p_vec.one("km"))
                            if t == 6:
                                dve.wait_ge(p_vec.sem, p_vec.at("km", ct))
                                if before is not None:
                                    dve.wait_ge(p_pe.sem, p_pe.at("bonus", before))
                                dve.scalar_tensor_tensor(rk, r_st, vcol("rk"), km, ALU.mult, ALU.mult).then_inc(p_vec.sem, p_vec.one("rk"))
                            if t == 9:
                                dve.wait_ge(p_act.sem, p_act.at("root", ct))
                                dve.tensor_scalar(sq, sq, 1e-12, None, ALU.max).then_inc(p_vec.sem, p_vec.one("nmax"))
                                dve.wait_ge(p_vec.sem, p_vec.at("nmax", ct))
                                dve.reciprocal(sq, sq).then_inc(p_vec.sem, p_vec.one("ninv"))
                            if t == 10:
                                dve.wait_ge(p_vec.sem, p_vec.at("ninv", ct))
                                dve.tensor_tensor(kk, kk, sq, ALU.mult).then_inc(p_vec.sem, p_vec.one("kk"))
                                dve.wait_ge(p_vec.sem, p_vec.at("kk", ct))
                                dve.tensor_tensor(b_t, kk, a_t, ALU.mult).then_inc(p_vec.sem, p_vec.one("b"))
                                dve.wait_ge(p_pe.sem, p_pe.at("bonus", ct))
                                dve.tensor_tensor(tile_of(hT, ct), banks[2], v_st, ALU.mult).then_inc(p_vec.sem, p_vec.one("bonus"))

                        def zero_masked():
                            for m, kept in (("ac", ac), ("be", be)):
                                for d in range(2):
                                    for h in heads:
                                        dve.memset(kept[d][h], 0.0).then_inc(zero_s.sem, zero_s.one(f"{m}{d}{h}"))
                            dve.wait_ge(zero_s.sem, zero_s.at("be11"))

                        def elementwise(t, ct, d, before):
                            if t == 0 and before is None and d == 0:
                                zero_masked()
                            if t == 12:
                                dve.wait_ge(p_act.sem, p_act.at("w1", ct))
                                if d:
                                    dve.wait_ge(e_act.sem, e_act.at("mid_0", ct))
                                elif before is not None:
                                    dve.wait_ge(e_act.sem, e_act.at("mid_1", before))
                                dve.tensor_tensor_scan(cum, table("reset", T), dirs[d](sg[d]), 0.0, ALU.mult, ALU.add
                                                       ).then_inc(e_vec.sem, e_vec.one(f"cum_{d}"))
                                dve.wait_ge(e_vec.sem, e_vec.at(f"cum_{d}", ct))
                                dve.tensor_tensor(by_chunk(cen), by_chunk(cum), by_chunk(cum)[:, :, HD - 1:HD].broadcast_to([P, NC, P]),
                                                  ALU.subtract).then_inc(e_vec.sem, e_vec.one(f"cen_{d}"))
                                dve.wait_ge(e_vec.sem, e_vec.at(f"cen_{d}", ct))
                                dve.tensor_tensor(cex, cen, dirs[d](sg[d]), ALU.subtract).then_inc(e_vec.sem, e_vec.one(f"cex_{d}"))
                            if t == (22 if d else 28):
                                dve.wait_ge(e_act.sem, e_act.at(f"mid_{d}", ct))
                                wait_chain(dve, ct, d, before)
                                dve.scalar_tensor_tensor(kr[d][:, :, 0, :], by_chunk(dirs[d](kk)), -1.0, by_chunk(prv),
                                                         ALU.mult, ALU.mult).then_inc(e_vec.sem, e_vec.one(f"kkP_{d}"))
                                if d:
                                    dve.wait_ge(i_pe.sem, i_pe.at("be11_0", ct))
                                elif before is not None:
                                    dve.wait_ge(i_pe.sem, i_pe.at("be11_1", before))
                                dve.tensor_tensor(b_i, dirs[d](b_t), neg, ALU.mult).then_inc(e_vec.sem, e_vec.one(f"bI_{d}"))
                                dve.tensor_tensor(carry[d][:, 0:3], by_chunk(pos)[:, 0:3, P - 1], mid[:, 1:4], ALU.mult
                                                  ).then_inc(e_vec.sem, e_vec.one(f"carry_{d}"))

                        def slot_I(t, ct, d, before):
                            kind, *which = slot_list[t]
                            if kind == "score":
                                m, h, q = which
                                if which == ["ac", 0, 0]:
                                    wait_chain(dve, ct, d, before)
                                dve.wait_ge(i_pe.sem, i_pe.at(f"{m}{h}{q}_{d}", ct))
                                hold(dve, "vec")
                                dve.copy_predicated(
                                    (ac if m == "ac" else be)[d][h][:, 2 * q:2 * q + 2, :, :].rearrange("p c w t -> p c (w t)"),
                                    causal.unsqueeze(1).broadcast_to([P, 2, 2 * P]),
                                    banks[score_bank[m, h, q]].rearrange("p (c w) -> p c w", c=2)).then_inc(i_vec.sem, i_vec.one(f"{m}{h}{q}_{d}"))
                                if which in (["ac", 1, 0], ["be", 0, 0]):
                                    x = 0 if m == "ac" else 1
                                    dve.wait_ge(i_vec.sem, i_vec.at(f"ac{x}1_{d}", ct))
                                    dve.tensor_tensor(by_chunk(x_t[d][x]), ac[d][x][:, :, 0, :],
                                                      over_chunks(table("up")), ALU.mult).then_inc(i_vec.sem, i_vec.one(f"xa{x}_{d}"))
                                    dve.wait_ge(i_vec.sem, i_vec.at(f"xa{x}_{d}", ct))
                                    dve.tensor_tensor(by_chunk(x_t[d][x]), by_chunk(x_t[d][x]), over_chunks(ident), ALU.add
                                                      ).then_inc(i_vec.sem, i_vec.one(f"xt{x}_{d}"))
                            if kind == "z":
                                n, h = which
                                if n < nl:
                                    dve.wait_ge(i_pe.sem, i_pe.at(f"z{n}{h}_{d}", ct))
                                    hold(dve, "vec")
                                    dve.copy_predicated(by_chunk(x_m[h]), over_chunks(table("low", P, n * P).bitcast(U32)),
                                                        by_chunk(banks[z_bank[h]])).then_inc(i_vec.sem, i_vec.one(f"z{n}{h}_{d}"))
                                dve.wait_ge(i_pe.sem, i_pe.at(f"zt{n}{h}_{d}", ct))
                                hold(dve, "vec")
                                dve.copy_predicated(by_chunk(x_t[d][h]), over_chunks(table("up", P, n * P).bitcast(U32)),
                                                    by_chunk(banks[zt_bank[h]])).then_inc(i_vec.sem, i_vec.one(f"zt{n}{h}_{d}"))

                        def chain_step(j, ct, d):
                            if j == 0:
                                dve.wait_ge(c_pe.sem, c_pe.at("o3_0", ct) if d else c_pe.passes(ct))
                                dve.memset(state, 0.0).then_inc(c_vec.sem, c_vec.one(f"zero_{d}"))
                            if 0 <= j < 4 * (NC - 1) and j % 4 >= 2:
                                c = j // 4
                                if j % 4 == 2:
                                    dve.wait_ge(c_pe.sem, c_pe.at(f"s{c}_{d}", ct))
                                    dve.tensor_tensor(added, banks[1][:, 2 * P:3 * P], state, ALU.add).then_inc(c_vec.sem, c_vec.one(f"add{c}_{d}"))
                                else:
                                    dve.wait_ge(c_vec.sem, c_vec.at(f"add{c}_{d}", ct))
                                    dve.wait_ge(c_pe.sem, c_pe.at(f"o{c}_{d}", ct))
                                    dve.scalar_tensor_tensor(state, added, carry[d][:, c:c + 1], blk, ALU.mult, ALU.mult
                                                             ).then_inc(c_vec.sem, c_vec.one(f"s{c}_{d}"))
                            if j == chain_end and d:
                                dve.wait_ge(c_pe.sem, c_pe.at("o3_1", ct))
                                dve.wait_ge(c_act.sem, c_act.at("out_0", ct))
                                dve.tensor_tensor(o_t, banks[2][:, ::-1], o_t, ALU.add).then_inc(c_vec.sem, c_vec.one("out_1"))

                        def finish(t, ct):
                            if t == 20:
                                dve.wait_ge(f_pe.sem, f_pe.at("mean", ct))
                                dve.scalar_tensor_tensor(o_t, banks[1], -1.0 / HD, o_t, ALU.mult, ALU.add).then_inc(f_vec.sem, f_vec.one("centre"))
                            if t == 25:
                                dve.wait_ge(f_act.sem, f_act.at("oroot", ct))
                                dve.reciprocal(osq, osq).then_inc(f_vec.sem, f_vec.one("oinv"))
                                dve.wait_ge(f_vec.sem, f_vec.at("oinv", ct))
                                dve.tensor_tensor(o_t, o_t, osq, ALU.mult).then_inc(f_vec.sem, f_vec.one("on"))
                            if t == 27:
                                dve.wait_ge(f_vec.sem, f_vec.at("on", ct))
                                dve.tensor_scalar(o_t, o_t, tile_col("gnw", ct), tile_col("gnb", ct), ALU.mult, ALU.add
                                                  ).then_inc(f_vec.sem, f_vec.one("og"))
                                dve.wait_ge(f_vec.sem, f_vec.at("og", ct))
                                dve.tensor_tensor(o_t, o_t, tile_of(hT, ct), ALU.add).then_inc(f_vec.sem, f_vec.one("ob"))
                            if t == 29:
                                dve.wait_ge(f_vec.sem, f_vec.at("ob", ct))
                                dve.tensor_tensor(tile_of(hT, ct), o_t, tile_of(proj, ct, 4), ALU.mult).then_inc(f_vec.sem, f_vec.one("res"))

                        run(dve, slot_I, prep, chain_step, elementwise, finish)

        with ExitStack() as inner:
            rwkv(inner)
        clear_semaphores()
        with ExitStack() as inner:
            rhs = halves(inner, "mix0_h", KD)
            add_to_residual(inner, "mix0_out", dram["ab_out"], rhs, dram["wk0"], SplitSource(inner, "mix0", h3, rhs))
        mixer0.close()

        def cross_attention(n, outer):
            kT, vt, qT = (area(outer, f"xa{n}_{m}", w) for m, w in (("k", KD * MEM), ("v", KD * MEM), ("q", KD * T)))
            v3 = vt.rearrange("p (b d) -> p b d", b=2)
            rhs = halves(outer, f"xa{n}_h", KD)
            with ExitStack() as inner:
                memn = halves(inner, f"mem{n}", KD, MEM)
                name = f"keys{n}"
                wk = Projection(inner, name, dram[f"wk{n}"], memn, KD, n=MEM)
                project(name, wk, NormSource(inner, name, mem3, memn, f"mem{n}", MEM, keep=None if n else mem_inv, kept=mem_inv if n else None),
                        vector=lambda dve, i, u: dve.tensor_copy(kT[:, bass.ds(i * (2 * MEM) + u * MEM, MEM)], banks[u][:, 0:MEM]),
                        following=dram[f"wv{n}"])
                name = f"values{n}"
                wv = Projection(inner, name, dram[f"wv{n}"], memn, 4, k=4, cuts=2, token_major=True)

                def values(dve, i, u):
                    for b in range(2):
                        ins = dve.tensor_copy(v3[:, b, bass.ds(i * 512 + u * 256, 256)], banks[2 * u + b][:, 0:256])
                    return ins
                project(name, wv, vector=values, following=dram[f"wq{n}"])
            with ExitStack() as inner:
                name = f"queries{n}"
                wq = Projection(inner, name, dram[f"wq{n}"], rhs, KD)
                project(name, wq, NormSource(inner, name, x3, rhs, f"xa{n}", squares=x_squares), scalar=lambda act, i, u: act.activation(
                    qT[:, bass.ds(i * (2 * T) + u * T, T)], banks[u], ACT.Copy, scale=1.0 / 16), reader="a")

            prob, prob_t = ([area(outer, f"xa{n}_{m}{u}", 4 * MEM) for u in range(2)] for m in ("prob", "probt"))
            sums = area(outer, f"xa{n}_sums", 16)
            top, total = ([sums[:, 8 * m + 4 * u:8 * m + 4 * u + 4] for u in range(2)] for m in range(2))
            k3, q3 = kT.rearrange("p (n m) -> p n m", m=MEM), qT.rearrange("p (n t) -> p n t", t=T)
            heads = range(D // 256)
            sc_s, sa_s, sv_s = steps(**{f"xa{n}_scores": ["s0", "s1"], f"xa{n}_exp": [f"exp{c}" for c in range(NC)],
                                        f"xa{n}_top": ["top0", "top1", "minus"]})
            pe_s, a_s, v_s = steps(**{f"xa{n}_pe": ["turn0", "turn1", "o0", "o1"], f"xa{n}_act": ["p0", "o0", "o1"],
                                      f"xa{n}_vec": ["total", "prob", "p1", "lo0", "lo1"]})

            def in_turn(scores, rest):
                scores(0)
                for h in heads:
                    if h + 1 < len(heads):
                        scores(h + 1)
                    rest(h)

            def score(h, c):
                return banks[2 * (h % 2) + c // 2][:, (c % 2) * MEM:(c % 2 + 1) * MEM]

            def prob_of(h):
                return prob[h % 2].rearrange("p (c m) -> p c m", c=NC)

            def turned(h):
                return prob_t[h % 2].rearrange("p (b t) -> p b t", b=2)

            with nc.Block() as block:
                @block.sync
                def _(sp):
                    ring.prefetch(sp, dram[f"wo{n}"])

                @block.tensor
                def _(pe):
                    def scores(h):
                        if h >= 2:
                            pe.wait_ge(sa_s.sem, sa_s.at("exp3", h - 2))
                        for c in range(NC):
                            for k in range(2):
                                ins = pe.matmul(score(h, c), chunk(q3[:, 2 * h + k, :], c), k3[:, 2 * h + k, :],
                                                start=k == 0, stop=k == 1)
                            if c % 2:
                                ins.then_inc(sc_s.sem, sc_s.one(f"s{c // 2}"))

                    def rest(h):
                        pe.wait_ge(v_s.sem, v_s.at("prob", h))
                        for b in range(2):
                            if h:
                                s = a_s if b == 0 else v_s
                                pe.wait_ge(s.sem, s.at(f"p{b}", h - 1))
                            for c in range(NC):
                                ins = pe.transpose(chunk(banks[4 + b], c), prob_of(h)[:, c, b * P:(b + 1) * P], ident)
                            ins.then_inc(pe_s.sem, pe_s.one(f"turn{b}"))
                        pe.wait_ge(a_s.sem, a_s.at("p0", h))
                        pe.wait_ge(v_s.sem, v_s.at("p1", h))
                        for d in range(2):
                            if h:
                                pe.wait_ge(v_s.sem, v_s.at(f"lo{d}", h - 1))
                            for b in range(2):
                                ins = pe.matmul(banks[6 + d], v3[:, b, h * 256 + d * P:h * 256 + (d + 1) * P],
                                                turned(h)[:, b, :], start=b == 0, stop=b == 1)
                            ins.then_inc(pe_s.sem, pe_s.one(f"o{d}"))
                    in_turn(scores, rest)

                @block.vector
                def _(dve):
                    def scores(h):
                        if h >= 2:
                            dve.wait_ge(sa_s.sem, sa_s.at("exp3", h - 2))
                        for b in range(2):
                            dve.wait_ge(sc_s.sem, sc_s.at(f"s{b}", h))
                            dve.tensor_reduce(top[h % 2][:, 2 * b:2 * b + 2], banks[2 * (h % 2) + b].rearrange("p (c m) -> p c m", c=2),
                                              AXX, ALU.max).then_inc(sv_s.sem, sv_s.one(f"top{b}"))
                        dve.wait_ge(sv_s.sem, sv_s.at("top1", h))
                        dve.tensor_scalar(top[h % 2], top[h % 2], -1.0, None, ALU.mult).then_inc(sv_s.sem, sv_s.one("minus"))

                    def rest(h):
                        dve.wait_ge(sa_s.sem, sa_s.at("exp3", h))
                        dve.reciprocal(total[h % 2], total[h % 2]).then_inc(v_s.sem, v_s.one("total"))
                        dve.wait_ge(v_s.sem, v_s.at("total", h))
                        dve.tensor_tensor(prob_of(h), prob_of(h), total[h % 2].unsqueeze(2).broadcast_to([P, NC, MEM]), ALU.mult
                                          ).then_inc(v_s.sem, v_s.one("prob"))
                        dve.wait_ge(pe_s.sem, pe_s.at("turn1", h))
                        dve.tensor_copy(turned(h)[:, 1, :], banks[5]).then_inc(v_s.sem, v_s.one("p1"))
                        for d in range(2):
                            dve.wait_ge(a_s.sem, a_s.at(f"o{d}", h))
                            dve.tensor_tensor(rhs.lo[:, 2 * h + d, :], banks[6 + d], as_f32(rhs.hi[:, 2 * h + d, :]), ALU.subtract
                                              ).then_inc(v_s.sem, v_s.one(f"lo{d}"))
                    in_turn(scores, rest)

                @block.scalar
                def _(act):
                    def scores(h):
                        if h >= 2:
                            act.wait_ge(pe_s.sem, pe_s.at("turn1", h - 2))
                        act.wait_ge(sv_s.sem, sv_s.at("minus", h))
                        for c in range(NC):
                            act.activation(prob_of(h)[:, c, :], score(h, c), ACT.Exp, bias=top[h % 2][:, c:c + 1],
                                           accum_out=total[h % 2][:, c:c + 1]).then_inc(sa_s.sem, sa_s.one(f"exp{c}"))

                    def rest(h):
                        act.wait_ge(pe_s.sem, pe_s.at("turn0", h))
                        act.activation(turned(h)[:, 0, :], banks[4], ACT.Copy).then_inc(a_s.sem, a_s.one("p0"))
                        for d in range(2):
                            act.wait_ge(pe_s.sem, pe_s.at(f"o{d}", h))
                            act.activation(rhs.hi[:, 2 * h + d, :], banks[6 + d], ACT.Copy).then_inc(a_s.sem, a_s.one(f"o{d}"))
                    in_turn(scores, rest)

            add_to_residual(outer, f"xa_out{n}", dram[f"wo{n}"], rhs, dram[f"f_in{n}"])

        def swiglu(n, outer, following):
            gated = halves(outer, f"ffn{n}_a", FT)
            with ExitStack() as scope:
                rhs = halves(scope, f"ffn{n}_h", KD)
                w_in = Projection(scope, f"ffn{n}_in", dram[f"f_in{n}"], rhs, 2 * FT)
                source = NormSource(scope, f"ffn{n}", x3, rhs, f"ffn{n}", squares=x_squares)
                w_in.ready = source.ready
                silu, both = area(scope, f"ffn{n}_silu", T), area(scope, f"ffn{n}_both", T)
                a_s, v_s = steps(**{f"ffn{n}_act": ["silu", "hi"], f"ffn{n}_vec": ["^", "gated", "lo"]})
                with nc.Block() as block:
                    @block.sync
                    def _(sp):
                        w_in.sync(sp, dram[f"f_out{n}"])

                    @block.tensor
                    def _(pe):
                        source.tensor(pe)
                        w_in.tensor(pe, (FT - 1, lambda u, i: pe.wait_ge(v_s.sem, v_s.at("gated", i)) if u
                                         else pe.wait_ge(a_s.sem, a_s.at("silu", i))))

                    @block.scalar
                    def _(act):
                        w_in.first_hi(act)
                        source.scalar(act)

                        def tile(i, u):
                            if u == 0:
                                act.wait_ge(v_s.sem, v_s.passes(i))
                                act.activation(silu, banks[0], ACT.Silu).then_inc(a_s.sem, a_s.one("silu"))
                            else:
                                act.wait_ge(v_s.sem, v_s.at("gated", i))
                                act.activation(gated.hi_flat[:, bass.ds(i * T, T)], both, ACT.Copy).then_inc(a_s.sem, a_s.one("hi"))
                        w_in.scalar(act, (FT, tile))

                    @block.vector
                    def _(dve):
                        dve.sem_inc(v_s.sem, 1)
                        w_in.first_lo(dve)
                        source.vector(dve)

                        def tile(i, u):
                            if u:
                                dve.wait_ge(v_s.sem, v_s.passes(i))
                                dve.wait_ge(a_s.sem, a_s.at("silu", i))
                                dve.tensor_tensor(both, silu, banks[1], ALU.mult).then_inc(v_s.sem, v_s.one("gated"))
                                dve.wait_ge(a_s.sem, a_s.at("hi", i))
                                at = bass.ds(i * T, T)
                                dve.tensor_tensor(gated.lo_flat[:, at], both, as_f32(gated.hi_flat)[:, at],
                                                  ALU.subtract).then_inc(v_s.sem, v_s.one("lo"))
                        w_in.vector(dve, (FT, tile))

                    @block.gpsimd
                    def _(pool):
                        source.gpsimd(pool)
                w_in.end()
            with ExitStack() as scope:
                add_to_residual(scope, f"ffn{n}_out", dram[f"f_out{n}"], gated, following, k=FT // 2, cuts=2)

        Q1, FWD1, BWD1, I1, G1 = (HEADS * j for j in range(5))

        def hgrn_projection(outer):
            rhs = halves(outer, "hg_h", KD)
            pr = Projection(outer, "hg_in", dram["hg_in"], rhs, 5 * HEADS)
            source = NormSource(outer, "hg_in", x3, rhs, "mix1", squares=x_squares)
            pr.ready = source.ready
            room = area(outer, "hg_gates", 2 * T + 24)
            sig = [room[:, u * T:(u + 1) * T] for u in range(2)]
            low, rest, top = (room[:, 2 * T + 8 * j:2 * T + 8 * j + 8] for j in range(3))
            a_s, f_s, pre_v, pre_a = steps(hg_emptied=["a0", "a1"], hg_gate=["^", "f0", "f1"],
                                           hg_pre_vec=["top", "d0", "d1", "sum", "inv", "low", "rest"], hg_pre_act=["e0", "e1"])
            with nc.Block() as block:
                @block.sync
                def _(sp):
                    pr.sync(sp, None)

                @block.tensor
                def _(pe):
                    source.tensor(pe)
                    pr.tensor(pe, (pr.passes - 1, lambda u, i: pe.wait_ge(a_s.sem, a_s.at(f"a{u}", i))))

                @block.scalar
                def _(act):
                    pr.first_hi(act)
                    act.wait_ge(pre_v.sem, pre_v.at("d1"))
                    act.activation(low, low, ACT.Exp).then_inc(pre_a.sem, pre_a.one("e0"))
                    act.activation(rest, rest, ACT.Exp).then_inc(pre_a.sem, pre_a.one("e1"))
                    source.scalar(act)

                    def emptier(func):
                        def tile(i, u):
                            act.activation(proj1[:, bass.ds(i * (2 * T) + u * T, T)], banks[u], func).then_inc(a_s.sem, a_s.one(f"a{u}"))
                        return tile

                    def gate(i, u):
                        act.wait_ge(f_s.sem, f_s.passes(i - HEADS // 2))
                        act.activation(sig[u], banks[u], ACT.Sigmoid).then_inc(a_s.sem, a_s.one(f"a{u}"))

                    pr.scalar(act, (HEADS // 2, emptier(ACT.Copy)), (HEADS, gate), (HEADS // 2, emptier(ACT.Copy)),
                              (HEADS // 2, emptier(ACT.Silu)))

                @block.vector
                def _(dve):
                    l0, l1 = col("lb0", 0, 8), col("lb1", 0, 8)
                    dve.tensor_tensor(top, l0, l1, ALU.max).then_inc(pre_v.sem, pre_v.one("top"))
                    dve.wait_ge(pre_v.sem, pre_v.at("top"))
                    dve.tensor_tensor(rest, l0, top, ALU.subtract).then_inc(pre_v.sem, pre_v.one("d0"))
                    dve.tensor_tensor(low, l1, top, ALU.subtract).then_inc(pre_v.sem, pre_v.one("d1"))
                    pr.first_lo(dve)
                    dve.wait_ge(pre_a.sem, pre_a.at("e1"))
                    dve.tensor_tensor(rest, low, rest, ALU.add).then_inc(pre_v.sem, pre_v.one("sum"))
                    dve.wait_ge(pre_v.sem, pre_v.at("sum"))
                    dve.reciprocal(rest, rest).then_inc(pre_v.sem, pre_v.one("inv"))
                    dve.wait_ge(pre_v.sem, pre_v.at("inv"))
                    dve.tensor_tensor(low, low, rest, ALU.mult).then_inc(pre_v.sem, pre_v.one("low"))
                    dve.wait_ge(pre_v.sem, pre_v.at("low"))
                    dve.tensor_scalar(rest, low, -1.0, 1.0, ALU.mult, ALU.add).then_inc(pre_v.sem, pre_v.one("rest"))
                    dve.wait_ge(pre_v.sem, pre_v.at("rest"))
                    dve.sem_inc(f_s.sem, 1)
                    source.vector(dve)

                    def gate(d):
                        def tile(i, u):
                            first = (HEADS // 2) * (1 + d)
                            dve.wait_ge(a_s.sem, a_s.at(f"a{u}", i))
                            c = bass.ds(i * 2 + (u - 2 * first), 1)
                            dve.tensor_scalar(proj1[:, bass.ds(i * (2 * T) + u * T, T)], dirs[d](sig[u]), rest[:, c], low[:, c],
                                              ALU.mult, ALU.add).then_inc(f_s.sem, f_s.one(f"f{u}"))
                        return tile

                    pr.vector(dve, (HEADS // 2, None), (HEADS // 2, gate(0)), (HEADS // 2, gate(1)), (HEADS, None))

                @block.gpsimd
                def _(pool):
                    source.gpsimd(pool)
            pr.end()

        def hgrn(outer):
            nl = len(LEVELS)
            words = 15400
            work = area(outer, "hg_work", words)
            used = [0]

            def take(n):
                used[0] += n
                assert used[0] <= words
                return work[:, used[0] - n:used[0]]

            def pairs_of(n):
                return [[take(n), take(n)] for _ in range(2)]

            q_d, i_d = [take(T), take(T)], [take(T), take(T)]
            qp, ks, tot, att, tot2 = pairs_of(T), pairs_of(T), pairs_of(T), pairs_of(T), pairs_of(T // 2)
            k_tok, v_tok = [take(T), take(T)], [take(T), take(T)]
            states, o_t, sq = take(3 * P), take(T), take(T)
            root = take(4)
            m_bank = [[0, 1], [2, 3]]
            v_bank, k_bank, add_bank, o_bank, norm_bank = 4, 5, 6, [7, 4], [5, 6]
            slot_list = [("diag", 0, 0), ("diag", 0, 1)] + [("level", n, d) for n in range(nl) for d in range(2)]
            slots_of_head = range(len(slot_list))

            def tile_of(first, h):
                return proj1[:, bass.ds(h * T + first * T, T)]

            def per_level(names):
                return [f"{k}{n}_{d}" for n in range(nl) for d in range(2) for k in names]

            l_pe, l_vec, l_pool = steps(hg_L_pe=["diag_0", "diag_1"] + per_level(["m"]),
                                        hg_L_vec=["diag_0", "diag_1"] + per_level(["q", "t", "m"]),
                                        hg_L_pool=per_level(["k"]))
            p_act, p_vec, p_pool = steps(hg_P_act=["q", "tot_0", "tot_1", "ks_0", "ks_1"], hg_P_vec=["qp_0", "qp_1"],
                                         hg_P_pool=["q"])
            t_pe, t_act, t_vec, t_pool = steps(
                hg_T_pe=["^", "v_0", "k_0", "v_1", "k_1", "add_0", "o_0", "add_1", "o_1", "sum", "spread"],
                hg_T_act=["i", "v_0", "k_0", "v_1", "k_1", "o", "square", "root"],
                hg_T_vec=["^", "st0_0", "st1_0", "st2_0", "st0_1", "st1_1", "st2_1", "o", "inv", "norm", "out"],
                hg_T_pool=["i"])

            def run(engine, level, tail, prep):
                for t in slots_of_head:
                    prep(t, 0, 0)
                for t in slots_of_head:
                    level(t, 0, 0)
                    prep(t, 1, 1)
                with fori(engine, 0, HEADS // 2 - 1) as j:
                    for t in slots_of_head:
                        level(t, j * 2 + 1, 1)
                        tail(t, j * 2, 0)
                        prep(t, j * 2 + 2, 0)
                    for t in slots_of_head:
                        level(t, j * 2 + 2, 0)
                        tail(t, j * 2 + 1, 1)
                        prep(t, j * 2 + 3, 1)
                for t in slots_of_head:
                    level(t, HEADS - 1, 1)
                    tail(t, HEADS - 2, 0)
                for t in slots_of_head:
                    tail(t, HEADS - 1, 1)

            def is_first(h, count=1):
                return isinstance(h, int) and h < count

            with nc.Block() as block:
                @block.sync
                def _(sp):
                    ring.prefetch(sp, dram["hg_out"])

                @block.gpsimd
                def _(pool):
                    def level(t, h, p):
                        kind, n, d = slot_list[t]
                        if kind != "level":
                            return
                        b = LEVELS[n]
                        pairs = T // (2 * b)
                        t_in = (tot if n % 2 == 0 else tot2)[p][d][:, 0:2 * pairs].rearrange("p (n two) -> p n two", two=2)
                        k4 = ks[p][d].rearrange("p (n two b) -> p n two b", two=2, b=b)[:, :, 0, :]
                        pool.wait_ge(l_pe.sem, l_pe.at(f"m{n}_{d}", h))
                        if n:
                            pool.wait_ge(l_vec.sem, l_vec.at(f"t{n - 1}_{d}", h))
                            pool.wait_ge(l_pool.sem, l_pool.at(f"k{n - 1}_{d}", h))
                        pool.tensor_tensor(k4, k4, t_in[:, :, 1:2].broadcast_to([P, pairs, b]), ALU.mult
                                           ).then_inc(l_pool.sem, l_pool.one(f"k{n}_{d}"))

                    def tail(t, h, p):
                        if t == 1:
                            pool.wait_ge(t_act.sem, t_act.at("i", h))
                            pool.wait_ge(t_pe.sem, t_pe.passes(h))
                            hold(pool, "pool")
                            pool.tensor_copy(i_d[1], i_d[0][:, ::-1]).then_inc(t_pool.sem, t_pool.one("i"))

                    def prep(t, h, p):
                        if t == 10:
                            pool.wait_ge(p_act.sem, p_act.at("q", h))
                            if not is_first(h):
                                pool.wait_ge(l_pe.sem, l_pe.at("diag_1", h - 1))
                                pool.wait_ge(p_vec.sem, p_vec.at("qp_1", h - 1))
                            hold(pool, "pool")
                            pool.tensor_copy(q_d[1], q_d[0][:, ::-1]).then_inc(p_pool.sem, p_pool.one("q"))

                    run(pool, level, tail, prep)

                @block.scalar
                def _(act):
                    def level(t, h, p):
                        pass

                    def tail(t, h, p):
                        if t == 0:
                            act.wait_ge(t_pe.sem, t_pe.passes(h))
                            act.wait_ge(t_vec.sem, t_vec.passes(h))
                            act.activation(i_d[0], tile_of(I1, h), ACT.Copy).then_inc(t_act.sem, t_act.one("i"))
                        copies = {2: ("v", 0), 3: ("k", 0), 4: ("v", 1), 5: ("k", 1)}
                        if t in copies:
                            m, d = copies[t]
                            act.wait_ge(t_pe.sem, t_pe.at(f"{m}_{d}", h))
                            act.activation((v_tok if m == "v" else k_tok)[d], banks[v_bank if m == "v" else k_bank], ACT.Copy
                                           ).then_inc(t_act.sem, t_act.one(f"{m}_{d}"))
                        if t == 8:
                            act.wait_ge(t_pe.sem, t_pe.at("o_0", h))
                            act.activation(o_t, banks[o_bank[0]], ACT.Copy).then_inc(t_act.sem, t_act.one("o"))
                        if t == 11:
                            act.wait_ge(t_vec.sem, t_vec.at("o", h))
                            act.activation(sq, o_t, ACT.Square).then_inc(t_act.sem, t_act.one("square"))
                        if t == 12:
                            act.wait_ge(t_pe.sem, t_pe.at("sum", h))
                            act.activation(root, banks[norm_bank[0]][:, 0:NC], ACT.Sqrt, bias=col("eps"), scale=1.0 / P
                                           ).then_inc(t_act.sem, t_act.one("root"))

                    def prep(t, h, p):
                        if t == 9:
                            if not is_first(h):
                                act.wait_ge(l_pe.sem, l_pe.at("diag_1", h - 1))
                                act.wait_ge(p_vec.sem, p_vec.at("qp_1", h - 1))
                                act.wait_ge(p_pool.sem, p_pool.at("q", h - 1))
                            act.activation(q_d[0], tile_of(Q1, h), ACT.Copy).then_inc(p_act.sem, p_act.one("q"))
                        if t in (9, 10):
                            d = t - 9
                            if not is_first(h, 2) and d == 0:
                                act.wait_ge(t_vec.sem, t_vec.at("st2_1", h - 2))
                                act.wait_ge(t_pe.sem, t_pe.at("k_1", h - 2))
                            act.activation(tot[p][d], tile_of((FWD1, BWD1)[d], h), ACT.Copy).then_inc(p_act.sem, p_act.one(f"tot_{d}"))
                        if t == 11:
                            for d in range(2):
                                act.wait_ge(p_act.sem, p_act.at(f"tot_{d}", h))
                                act.activation(ks[p][d], tot[p][d], ACT.Identity, scale=-1.0, bias=col("one")).then_inc(p_act.sem, p_act.one(f"ks_{d}"))

                    run(act, level, tail, prep)

                @block.tensor
                def _(pe):
                    pe.sem_inc(t_pe.sem, 1)

                    def level(t, h, p):
                        kind, n, d = slot_list[t]
                        if kind == "diag":
                            pe.wait_ge(p_act.sem, p_act.at(f"ks_{d}", h))
                            if d:
                                pe.wait_ge(p_pool.sem, p_pool.at("q", h))
                            if not is_first(h):
                                pe.wait_ge(l_vec.sem, l_vec.at(f"m{nl - 2}_{d}", h - 1))
                            for c in range(NC):
                                ins = pe.matmul(chunk(banks[d], c), chunk(ks[p][d], c), chunk(q_d[d], c), start=True, stop=True)
                            ins.then_inc(l_pe.sem, l_pe.one(f"diag_{d}"))
                        else:
                            if n == 0:
                                pe.wait_ge(p_vec.sem, p_vec.at(f"qp_{d}", h))
                                if not is_first(h):
                                    pe.wait_ge(l_vec.sem, l_vec.at(f"m{nl - 1}_{d}", h - 1))
                            else:
                                pe.wait_ge(l_vec.sem, l_vec.at(f"q{n - 1}_{d}", h))
                                pe.wait_ge(l_pool.sem, l_pool.at(f"k{n - 1}_{d}", h))
                                pe.wait_ge(l_vec.sem, l_vec.at(f"m{n - 2}_{d}" if n > 1 else f"diag_{d}", h))
                            for c in range(NC):
                                ins = pe.matmul(chunk(banks[m_bank[n % 2 == 0][d]], c), chunk(ks[p][d], c), chunk(qp[p][d], c),
                                                start=True, stop=True)
                            ins.then_inc(l_pe.sem, l_pe.one(f"m{n}_{d}"))

                    def tail(t, h, p):
                        turns = {1: ("v", 0), 2: ("k", 0), 3: ("v", 1), 4: ("k", 1)}
                        if t in turns:
                            m, d = turns[t]
                            src, bank = (i_d[d], v_bank) if m == "v" else (ks[p][d], k_bank)
                            if m == "v" and d == 0:
                                pe.wait_ge(t_act.sem, t_act.at("i", h))
                                pe.wait_ge(t_vec.sem, t_vec.passes(h))
                            elif m == "k" and d == 0:
                                pe.wait_ge(l_pool.sem, l_pool.at(f"k{nl - 1}_1", h))
                            elif m == "v":
                                pe.wait_ge(t_pool.sem, t_pool.at("i", h))
                                pe.wait_ge(t_act.sem, t_act.at("v_0", h))
                            else:
                                pe.wait_ge(t_act.sem, t_act.at("k_0", h))
                            for c in range(NC):
                                ins = pe.transpose(chunk(banks[bank], c), chunk(src, c), ident)
                            ins.then_inc(t_pe.sem, t_pe.one(f"{m}_{d}"))
                        for d, at in ((0, 5), (1, 8)):
                            if t == at:
                                pe.wait_ge(t_act.sem, t_act.at(f"k_{d}", h))
                                if d:
                                    pe.wait_ge(t_vec.sem, t_vec.at("st2_0", h))
                                for c in range(NC - 1):
                                    ins = pe.matmul(chunk(banks[add_bank], c), chunk(k_tok[d], c), chunk(v_tok[d], c), start=True, stop=True)
                                ins.then_inc(t_pe.sem, t_pe.one(f"add_{d}"))
                        for d, at in ((0, 7), (1, 10)):
                            if t == at:
                                pe.wait_ge(t_vec.sem, t_vec.at(f"st2_{d}", h))
                                if d == 0:
                                    pe.wait_ge(l_vec.sem, l_vec.at(f"m{nl - 1}_1", h))
                                for c in range(NC):
                                    out = chunk(banks[o_bank[d]], c)
                                    ins = pe.matmul(out, chunk(v_tok[d], c), chunk(att[p][d], c), start=True, stop=c == 0)
                                    if c:
                                        ins = pe.matmul(out, chunk(states, c - 1), chunk(qp[p][d], c), start=False, stop=True)
                                ins.then_inc(t_pe.sem, t_pe.one(f"o_{d}"))
                        if t == 12:
                            pe.wait_ge(t_act.sem, t_act.at("square", h))
                            for c in range(NC):
                                ins = pe.matmul(banks[norm_bank[0]][:, c:c + 1], chunk(sq, c), ones[:, 0:1], start=True, stop=True)
                            ins.then_inc(t_pe.sem, t_pe.one("sum"))
                        if t == 14:
                            pe.wait_ge(t_vec.sem, t_vec.at("inv", h))
                            for c in range(NC):
                                ins = pe.matmul(chunk(banks[norm_bank[1]], c), root[:, c:c + 1].broadcast_to([P, P]), ident,
                                                start=True, stop=True)
                            ins.then_inc(t_pe.sem, t_pe.one("spread"))

                    def prep(t, h, p):
                        pass

                    run(pe, level, tail, prep)

                @block.vector
                def _(dve):
                    dve.sem_inc(t_vec.sem, 1)

                    def level(t, h, p):
                        kind, n, d = slot_list[t]
                        if kind == "diag":
                            dve.wait_ge(l_pe.sem, l_pe.at(f"diag_{d}", h))
                            dve.tensor_tensor(by_chunk(att[p][d]), by_chunk(banks[d]), over_chunks(ident), ALU.mult
                                              ).then_inc(l_vec.sem, l_vec.one(f"diag_{d}"))
                            return
                        b = LEVELS[n]
                        pairs = T // (2 * b)
                        t_in, t_out = (tot, tot2) if n % 2 == 0 else (tot2, tot)
                        t_in = t_in[p][d][:, 0:2 * pairs].rearrange("p (n two) -> p n two", two=2)
                        q4 = qp[p][d].rearrange("p (n two b) -> p n two b", two=2, b=b)[:, :, 1, :]
                        dve.wait_ge(l_pe.sem, l_pe.at(f"m{n}_{d}", h))
                        if n:
                            dve.wait_ge(l_vec.sem, l_vec.at(f"t{n - 1}_{d}", h))
                        dve.tensor_tensor(q4, q4, t_in[:, :, 0:1].broadcast_to([P, pairs, b]), ALU.mult).then_inc(l_vec.sem, l_vec.one(f"q{n}_{d}"))
                        if n:
                            dve.wait_ge(l_pool.sem, l_pool.at(f"k{n - 1}_{d}", h))
                        dve.tensor_tensor(t_out[p][d][:, 0:pairs], t_in[:, :, 0], t_in[:, :, 1], ALU.mult).then_inc(l_vec.sem, l_vec.one(f"t{n}_{d}"))
                        dve.wait_ge(l_vec.sem, l_vec.at(f"m{n - 1}_{d}" if n else f"diag_{d}", h))
                        hold(dve, "vec")
                        dve.copy_predicated(by_chunk(att[p][d]), over_chunks(table("up", P, n * P).bitcast(U32)),
                                            by_chunk(banks[m_bank[n % 2 == 0][d]])).then_inc(l_vec.sem, l_vec.one(f"m{n}_{d}"))

                    def tail(t, h, p):
                        for d, at in ((0, 6), (1, 9)):
                            if t == at:
                                whole = (tot2 if nl % 2 else tot)[p][d]
                                dve.wait_ge(l_vec.sem, l_vec.at(f"m{nl - 1}_1", h))
                                dve.wait_ge(t_pe.sem, t_pe.at(f"add_{d}", h))
                                dve.tensor_copy(chunk(states, 0), chunk(banks[add_bank], 0)).then_inc(t_vec.sem, t_vec.one(f"st0_{d}"))
                                for c in (1, 2):
                                    dve.wait_ge(t_vec.sem, t_vec.at(f"st{c - 1}_{d}", h))
                                    dve.scalar_tensor_tensor(chunk(states, c), chunk(states, c - 1), whole[:, c:c + 1],
                                                             chunk(banks[add_bank], c), ALU.mult, ALU.add).then_inc(t_vec.sem, t_vec.one(f"st{c}_{d}"))
                        if t == 11:
                            dve.wait_ge(t_act.sem, t_act.at("o", h))
                            dve.wait_ge(t_pe.sem, t_pe.at("o_1", h))
                            dve.tensor_tensor(o_t, banks[o_bank[1]][:, ::-1], o_t, ALU.add).then_inc(t_vec.sem, t_vec.one("o"))
                        if t == 13:
                            dve.wait_ge(t_act.sem, t_act.at("root", h))
                            dve.reciprocal(root, root).then_inc(t_vec.sem, t_vec.one("inv"))
                        if t == 15:
                            dve.wait_ge(t_pe.sem, t_pe.at("spread", h))
                            dve.scalar_tensor_tensor(o_t, o_t, cols[:, bass.ds(h + COL["hgw"], 1)], banks[norm_bank[1]],
                                                     ALU.mult, ALU.mult).then_inc(t_vec.sem, t_vec.one("norm"))
                            dve.wait_ge(t_vec.sem, t_vec.at("norm", h))
                            dve.tensor_tensor(hT1[:, bass.ds(h * T, T)], o_t, tile_of(G1, h), ALU.mult).then_inc(t_vec.sem, t_vec.one("out"))

                    def prep(t, h, p):
                        if t in (12, 13):
                            d = t - 12
                            if not is_first(h, 2):
                                dve.wait_ge(t_pe.sem, t_pe.at("o_1", h - 2))
                            if d:
                                dve.wait_ge(p_pool.sem, p_pool.at("q", h))
                            dve.wait_ge(p_act.sem, p_act.at(f"tot_{d}", h))
                            dve.tensor_tensor(qp[p][d], q_d[d], tot[p][d], ALU.mult).then_inc(p_vec.sem, p_vec.one(f"qp_{d}"))

                    run(dve, level, tail, prep)

        def final_norm(outer):
            name, src, width, gain = "norm_final", x3, T, "final"
            dst = area(outer, "normed", KD * T).rearrange("p (n t) -> p n t", t=T)
            root, inv = area(outer, "final_root", T), area(outer, "final_inverse", T)
            with ExitStack() as scope:
                act_s, pe_s, v_s = steps(**{
                    name + "_act": ["root"], name + "_pe": ["sum"],
                    name + "_vec": ["inverse"] + [f"out{k}" for k in range(KD)]})
                with nc.Block() as block:
                    @block.sync
                    def _(sp):
                        for k in range(KD):
                            sp.wait_ge(v_s.sem, v_s.at(f"out{k}"))
                            sp.dma_start(out_d[:, k, :], dst[:, k, :]).then_inc(stored, 16)
                        sp.wait_ge(stored, 16 * KD)

                    @block.scalar
                    def _(act):
                        act.wait_ge(pe_s.sem, pe_s.at("sum"))
                        act.activation(root, banks[0][:, 0:width], ACT.Sqrt, bias=col("eps"),
                                                  scale=1.0 / D).then_inc(act_s.sem, act_s.one("root"))

                    @block.tensor
                    def _(pe):
                        pe.matmul(banks[0][:, 0:width], ones, x_squares, start=True, stop=True).then_inc(pe_s.sem, pe_s.one("sum"))

                    @block.vector
                    def _(dve):
                        dve.wait_ge(act_s.sem, act_s.at("root"))
                        dve.reciprocal(inv, root).then_inc(v_s.sem, v_s.one("inverse"))
                        dve.wait_ge(v_s.sem, v_s.at("inverse"))
                        for k in range(KD):
                            dve.scalar_tensor_tensor(dst[:, k, :], src[:, k, :], col(gain, k), inv,
                                                              ALU.mult, ALU.mult).then_inc(v_s.sem, v_s.one(f"out{k}"))


        with ExitStack() as inner:
            cross_attention(0, inner)
        clear_semaphores()
        with ExitStack() as inner:
            swiglu(0, inner, dram["hg_in"])
        with ExitStack() as mixer1:
            proj1 = area(mixer1, "proj1", 5 * HEADS * T)
            with ExitStack() as inner:
                hgrn_projection(inner)
            hT1 = area(mixer1, "hT1", KD * T)
            with ExitStack() as inner:
                hgrn(inner)
            clear_semaphores()
            rhs = halves(mixer1, "mix1_h", KD)
            add_to_residual(mixer1, "mix1_out", dram["hg_out"], rhs, dram["wk1"],
                            SplitSource(mixer1, "mix1", hT1.rearrange("p (n t) -> p n t", t=T), rhs))
        with ExitStack() as inner:
            cross_attention(1, inner)
        clear_semaphores()
        with ExitStack() as inner:
            swiglu(1, inner, None)
        with ExitStack() as inner:
            final_norm(inner)


def tiles(w, width=P, cuts=1):
    k, n = w.shape
    w = w.reshape(cuts, k // P // cuts, P, n // width, width).transpose(3, 0, 2, 1, 4)
    return np.ascontiguousarray(w.reshape(n // width * cuts, P, -1))


def channels(v):
    return v.reshape(-1, P).T


def kernel(**inputs):
    import concourse.bacc as bacc
    from concourse.bass_utils import run_bass_kernel_spmd as run

    a = {k: np.asarray(v) for k, v in inputs.items()}
    f = np.float32
    ab = a["ab_w_in"][0]
    z0 = RW_TILES * P
    order = np.concatenate([ab[:, :z0], ab[:, z0 + 512:z0 + 1536], ab[:, z0:z0 + 512], ab[:, z0 + 1536:],
                            np.zeros((D, P - HEADS), f)], axis=1)
    zero = np.zeros((64, 512), f)
    lora = np.concatenate([
        np.concatenate([a["rw_w2"][0, 0], zero]).reshape(P, 512), np.concatenate([a["rw_w2"][0, 1], zero]),
        np.concatenate([zero, a["rw_a2"][0]]), a["rw_g2"][0]], axis=1)

    tri = np.arange(P)
    up, low = tri[:, None] < tri[None, :], tri[:, None] > tri[None, :]
    eye = np.eye(P, dtype=f)
    head = (tri[:, None] // HD == tri[None, :] // HD).astype(f)
    levels = [((tri[:, None] // b) % 2 == 0) & (tri[None, :] // b == tri[:, None] // b + 1) for b in LEVELS]
    reset = np.ones((P, T), f)
    reset[:, ::P] = 0.0
    tab = np.concatenate([eye, np.ones((P, P), f), head, up.astype(f), (up | (eye > 0)).astype(f), reset] + [m.astype(f) for m in levels]
                         + [m.T.astype(f) for m in levels], axis=1)

    cols = np.zeros((P, NCOLS), f)

    def put(name, block):
        cols[0:block.shape[0], COL[name]:COL[name] + block.shape[1]] = block

    put("one", np.ones((P, 1), f))
    put("eps", np.full((P, 1), 1e-6, f))
    put("gneps", np.full((P, 1), 64e-5, f))
    for n in range(2):
        put(f"mix{n}", channels(a["mix_norm"][n]))
        put(f"xa{n}", channels(a["xa_norm"][n]))
        put(f"mem{n}", channels(a["mem_norm"][n]))
        put(f"ffn{n}", channels(a["ffn_norm"][n]))
        put(f"lb{n}", channels(a["hg_lb"][n]))
    put("final", channels(a["final_norm"]))
    put("mu", channels(a["rw_mu"][0]))
    taps = [channels(v) for v in (*a["ssd_conv_w"][0], a["ssd_conv_b"][0])]
    put("taps", np.stack(taps, axis=2).reshape(P, 32))
    vecs = [a["rw_w0"][0, 0], a["rw_w0"][0, 1], a["rw_a0"][0], a["rw_k_k"][0], a["rw_k_a"][0],
            a["rw_r_k"][0].reshape(-1), a["rw_gn_w"][0], a["rw_gn_b"][0]]
    put("rw", np.stack([channels(v) for v in vecs], axis=2).reshape(P, -1))
    put("ssd_d", channels(np.repeat(a["ssd_d"][0], HD)))
    put("ssd_w", channels(a["ssd_norm_w"][0]))
    put("hgw", channels(a["hg_norm_w"][0]))
    put("dtb", a["ssd_dt_bias"][0].T)
    put("alog", a["ssd_a_log"][0].T)

    arrays = {
        "xT": np.ascontiguousarray(a["x"][0].T.reshape(KD, P, T).transpose(1, 0, 2).reshape(P, -1)),
        "memT": np.ascontiguousarray(a["mem"][0].T.reshape(KD, P, MEM).transpose(1, 0, 2).reshape(P, -1)),
        "tab": tab, "cols": cols, "lora": np.ascontiguousarray(lora),
        "ab_in": tiles(order), "ab_out": tiles(a["ab_w_out"][0]),
        "hg_in": tiles(a["hg_w_in"][0]), "hg_out": tiles(a["hg_w_out"][0]),
    }
    for n in range(2):
        arrays[f"wq{n}"] = tiles(a["xa_wq"][n])
        arrays[f"wk{n}"] = tiles(a["xa_wkv"][n][:, :D])
        arrays[f"wv{n}"] = tiles(a["xa_wkv"][n][:, D:], 256, 2)
        arrays[f"wo{n}"] = tiles(a["xa_wo"][n])
        w = a["ffn_w_in"][n]
        arrays[f"f_in{n}"] = tiles(np.ascontiguousarray(w.reshape(D, 2, FT, P).transpose(0, 2, 1, 3)).reshape(D, 2 * FFN))
        arrays[f"f_out{n}"] = tiles(a["ffn_w_out"][n], cuts=2)

    nc = bacc.Bacc("TRN2", target_bir_lowering=False, num_devices=1)
    dram = {k: nc.dram_tensor("in_" + k, v.shape, F32, kind="ExternalInput").ap() for k, v in arrays.items()}
    out_d = nc.dram_tensor("out_yT", (P, KD, T), F32, kind="ExternalOutput").ap()
    scratch_d = nc.dram_tensor("scratch_cum", (2 * 8 * T,), F32, kind="Internal").ap()
    build_program(nc, dram, out_d, scratch_d)
    r = run(nc, [{"in_" + k: v for k, v in arrays.items()}], core_ids=[0])
    y = r.results[0]["out_yT"]
    return np.ascontiguousarray(y.transpose(1, 0, 2).reshape(D, T).T.reshape(1, T, D))
```

```python
from contextlib import ExitStack

import numpy as np
import concourse.bass as bass
from concourse import mybir

F32 = mybir.dt.float32
F32R = mybir.dt.float32r
U32 = mybir.dt.uint32
ALU = mybir.AluOpType
ACT = mybir.ActivationFunctionType
AXX = mybir.AxisListType.X

P = 128
D, T, MEM = 1024, 512, 256
KD = D // P
NC = T // P
HD = 64
RW_TILES = 14
XBC_TILES = 8
Z_TILES = 4
XS0, B0, C0, Z0, REV0 = 14, 18, 20, 22, 26
HEADS = 8
FFN = 2816
FT = FFN // P
PART = FT // 2 * P
DECAY_SCALE = float(np.exp(-0.5))
RW_WORDS = 14700
LEVELS = [1, 2, 4, 8, 16, 32, 64]
RW_VECS = ["w0f", "w0b", "a0", "kk", "ka", "rk", "gnw", "gnb"]


def column_layout():
    at, n = {}, 0
    for name, width in [("one", 1), ("eps", 1), ("gneps", 1), ("mix0", 8), ("mix1", 8), ("xa0", 8), ("xa1", 8),
                        ("mem0", 8), ("mem1", 8), ("ffn0", 8), ("ffn1", 8), ("final", 8), ("mu", 14),
                        ("taps", 32), ("rw", 4 * len(RW_VECS)), ("ssd_d", 4), ("ssd_w", 4), ("hgw", 8),
                        ("lb0", 8), ("lb1", 8), ("dtb", 2), ("alog", 2)]:
        at[name] = n
        n += width
    return at, n


COL, NCOLS = column_layout()
TAB = dict(ident=0, ones=128, blk=256, strict=384, incl=512, reset=640, up=1152, low=1152 + 7 * P)
NTAB = 1152 + 14 * P


class Steps:

    def __init__(self, sem, names):
        self.opened = names[0] == "^"
        self.sem, self.names, self.next = sem, list(names[self.opened:]), 0
        self.value = {n: j + 1 for j, n in enumerate(self.names)}
        assert len(self.value) == len(self.names), "step names repeat"

    def one(self, name):
        assert self.names[self.next % len(self.names)] == name, (self.names[self.next % len(self.names)], name)
        self.next += 1
        return 1

    def at(self, name, i=0):
        return i * len(self.names) + (self.value[name] + self.opened)

    def passes(self, i):
        assert self.opened
        return i * len(self.names) + 1


class Ring:

    def __init__(self, slots, sems):
        self.slots, self.sems, self.base = slots, sems, [0, 0]

    def load(self, sp, w, j, u):
        sp.dma_start(self.slots[u][:, 0:w.shape[2]], w[bass.ds(j, 1), :, :].rearrange("a p n -> (a p) n")
                     ).then_inc(self.sems[u], 16)

    def prefetch(self, sp, w):
        for u in range(2):
            self.load(sp, w, u, u)

    def at(self, u, n):
        return n * 16 + (self.base[u] + 16)

    def used(self, u, n):
        self.base[u] += 16 * n


class Halves:

    def __init__(self, hi, lo, n):
        self.hi_flat, self.lo_flat = hi, lo
        self.hi, self.lo = (t.rearrange("p (n t) -> p n t", t=n) for t in (hi, lo))


def fori(engine, n0, n1):
    return engine.Fori(n0, n1)


def build_program(nc, dram, out_d, scratch_d):
    ctx = ExitStack()
    with ctx:
        def sb(name, words):
            return ctx.enter_context(nc.sbuf_tensor(name, [P, words], F32))[:, :]

        banks = [ctx.enter_context(nc.psum_tensor(f"bank{i}", [P, 512], F32))[:, :] for i in range(8)]
        xT = sb("xT", KD * T)
        slots = [sb(f"wslot{u}", PART) for u in range(2)]
        tab = sb("tab", NTAB)
        cols = sb("cols", NCOLS)
        memT = sb("memT", KD * MEM)
        x_squares = sb("x_squares", T)
        mem_inv = sb("mem_inv", MEM)
        loads = ctx.enter_context(nc.semaphore("first_loads"))
        loads2 = ctx.enter_context(nc.semaphore("table_loads"))
        loads3 = ctx.enter_context(nc.semaphore("column_loads"))
        loads4 = ctx.enter_context(nc.semaphore("memory_loads"))
        loads6 = ctx.enter_context(nc.semaphore("first_table_loads"))
        loads5 = ctx.enter_context(nc.semaphore("low_rank_loads"))
        stored = ctx.enter_context(nc.semaphore("stored"))
        ring = Ring(slots, [ctx.enter_context(nc.semaphore(f"weights{u}_loaded")) for u in range(2)])

        x3 = xT.rearrange("p (n t) -> p n t", t=T)
        mem3 = memT.rearrange("p (n m) -> p n m", m=MEM)

        def table(name, width=P, at=0):
            return tab[:, TAB[name] + at:TAB[name] + at + width]

        ident, ones, blk = table("ident"), table("ones"), table("blk")

        def col(name, j=0, n=1):
            return cols[:, COL[name] + j:COL[name] + j + n]

        def chunk(ap, c):
            return ap[:, c * P:(c + 1) * P]

        def over_chunks(ap):
            return ap.unsqueeze(1).broadcast_to([P, NC, P])

        def by_chunk(ap):
            return ap.rearrange("p (c t) -> p c t", t=P)

        def block_mask(name, n, which):
            return (table(name, P, n * P).bitcast(U32).rearrange("p (n two b) -> p n two b", two=2, b=LEVELS[n])[:, :, which, :]
                    .unsqueeze(1).broadcast_to([P, NC, P // (2 * LEVELS[n]), LEVELS[n]]))

        def blocks_of_chunks(ap, b, which):
            return ap.rearrange("p (c n two b) -> p c n two b", c=NC, two=2, b=b)[:, :, :, which, :]

        def blocks(ap, b, which):
            return ap.rearrange("p (n two b) -> p n two b", two=2, b=b)[:, :, which, :]

        dirs = (lambda ap: ap, lambda ap: ap[:, ::-1])

        held = {n: ctx.enter_context(nc.semaphore(f"held_{n}")) for n in ("vec", "pool")}

        def hold(engine, name):
            engine.sem_inc(held[name], 1)

        taken = []

        def clear_semaphores():
            with nc.Block() as block:
                @block.gpsimd
                def _(pool):
                    for s in taken:
                        pool.sem_clear(s)
            for s in taken:
                nc.release_semaphore(s)
            taken.clear()

        def steps(**named):
            sems = {n: nc.alloc_semaphore(name=n) for n in named}
            taken.extend(sems.values())
            return [Steps(sems[n], v) for n, v in named.items()]

        def area(scope, name, words):
            return scope.enter_context(nc.sbuf_tensor(name, [P, words], F32))[:, :]

        def halves(scope, name, tiles, n=T):
            return Halves(*(scope.enter_context(nc.sbuf_tensor(f"{name}_{part}", [P, tiles * n], F32R))[:, :]
                            for part in ("hi", "lo")), n)

        def as_f32(ap):
            return ap.bitcast(F32)

        class Projection:

            def __init__(self, scope, name, w, rhs, tiles, k=KD, n=T, cuts=1, token_major=False, extra=0):
                self.name, self.w, self.rhs, self.k, self.n, self.cuts, self.tm = name, w, rhs, k, n, cuts, token_major
                self.passes, self.parts, self.extra = tiles // 2, 2 * cuts, extra
                words = w.shape[2]
                self.words = words
                self.wt = [halves(scope, f"{name}_w{u}", 1, words) for u in range(2)]
                each = range(self.parts)
                self.pe_s, self.hi_s, self.lo_s = steps(**{
                    name + "_tile": [f"tile{p}" for p in each], name + "_hi": [f"hi{p}" for p in each],
                    name + "_lo": [f"lo{p}" for p in each]})
                self.ready = None

            def load(self, sp, i, p):
                ring.load(sp, self.w, i * self.parts + p, p % 2)

            def sync(self, sp, following):
                def one(i, last):
                    for p in range(self.parts):
                        sp.wait_ge(self.lo_s.sem, self.lo_s.at(f"lo{p}", i))
                        if p + 2 < self.parts:
                            self.load(sp, i, p + 2)
                        elif not last:
                            self.load(sp, i + 1, p + 2 - self.parts)
                        elif p % 2 < self.extra:
                            ring.load(sp, self.w, self.passes * self.parts + p % 2, p % 2)
                        elif following is not None:
                            ring.load(sp, following, p % 2, p % 2)
                with fori(sp, 0, self.passes - 1) as i:
                    one(i, False)
                one(self.passes - 1, True)

            def split_hi(self, act, i, p):
                u = p % 2
                act.wait_ge(ring.sems[u], ring.at(u, i * self.cuts + p // 2))
                act.activation(self.wt[u].hi_flat, slots[u][:, 0:self.words], ACT.Copy).then_inc(
                    self.hi_s.sem, self.hi_s.one(f"hi{p}"))

            def split_lo(self, dve, i, p):
                u = p % 2
                dve.wait_ge(self.hi_s.sem, self.hi_s.at(f"hi{p}", i))
                dve.tensor_tensor(self.wt[u].lo_flat, slots[u][:, 0:self.words], as_f32(self.wt[u].hi_flat),
                                  ALU.subtract).then_inc(self.lo_s.sem, self.lo_s.one(f"lo{p}"))

            def in_turns(self, engine, split, segments):
                def one(i, last, function):
                    for p in range(self.parts):
                        within = p + 2 < self.parts
                        if within or not last:
                            engine.wait_ge(self.pe_s.sem, self.pe_s.at(f"tile{p}", i))
                            if within:
                                split(engine, i, p + 2)
                            else:
                                split(engine, i + 1, p + 2 - self.parts)
                        if function and p % self.cuts == self.cuts - 1:
                            engine.wait_ge(self.pe_s.sem, self.pe_s.at(f"tile{p}", i))
                            function(i, p // self.cuts)
                done = 0
                for count, function in segments:
                    end = done + count
                    stop = min(end, self.passes - 1)
                    if stop > done:
                        with fori(engine, done, stop) as i:
                            one(i, False, function)
                    if end == self.passes:
                        one(end - 1, True, function)
                    done = end
                assert done == self.passes

            def first_hi(self, act, source=None):
                self.split_hi(act, 0, 0)
                if source:
                    source.scalar(act, lambda: self.split_hi(act, 0, 1))
                else:
                    self.split_hi(act, 0, 1)

            def first_lo(self, dve, source=None):
                self.split_lo(dve, 0, 0)
                if source:
                    source.vector(dve, lambda: self.split_lo(dve, 0, 1))
                else:
                    self.split_lo(dve, 0, 1)

            def scalar(self, act, *segments):
                self.in_turns(act, self.split_hi, segments or [(self.passes, None)])

            def vector(self, dve, *segments):
                self.in_turns(dve, self.split_lo, segments or [(self.passes, None)])

            def products(self, pe, p, bank, ready=None):
                w, r, k0 = self.wt[p % 2], self.rhs, p % self.cuts * self.k
                first, last = p % self.cuts == 0, p % self.cuts == self.cuts - 1
                for k in range(self.k):
                    if ready:
                        ready(pe, k)
                    for n, (wp, rp) in enumerate(((w.hi_flat, r.hi), (w.lo_flat, r.hi), (w.hi_flat, r.lo))):
                        start, stop = first and k == 0 and n == 0, last and k == self.k - 1 and n == 2
                        if self.tm:
                            for m in range(MEM // P):
                                ins = pe.matmul(banks[2 * bank + m][:, 0:256], rp[:, k0 + k, m * P:(m + 1) * P],
                                                wp[:, k * 256:(k + 1) * 256], start=start, stop=stop)
                        else:
                            ins = pe.matmul(banks[bank][:, 0:self.n], wp[:, k * P:(k + 1) * P], rp[:, k0 + k, :],
                                            start=start, stop=stop)
                return ins

            def tensor(self, pe, *segments):
                def one(i, emptied):
                    for p in range(self.parts):
                        pe.wait_ge(self.lo_s.sem, self.lo_s.at(f"lo{p}", i))
                        if emptied and p % self.cuts == 0:
                            emptied(p // self.cuts, i - 1)
                        ready = self.ready if emptied is None and p == 0 else None
                        self.products(pe, p, p // self.cuts, ready).then_inc(self.pe_s.sem, self.pe_s.one(f"tile{p}"))
                one(0, None)
                done = 1
                for count, emptied in segments:
                    with fori(pe, done, done + count) as i:
                        one(i, emptied)
                    done += count
                assert done == self.passes, (self.name, done)

            def end(self):
                for u in range(2):
                    ring.used(u, self.passes * self.cuts + (u < self.extra))

        class SplitSource:

            def __init__(self, scope, name, src, rhs):
                self.src, self.rhs = src, rhs
                self.a_s, self.v_s = steps(**{name + "_src_hi": [f"hi{k}" for k in range(KD)],
                                                     name + "_src_lo": [f"lo{k}" for k in range(KD)]})

            def scalar(self, act, between):
                for k in range(KD):
                    if k == 4:
                        between()
                    act.activation(self.rhs.hi[:, k, :], self.src[:, k, :], ACT.Copy).then_inc(
                        self.a_s.sem, self.a_s.one(f"hi{k}"))

            def vector(self, dve, between):
                for k in range(KD):
                    if k == 4:
                        between()
                    dve.wait_ge(self.a_s.sem, self.a_s.at(f"hi{k}"))
                    dve.tensor_tensor(self.rhs.lo[:, k, :], self.src[:, k, :], as_f32(self.rhs.hi[:, k, :]),
                                      ALU.subtract).then_inc(self.v_s.sem, self.v_s.one(f"lo{k}"))

            def tensor(self, pe):
                pass

            def gpsimd(self, pool):
                pass

            def ready(self, pe, k):
                pe.wait_ge(self.v_s.sem, self.v_s.at(f"lo{k}"))

        class NormSource:

            def __init__(self, scope, name, src, rhs, gain, width=T, room=None, squares=None, keep=None, kept=None):
                self.squares, self.kept = squares, kept
                self.src, self.rhs, self.gain, self.width = src, rhs, gain, width
                room = area(scope, name + "_norm", 5 * width) if room is None else room
                self.tmp = [room[:, j * width:(j + 1) * width] for j in range(4)]
                self.inv = keep if keep is not None else kept if kept is not None else room[:, 4 * width:5 * width]
                ks = range(KD)
                self.own_lo = (0, 2, 4, 6)
                self.factor = self.inv if squares is None else banks[6][:, 0:width]
                self.few = self.inv if squares is None else self.inv[:, 0:NC]
                squared = [] if squares is not None or kept is not None else list(ks)
                vec = [f"square{k}" for k in squared if k % 2] + ([] if kept is not None else ["inverse"])
                for k in ks:
                    vec += [f"out{k}"] + ([f"lo{k - 1}"] if k - 1 in self.own_lo else [])
                self.a_s, self.v_s, self.pe_s, self.g_s = steps(**{
                    name + "_norm_act": [f"square{k}" for k in squared if k % 2 == 0]
                    + ([] if kept is not None else ["root"]) + [f"hi{k}" for k in ks],
                    name + "_norm_vec": vec, name + "_norm_pe": [f"sum{k}" for k in squared or [KD - 1]]
                    + ([] if squares is None else ["spread"]),
                    name + "_norm_pool": [f"lo{k}" for k in ks if k not in self.own_lo]})
                self.squared = squared

            def scalar(self, act, between):
                a_s, pe_s, v_s = self.a_s, self.pe_s, self.v_s
                for k in self.squared[::2]:
                    if k >= 4:
                        act.wait_ge(pe_s.sem, pe_s.at(f"sum{k - 4}"))
                    act.activation(self.tmp[k % 4], self.src[:, k, :], ACT.Square).then_inc(a_s.sem, a_s.one(f"square{k}"))
                if self.kept is None:
                    act.wait_ge(pe_s.sem, pe_s.at(f"sum{KD - 1}"))
                    act.activation(self.few, banks[7][:, 0:self.few.shape[1]], ACT.Sqrt, bias=col("eps"),
                                   scale=1.0 / D).then_inc(a_s.sem, a_s.one("root"))
                between()
                for k in range(KD):
                    act.wait_ge(v_s.sem, v_s.at(f"out{k}"))
                    act.activation(self.rhs.hi[:, k, :], self.tmp[k % 4], ACT.Copy).then_inc(a_s.sem, a_s.one(f"hi{k}"))

            def tensor(self, pe):
                a_s, pe_s, v_s = self.a_s, self.pe_s, self.v_s
                if self.squares is not None:
                    for c in range(NC):
                        ins = pe.matmul(banks[7][:, c:c + 1], chunk(self.squares, c), ones[:, 0:1], start=c == 0, stop=c == NC - 1)
                    ins.then_inc(pe_s.sem, pe_s.one(f"sum{KD - 1}"))
                    pe.wait_ge(v_s.sem, v_s.at("inverse"))
                    for c in range(NC):
                        ins = pe.matmul(chunk(banks[6], c), self.inv[:, c:c + 1].broadcast_to([P, P]), ident, start=True, stop=True)
                    ins.then_inc(pe_s.sem, pe_s.one("spread"))
                for k in self.squared:
                    if k % 2:
                        pe.wait_ge(v_s.sem, v_s.at(f"square{k}"))
                    else:
                        pe.wait_ge(a_s.sem, a_s.at(f"square{k}"))
                    pe.matmul(banks[7][:, 0:self.width], ones, self.tmp[k % 4], start=k == 0,
                              stop=k == KD - 1).then_inc(pe_s.sem, pe_s.one(f"sum{k}"))

            def lo(self, engine, k, done):
                engine.wait_ge(self.a_s.sem, self.a_s.at(f"hi{k}"))
                engine.tensor_tensor(self.rhs.lo[:, k, :], self.tmp[k % 4], as_f32(self.rhs.hi[:, k, :]),
                                     ALU.subtract).then_inc(done.sem, done.one(f"lo{k}"))

            def vector(self, dve, between):
                a_s, pe_s, v_s, g_s = self.a_s, self.pe_s, self.v_s, self.g_s
                for k in self.squared[1::2]:
                    if k >= 4:
                        dve.wait_ge(pe_s.sem, pe_s.at(f"sum{k - 4}"))
                    dve.tensor_tensor(self.tmp[k % 4], self.src[:, k, :], self.src[:, k, :], ALU.mult).then_inc(
                        v_s.sem, v_s.one(f"square{k}"))
                if self.kept is None:
                    dve.wait_ge(a_s.sem, a_s.at("root"))
                    dve.reciprocal(self.few, self.few).then_inc(v_s.sem, v_s.one("inverse"))
                    if self.squares is None:
                        dve.wait_ge(v_s.sem, v_s.at("inverse"))
                    else:
                        dve.wait_ge(pe_s.sem, pe_s.at("spread"))
                for k in range(KD):
                    if k == 4:
                        between()
                    if k >= 4:
                        s = v_s if k - 4 in self.own_lo else g_s
                        dve.wait_ge(s.sem, s.at(f"lo{k - 4}"))
                    dve.scalar_tensor_tensor(self.tmp[k % 4], self.src[:, k, :], col(self.gain, k), self.factor,
                                             ALU.mult, ALU.mult).then_inc(v_s.sem, v_s.one(f"out{k}"))
                    if k - 1 in self.own_lo:
                        self.lo(dve, k - 1, v_s)

            def gpsimd(self, pool):
                for k in range(KD):
                    if k not in self.own_lo:
                        self.lo(pool, k, self.g_s)

            def ready(self, pe, k):
                s = self.v_s if k in self.own_lo else self.g_s
                pe.wait_ge(s.sem, s.at(f"lo{k}"))

        def project(name, pr, source=None, vector=None, scalar=None, following=None, reader="v"):
            with ExitStack() as scope:
                v_s, a_s = steps(**{name + "_vec": ["v0", "v1"], name + "_act": ["a0", "a1"]})
                emptied_by = v_s if reader == "v" else a_s
                if source:
                    pr.ready = source.ready
                with nc.Block() as block:
                    @block.sync
                    def _(sp):
                        pr.sync(sp, following)

                    @block.tensor
                    def _(pe):
                        if source:
                            source.tensor(pe)
                        pr.tensor(pe, (pr.passes - 1, lambda u, i: pe.wait_ge(emptied_by.sem, emptied_by.at(f"{reader}{u}", i))))

                    @block.scalar
                    def _(act):
                        pr.first_hi(act, source)
                        pr.scalar(act, (pr.passes, scalar and (
                            lambda i, u: scalar(act, i, u).then_inc(a_s.sem, a_s.one(f"a{u}")))))

                    @block.vector
                    def _(dve):
                        pr.first_lo(dve, source)
                        pr.vector(dve, (pr.passes, vector and (
                            lambda i, u: vector(dve, i, u).then_inc(v_s.sem, v_s.one(f"v{u}")))))

                    @block.gpsimd
                    def _(pool):
                        if source:
                            source.gpsimd(pool)
                pr.end()

        def add_to_residual(scope, name, w, rhs, following, source=None, **shape):
            pr = Projection(scope, name, w, rhs, KD, **shape)
            square = [area(scope, f"{name}_square{u}", T) for u in range(2)]
            zero_s, v_s, a_s = steps(**{name + "_zero": ["zero"], name + "_vec": ["x0", "sum0", "x1", "sum1"],
                                        name + "_act": ["square0", "square1"]})
            if source:
                pr.ready = source.ready

            def tile(i, u):
                return xT[:, bass.ds(i * (2 * T) + u * T, T)]

            with nc.Block() as block:
                @block.sync
                def _(sp):
                    pr.sync(sp, following)

                @block.tensor
                def _(pe):
                    pr.tensor(pe, (pr.passes - 1, lambda u, i: pe.wait_ge(v_s.sem, v_s.at(f"x{u}", i))))

                @block.scalar
                def _(act):
                    pr.first_hi(act, source)

                    def squared(i, u):
                        act.wait_ge(v_s.sem, v_s.at(f"x{u}", i))
                        act.activation(square[u], tile(i, u), ACT.Square).then_inc(a_s.sem, a_s.one(f"square{u}"))
                    pr.scalar(act, (pr.passes, squared))

                @block.vector
                def _(dve):
                    dve.memset(x_squares, 0.0).then_inc(zero_s.sem, zero_s.one("zero"))
                    pr.first_lo(dve, source)
                    dve.wait_ge(zero_s.sem, zero_s.at("zero"))

                    def add(i, u):
                        dve.tensor_tensor(tile(i, u), banks[u], tile(i, u), ALU.add).then_inc(v_s.sem, v_s.one(f"x{u}"))
                        dve.wait_ge(a_s.sem, a_s.at(f"square{u}", i))
                        dve.tensor_tensor(x_squares, square[u], x_squares, ALU.add).then_inc(v_s.sem, v_s.one(f"sum{u}"))
                    pr.vector(dve, (pr.passes, add))
            pr.end()

        mixer0 = ctx.enter_context(ExitStack())
        proj = area(mixer0, "proj0", REV0 * T + 8 * T)
        p3 = proj.rearrange("p (n t) -> p n t", t=T)
        lora = area(mixer0, "lora", 4 * T)
        dt_cum = area(mixer0, "dt_cum", 4 * T)
        with nc.Block() as block:
            @block.sync
            def _(sp):
                sp.dma_start(xT, dram["xT"]).then_inc(loads, 16)
                sp.dma_start(cols, dram["cols"]).then_inc(loads3, 16)
                sp.dma_start(tab[:, 0:2 * P], dram["tab"][:, 0:2 * P]).then_inc(loads6, 16)
                ring.prefetch(sp, dram["ab_in"])
                sp.dma_start(tab[:, 2 * P:NTAB], dram["tab"][:, 2 * P:NTAB]).then_inc(loads2, 16)
                sp.dma_start(lora, dram["lora"]).then_inc(loads5, 16)
                sp.dma_start(memT, dram["memT"]).then_inc(loads4, 16)
                for s in (loads, loads3, loads6):
                    sp.wait_ge(s, 16)

        def rwkv_ssd_projection(outer):
            work = area(outer, "ab_work", 5160)
            raw = [work[:, u * 520:u * 520 + 514] for u in range(2)]
            t1, t2, conv, sil = ([work[:, 1040 + j * 1024 + u * 512:1552 + j * 1024 + u * 512] for u in range(2)]
                                 for j in range(4))
            mu_half, mu_rest, decay_rate = work[:, 5136:5136 + 14], proj[:, 33 * T:33 * T + 14], work[0:8, 5152:5154]
            dt_x, dt_m, dt, cum = work[0:8, 1040:2064], work[0:8, 2064:3088], dt_cum[0:8, 0:1024], dt_cum[0:8, 1024:2048]
            rhs = halves(outer, "ab_h", KD)
            pr = Projection(outer, "ab_in", dram["ab_in"], rhs, 26, extra=1)
            source = NormSource(outer, "ab_in", x3, rhs, "mix0", room=work[:, 0:5 * T])
            pr.ready = source.ready
            with ExitStack() as scope:
                pe_s = pr.pe_s
                dtp_s, dth_s, dtl_s = steps(ab_dt_tile=["dt"], ab_dt_hi=["hi"], ab_dt_lo=["lo"])
                set_s, = steps(ab_setup=["zero0", "zero1", "zero2", "zero3", "half", "rest"])
                act_s, = steps(ab_raw=["raw0", "raw1"])
                v_s, = steps(ab_taps=["^", "mid0", "left0", "right0", "mid1", "left1", "right1"])
                vc_s, = steps(ab_conv=["^", "mid0", "left0", "right0", "mid1", "left1", "right1"])
                ac_s, = steps(ab_silu=["raw0", "silu0", "raw1", "silu1"])
                g_s, = steps(ab_reverse=["^", "fwd0", "rev0", "fwd1", "rev1"])
                az_s, = steps(ab_z=["z0", "z1"])
                dta_s, = steps(ab_dt_act=["rate", "exp", "log"])
                dtv_s, = steps(ab_dt_vec=["x0", "x1", "minus", "negrate", "dt0", "dt1", "la0", "la1",
                                                 "cum0", "cum1"])
                nrw, nx, nz = RW_TILES // 2, XBC_TILES // 2, Z_TILES // 2
                with nc.Block() as block:
                    @block.sync
                    def _(sp):
                        pr.sync(sp, None)
                        sp.wait_ge(dtv_s.sem, dtv_s.at("cum1"))
                        sp.dma_start(scratch_d.rearrange("(d h t) -> h d t", d=2, h=8),
                                     cum.rearrange("h (d t) -> h d t", d=2)).then_inc(stored_cum, 16)
                        for s in (stored_cum, loads2, loads4, loads5):
                            sp.wait_ge(s, 16)

                    @block.tensor
                    def _(pe):
                        source.tensor(pe)
                        def after(sem, name):
                            return lambda u, i: pe.wait_ge(sem.sem, sem.at(f"{name}{u}", i))

                        pr.tensor(pe, (nrw, after(act_s, "raw")),
                                  (nx, lambda u, i: pe.wait_ge(ac_s.sem, ac_s.at(f"raw{u}", i - nrw))),
                                  (nz - 1, lambda u, i: pe.wait_ge(az_s.sem, az_s.at(f"z{u}", i - (nrw + nx)))))
                        pe.wait_ge(dtl_s.sem, dtl_s.at("lo"))
                        ins = pr.products(pe, 0, 2)
                        ins.then_inc(dtp_s.sem, dtp_s.one("dt"))

                    @block.scalar
                    def _(act):
                        pr.first_hi(act, source)
                        act.wait_ge(set_s.sem, set_s.at("zero3"))

                        def rwkv_tile(i, u):
                            act.wait_ge(v_s.sem, v_s.passes(i))
                            act.activation(raw[u][:, 1:513], banks[u], ACT.Copy).then_inc(act_s.sem, act_s.one(f"raw{u}"))

                        def conv_tile(i, u):
                            i = i - nrw
                            act.wait_ge(v_s.sem, v_s.at("right1", nrw - 1))
                            act.wait_ge(vc_s.sem, vc_s.passes(i))
                            act.activation(raw[u][:, 1:513], banks[u], ACT.Copy).then_inc(ac_s.sem, ac_s.one(f"raw{u}"))
                            act.wait_ge(vc_s.sem, vc_s.at(f"right{u}", i))
                            act.wait_ge(g_s.sem, g_s.passes(i))
                            act.activation(sil[u], conv[u], ACT.Silu).then_inc(ac_s.sem, ac_s.one(f"silu{u}"))

                        def z_tile(i, u):
                            act.activation(proj[:, bass.ds(i * (2 * T) + (Z0 + u - 2 * (nrw + nx)) * T, T)], banks[u],
                                           ACT.Silu).then_inc(az_s.sem, az_s.one(f"z{u}"))

                        pr.scalar(act, (nrw, rwkv_tile), (nx, conv_tile), (nz, z_tile))
                        act.wait_ge(ring.sems[0], ring.at(0, pr.passes))
                        act.activation(pr.wt[0].hi_flat, slots[0][:, 0:pr.words], ACT.Copy).then_inc(dth_s.sem, dth_s.one("hi"))
                        act.activation(decay_rate, cols[0:8, COL["alog"]:COL["alog"] + 2], ACT.Exp).then_inc(dta_s.sem, dta_s.one("rate"))
                        act.wait_ge(dtv_s.sem, dtv_s.at("minus"))
                        act.activation(dt_m, dt_m, ACT.Exp).then_inc(dta_s.sem, dta_s.one("exp"))
                        act.wait_ge(dta_s.sem, dta_s.at("exp"))
                        act.activation(dt_m, dt_m, ACT.Ln, bias=1.0).then_inc(dta_s.sem, dta_s.one("log"))

                    @block.vector
                    def _(dve):
                        dve.sem_inc(v_s.sem, 1)
                        dve.sem_inc(vc_s.sem, 1)
                        pr.first_lo(dve, source)
                        dve.wait_ge(source.g_s.sem, source.g_s.at(f"lo{KD - 1}"))
                        dve.wait_ge(source.v_s.sem, source.v_s.at(f"lo{max(source.own_lo)}"))
                        for u in range(2):
                            dve.memset(raw[u][:, 0:1], 0.0).then_inc(set_s.sem, set_s.one(f"zero{2 * u}"))
                            dve.memset(raw[u][:, 513:514], 0.0).then_inc(set_s.sem, set_s.one(f"zero{2 * u + 1}"))
                        dve.tensor_scalar(mu_half, col("mu", 0, 14), 0.5, None, ALU.mult).then_inc(set_s.sem, set_s.one("half"))
                        dve.tensor_scalar(mu_rest, col("mu", 0, 14), -1.0, 1.0, ALU.mult, ALU.add).then_inc(set_s.sem, set_s.one("rest"))
                        dve.wait_ge(set_s.sem, set_s.at("rest"))
                        def rwkv_tile(i, u):
                            j = i * 2 + u
                            half = mu_half[:, bass.ds(j, 1)]
                            dve.wait_ge(act_s.sem, act_s.at(f"raw{u}", i))
                            dve.tensor_scalar(t1[u], raw[u][:, 1:513], mu_rest[:, bass.ds(j, 1)], None,
                                              ALU.mult).then_inc(v_s.sem, v_s.one(f"mid{u}"))
                            dve.wait_ge(v_s.sem, v_s.at(f"mid{u}", i))
                            dve.scalar_tensor_tensor(t2[u], raw[u][:, 0:512], half, t1[u],
                                                     ALU.mult, ALU.add).then_inc(v_s.sem, v_s.one(f"left{u}"))
                            dve.wait_ge(v_s.sem, v_s.at(f"left{u}", i))
                            dve.scalar_tensor_tensor(proj[:, bass.ds(i * (2 * T) + u * T, T)],
                                                     raw[u][:, 2:514], half, t2[u], ALU.mult, ALU.add).then_inc(v_s.sem, v_s.one(f"right{u}"))

                        def conv_tile(i, u):
                            def tap(n):
                                return cols[:, bass.ds(i * 8 + (COL["taps"] + 4 * u + n - 8 * nrw), 1)]
                            i0 = i - nrw
                            dve.wait_ge(v_s.sem, v_s.at("right1", nrw - 1))
                            dve.wait_ge(ac_s.sem, ac_s.at(f"raw{u}", i0))
                            dve.tensor_scalar(t1[u], raw[u][:, 1:513], tap(1), tap(3), ALU.mult, ALU.add).then_inc(vc_s.sem, vc_s.one(f"mid{u}"))
                            dve.wait_ge(vc_s.sem, vc_s.at(f"mid{u}", i0))
                            dve.scalar_tensor_tensor(t2[u], raw[u][:, 0:512], tap(0), t1[u],
                                                     ALU.mult, ALU.add).then_inc(vc_s.sem, vc_s.one(f"left{u}"))
                            dve.wait_ge(vc_s.sem, vc_s.at(f"left{u}", i0))
                            dve.scalar_tensor_tensor(conv[u], raw[u][:, 2:514], tap(2), t2[u],
                                                     ALU.mult, ALU.add).then_inc(vc_s.sem, vc_s.one(f"right{u}"))

                        pr.vector(dve, (nrw, rwkv_tile), (nx, conv_tile), (nz, None))
                        dve.wait_ge(dth_s.sem, dth_s.at("hi"))
                        dve.tensor_tensor(pr.wt[0].lo_flat, slots[0][:, 0:pr.words], as_f32(pr.wt[0].hi_flat),
                                          ALU.subtract).then_inc(dtl_s.sem, dtl_s.one("lo"))
                        dve.wait_ge(dtp_s.sem, dtp_s.at("dt"))
                        for d in range(2):
                            dve.tensor_scalar(dt_x[:, d * T:(d + 1) * T], banks[2][0:8, :],
                                                         cols[0:8, COL["dtb"] + d:COL["dtb"] + d + 1], None, ALU.add).then_inc(dtv_s.sem, dtv_s.one(f"x{d}"))
                        dve.wait_ge(dtv_s.sem, dtv_s.at("x1"))
                        dve.scalar_tensor_tensor(dt_m, dt_x, -1.0, dt_x, ALU.mult, ALU.min).then_inc(dtv_s.sem, dtv_s.one("minus"))
                        dve.wait_ge(dta_s.sem, dta_s.at("rate"))
                        dve.tensor_scalar(decay_rate, decay_rate, -1.0, None, ALU.mult).then_inc(dtv_s.sem, dtv_s.one("negrate"))
                        dve.wait_ge(dta_s.sem, dta_s.at("log"))
                        for d in range(2):
                            dve.scalar_tensor_tensor(
                                dt[:, d * T:(d + 1) * T], dirs[d](dt_x[:, d * T:(d + 1) * T]), 0.0,
                                dirs[d](dt_m[:, d * T:(d + 1) * T]), ALU.max, ALU.add).then_inc(dtv_s.sem, dtv_s.one(f"dt{d}"))
                        dve.wait_ge(dtv_s.sem, dtv_s.at("dt1"))
                        for d in range(2):
                            dve.tensor_scalar(dt_x[:, d * T:(d + 1) * T], dt[:, d * T:(d + 1) * T],
                                                         decay_rate[:, d:d + 1], None, ALU.mult).then_inc(dtv_s.sem, dtv_s.one(f"la{d}"))
                        dve.wait_ge(dtv_s.sem, dtv_s.at("la1"))
                        dve.wait_ge(loads2, 16)
                        for d in range(2):
                            dve.tensor_tensor_scan(cum[:, d * T:(d + 1) * T], tab[0:8, TAB["reset"]:TAB["reset"] + T],
                                                              dt_x[:, d * T:(d + 1) * T], 0.0, ALU.mult, ALU.add).then_inc(dtv_s.sem, dtv_s.one(f"cum{d}"))

                    @block.gpsimd
                    def _(pool):
                        pool.sem_inc(g_s.sem, 1)
                        source.gpsimd(pool)
                        with fori(pool, 0, nx) as i:
                            for u in range(2):
                                pool.wait_ge(ac_s.sem, ac_s.at(f"silu{u}", i))
                                for name, at, src in (("fwd", XS0, sil[u]), ("rev", REV0, sil[u][:, ::-1])):
                                    pool.tensor_copy(proj[:, bass.ds(i * (2 * T) + (at + u) * T, T)], src).then_inc(g_s.sem, g_s.one(f"{name}{u}"))
                pr.end()
            return dt, cum

        stored_cum = ctx.enter_context(nc.semaphore("cum_stored"))
        with ExitStack() as inner:
            dt_sb, cum_sb = rwkv_ssd_projection(inner)
        hT = area(mixer0, "hT0", KD * T)
        h3 = hT.rearrange("p (n t) -> p n t", t=T)

        def ssd(outer):
            PASSES = [(d, g) for d in range(2) for g in range(2)]
            UNITS = [(d, g, c) for d, g in PASSES for c in range(NC)]
            room = area(outer, "ssd_room", 27 * T)
            used = [0]

            def take(n):
                used[0] += n
                return room[:, used[0] - n:used[0]]

            cumb = [take(4 * T) for _ in PASSES]
            state = take(256)
            dt_tok, cum_tok, ecum = take(64), take(64), take(64)
            eend, wexp = take(64), take(64)
            dec, mix = [take(T), take(T)], [take(T), take(T)]
            sm, btok = [take(P), take(P)], [take(P), take(P)]
            xdt, xdtw, y2 = [take(256), take(256)], [take(256), take(256)], [take(256), take(256)]
            y1, tmp = take(256), take(256)
            score_bank, turn_bank, y_bank, off_bank, add_bank, back_bank = [0, 1], [2, 7], 3, 4, 5, 6

            def tile(first, d, n):
                return p3[:, (REV0 - XS0) * d + first + n, :]

            def h4(ap):
                return ap.rearrange("p (h w) -> p h w", h=4)

            def heads_of(ap, d, g, c):
                return ap[:, (d * NC + c) * 8 + g * 4:(d * NC + c) * 8 + g * 4 + 4]

            def per_head(ap, unit, w):
                return heads_of(ap, *unit).unsqueeze(2).broadcast_to([P, 4, w])

            def chunk_ends(it):
                return cumb[it].rearrange("p (h c t) -> p c h t", h=4, t=P)[:, :, :, P - 1]

            def heads_of_pass(ap, d, g):
                return ap.rearrange("p (n h) -> p n h", h=8)[:, d * NC:(d + 1) * NC, g * 4:g * 4 + 4]

            pre_pe, pre_v, pre_a = steps(ssd_pre_pe=["tok"], ssd_pre_vec=["dt_tok", "cum_tok", "state"] + [f"wdiff{i}" for i in range(4)],
                                         ssd_pre_act=["ecum"] + [f"{n}{i}" for i in range(4) for n in ("eend", "wexp")])
            f_pe, f_act, f_vec, f_pool = steps(ssd_F_pe=["scores", "turned"], ssd_F_act=["dec", "btok"],
                                               ssd_F_vec=["sm", "xdt", "xdtw", "mix"], ssd_F_pool=["dec", "cap"])
            off_pe, b_pe, b_act, b_vec = steps(ssd_off_pe=["off"], ssd_B_pe=["add", "y", "back"], ssd_B_act=["out"],
                                       ssd_B_vec=["y1", "hdecay", "hadd", "y2"])
            cumb_sem = [ctx.enter_context(nc.semaphore(f"cumb{i}_loaded")) for i in range(len(PASSES))]

            def in_turn(front, back):
                front(0)
                for w in range(len(UNITS)):
                    if w + 1 < len(UNITS):
                        front(w + 1)
                    back(w)

            with nc.Block() as block:
                @block.sync
                def _(sp):
                    for it in range(len(PASSES)):
                        sp.dma_start(cumb[it], scratch_d[it * 4 * T:(it + 1) * 4 * T].partition_broadcast(P)).then_inc(cumb_sem[it], 16)

                @block.tensor
                def _(pe):
                    for d in range(2):
                        for c in range(NC):
                            w = d * T + c * P
                            k = (d * NC + c) * 8
                            pe.transpose(banks[0][:, k:k + 8], dt_sb[:, w:w + P], ident[0:8, 0:8])
                            ins = pe.transpose(banks[1][:, k:k + 8], cum_sb[:, w:w + P], ident[0:8, 0:8])
                    ins.then_inc(pre_pe.sem, pre_pe.one("tok"))
                    pe.wait_ge(pre_v.sem, pre_v.at("cum_tok"))

                    def front(w):
                        (d, g, c), u = UNITS[w], w % 2
                        if w >= 2:
                            pe.wait_ge(f_vec.sem, f_vec.at("sm", w - 2))
                        pe.matmul(banks[score_bank[u]][:, 0:P], chunk(tile(B0, d, g), c), chunk(tile(C0, d, g), c), start=True, stop=True
                                  ).then_inc(f_pe.sem, f_pe.one("scores"))
                        if w >= 2:
                            pe.wait_ge(f_act.sem, f_act.at("btok", w - 2))
                        bank = banks[turn_bank[u]]
                        for j in range(2):
                            pe.transpose(chunk(bank, j), chunk(tile(XS0, d, 2 * g + j), c), ident)
                        pe.transpose(chunk(bank, 2), chunk(tile(B0, d, g), c), ident).then_inc(f_pe.sem, f_pe.one("turned"))

                    def back(w):
                        (d, g, c), u = UNITS[w], w % 2
                        if w:
                            pe.wait_ge(b_vec.sem, b_vec.at("hadd", w - 1))
                        if c:
                            pe.matmul(banks[off_bank][:, 0:256], chunk(tile(C0, d, g), c), state, start=True, stop=True
                                      ).then_inc(off_pe.sem, off_pe.one("off"))
                        pe.wait_ge(f_vec.sem, f_vec.at("xdtw", w))
                        pe.wait_ge(f_act.sem, f_act.at("btok", w))
                        pe.matmul(banks[add_bank][:, 0:256], btok[u], xdtw[u], start=True, stop=True).then_inc(b_pe.sem, b_pe.one("add"))
                        pe.wait_ge(f_vec.sem, f_vec.at("mix", w))
                        if w:
                            pe.wait_ge(b_vec.sem, b_vec.at("y2", w - 1))
                        for h in range(4):
                            ins = pe.matmul(banks[y_bank][:, h * HD:(h + 1) * HD], chunk(mix[u], h),
                                            xdt[u][:, h * HD:(h + 1) * HD], start=True, stop=True)
                        ins.then_inc(b_pe.sem, b_pe.one("y"))
                        pe.wait_ge(b_vec.sem, b_vec.at("y2", w))
                        if w:
                            pe.wait_ge(b_act.sem, b_act.at("out", w - 1))
                        for j in range(2):
                            ins = pe.transpose(chunk(banks[back_bank], j), chunk(y2[u], j), ident)
                        ins.then_inc(b_pe.sem, b_pe.one("back"))
                    in_turn(front, back)

                @block.scalar
                def _(act):
                    act.wait_ge(pre_v.sem, pre_v.at("cum_tok"))
                    act.activation(ecum, cum_tok, ACT.Exp).then_inc(pre_a.sem, pre_a.one("ecum"))
                    for it, (d, g) in enumerate(PASSES):
                        act.wait_ge(cumb_sem[it], 16)
                        act.activation(heads_of_pass(eend, d, g), chunk_ends(it), ACT.Exp).then_inc(pre_a.sem, pre_a.one(f"eend{it}"))
                        act.wait_ge(pre_v.sem, pre_v.at(f"wdiff{it}"))
                        act.activation(heads_of_pass(wexp, d, g), heads_of_pass(wexp, d, g), ACT.Exp).then_inc(pre_a.sem, pre_a.one(f"wexp{it}"))

                    def front(w):
                        u = w % 2
                        act.wait_ge(f_pool.sem, f_pool.at("cap", w))
                        act.activation(dec[u], dec[u], ACT.Exp).then_inc(f_act.sem, f_act.one("dec"))
                        act.wait_ge(f_vec.sem, f_vec.at("xdt", w))
                        if w >= 2:
                            act.wait_ge(b_pe.sem, b_pe.at("add", w - 2))
                        act.activation(btok[u], chunk(banks[turn_bank[u]], 2), ACT.Copy).then_inc(f_act.sem, f_act.one("btok"))

                    def back(w):
                        d, g, c = UNITS[w]
                        act.wait_ge(b_pe.sem, b_pe.at("back", w))
                        act.activation(h3[:, d * 4 + g * 2:d * 4 + g * 2 + 2, c * P:(c + 1) * P],
                                       banks[back_bank][:, 0:256].rearrange("p (j t) -> p j t", t=P),
                                       ACT.Copy).then_inc(b_act.sem, b_act.one("out"))
                    in_turn(front, back)

                @block.gpsimd
                def _(pool):
                    pool.wait_ge(pre_v.sem, pre_v.at("cum_tok"))
                    for w, (d, g, c) in enumerate(UNITS):
                        it = w // NC
                        if c == 0:
                            pool.wait_ge(cumb_sem[it], 16)
                        if w >= 2:
                            pool.wait_ge(f_vec.sem, f_vec.at("mix", w - 2))
                        pool.tensor_tensor(h4(dec[w % 2]), h4(cumb[it])[:, :, c * P:(c + 1) * P], per_head(cum_tok, (d, g, c), P),
                                           ALU.subtract).then_inc(f_pool.sem, f_pool.one("dec"))
                        pool.wait_ge(f_pool.sem, f_pool.at("dec", w))
                        pool.tensor_scalar(dec[w % 2], dec[w % 2], 0.0, None, ALU.min).then_inc(f_pool.sem, f_pool.one("cap"))

                @block.vector
                def _(dve):
                    dve.wait_ge(pre_pe.sem, pre_pe.at("tok"))
                    dve.tensor_copy(dt_tok, banks[0][:, 0:64]).then_inc(pre_v.sem, pre_v.one("dt_tok"))
                    dve.tensor_copy(cum_tok, banks[1][:, 0:64]).then_inc(pre_v.sem, pre_v.one("cum_tok"))
                    dve.memset(state, 0.0).then_inc(pre_v.sem, pre_v.one("state"))
                    dve.wait_ge(pre_v.sem, pre_v.at("state"))
                    for it, (d, g) in enumerate(PASSES):
                        dve.wait_ge(cumb_sem[it], 16)
                        dve.tensor_tensor(heads_of_pass(wexp, d, g), chunk_ends(it), heads_of_pass(cum_tok, d, g),
                                          ALU.subtract).then_inc(pre_v.sem, pre_v.one(f"wdiff{it}"))

                    def front(w):
                        unit, u = UNITS[w], w % 2
                        dve.wait_ge(f_pe.sem, f_pe.at("scores", w))
                        if w >= 2:
                            dve.wait_ge(f_vec.sem, f_vec.at("mix", w - 2))
                        dve.tensor_tensor(sm[u], banks[score_bank[u]][:, 0:P], table("incl"), ALU.mult).then_inc(f_vec.sem, f_vec.one("sm"))
                        dve.wait_ge(f_pe.sem, f_pe.at("turned", w))
                        if w >= 2:
                            dve.wait_ge(b_pe.sem, b_pe.at("y", w - 2))
                        dve.tensor_tensor(h4(xdt[u]), h4(banks[turn_bank[u]][:, 0:256]), per_head(dt_tok, unit, HD), ALU.mult).then_inc(f_vec.sem, f_vec.one("xdt"))
                        if w == 0:
                            dve.wait_ge(pre_a.sem, pre_a.at("wexp3"))
                        dve.wait_ge(f_vec.sem, f_vec.at("xdt", w))
                        dve.tensor_tensor(h4(xdtw[u]), h4(xdt[u]), per_head(wexp, unit, HD), ALU.mult).then_inc(f_vec.sem, f_vec.one("xdtw"))

                    def mixed(w):
                        u = w % 2
                        dve.wait_ge(f_act.sem, f_act.at("dec", w))
                        dve.tensor_tensor(h4(mix[u]), h4(dec[u]), sm[u].unsqueeze(1).broadcast_to([P, 4, P]), ALU.mult).then_inc(f_vec.sem, f_vec.one("mix"))

                    def back(w):
                        unit, u = UNITS[w], w % 2
                        first = unit[2] == 0
                        if not first:
                            dve.wait_ge(off_pe.sem, off_pe.at("off", w // NC * (NC - 1) + unit[2] - 1))
                        if w:
                            dve.wait_ge(b_vec.sem, b_vec.at("y2", w - 1))
                        if first:
                            dve.memset(y1, 0.0).then_inc(b_vec.sem, b_vec.one("y1"))
                            dve.memset(tmp, 0.0).then_inc(b_vec.sem, b_vec.one("hdecay"))
                        else:
                            dve.tensor_tensor(h4(y1), h4(banks[off_bank][:, 0:256]), per_head(ecum, unit, HD), ALU.mult).then_inc(b_vec.sem, b_vec.one("y1"))
                            dve.tensor_tensor(h4(tmp), h4(state), per_head(eend, unit, HD), ALU.mult).then_inc(b_vec.sem, b_vec.one("hdecay"))
                        dve.wait_ge(b_pe.sem, b_pe.at("add", w))
                        dve.wait_ge(b_vec.sem, b_vec.at("hdecay", w))
                        dve.tensor_tensor(state, banks[add_bank][:, 0:256], tmp, ALU.add).then_inc(b_vec.sem, b_vec.one("hadd"))
                        if w + 1 < len(UNITS):
                            mixed(w + 1)
                        dve.wait_ge(b_pe.sem, b_pe.at("y", w))
                        if w >= 2:
                            dve.wait_ge(b_pe.sem, b_pe.at("back", w - 2))
                        dve.tensor_tensor(y2[u], banks[y_bank][:, 0:256], y1, ALU.add).then_inc(b_vec.sem, b_vec.one("y2"))

                    def first_front(w):
                        front(w)
                        if w == 0:
                            mixed(w)
                    in_turn(first_front, back)

        def ssd_gate(outer):
            both, skip, sq = (area(outer, "gate_" + n, 4 * T) for n in ("both", "skip", "square"))
            root, inv = (area(outer, "gate_" + n, 2 * T) for n in ("root", "inverse"))
            with ExitStack() as scope:
                v_s, a_s, pe_s = steps(
                    gate_vec=["both"] + [f"skip{j}" for j in range(4)] + ["gated", "inverse"] + [f"out{j}" for j in range(4)],
                    gate_act=["square", "root0", "root1"], gate_pe=["sum0", "sum1"])
                with nc.Block() as block:
                    @block.vector
                    def _(dve):
                        dve.tensor_tensor(both.rearrange("p (j t) -> p j t", t=T), h3[:, 0:4, :], h3[:, 4:8, ::-1],
                                                   ALU.add).then_inc(v_s.sem, v_s.one("both"))
                        dve.wait_ge(v_s.sem, v_s.at("both"))
                        for j in range(4):
                            dve.scalar_tensor_tensor(skip[:, j * T:(j + 1) * T], p3[:, XS0 + j, :], col("ssd_d", j),
                                                              both[:, j * T:(j + 1) * T], ALU.mult, ALU.add).then_inc(v_s.sem, v_s.one(f"skip{j}"))
                        dve.wait_ge(v_s.sem, v_s.at("skip3"))
                        dve.tensor_tensor(hT[:, 4 * T:8 * T], skip, proj[:, Z0 * T:(Z0 + 4) * T], ALU.mult).then_inc(v_s.sem, v_s.one("gated"))
                        dve.wait_ge(a_s.sem, a_s.at("root1"))
                        dve.reciprocal(inv, root).then_inc(v_s.sem, v_s.one("inverse"))
                        dve.wait_ge(v_s.sem, v_s.at("inverse"))
                        for j in range(4):
                            dve.scalar_tensor_tensor(h3[:, 4 + j, :], h3[:, 4 + j, :], col("ssd_w", j),
                                                              inv[:, (j // 2) * T:(j // 2 + 1) * T], ALU.mult, ALU.mult).then_inc(v_s.sem, v_s.one(f"out{j}"))

                    @block.scalar
                    def _(act):
                        act.wait_ge(v_s.sem, v_s.at("gated"))
                        act.activation(sq, hT[:, 4 * T:8 * T], ACT.Square).then_inc(a_s.sem, a_s.one("square"))
                        for g in range(2):
                            act.wait_ge(pe_s.sem, pe_s.at(f"sum{g}"))
                            act.activation(root[:, g * T:(g + 1) * T], banks[g], ACT.Sqrt, bias=col("eps"),
                                                    scale=1.0 / 256).then_inc(a_s.sem, a_s.one(f"root{g}"))

                    @block.tensor
                    def _(pe):
                        pe.wait_ge(a_s.sem, a_s.at("square"))
                        for g in range(2):
                            for j in range(2):
                                ins = pe.matmul(banks[g], ones, sq[:, (2 * g + j) * T:(2 * g + j + 1) * T],
                                                start=j == 0, stop=j == 1)
                            ins.then_inc(pe_s.sem, pe_s.one(f"sum{g}"))

        with ExitStack() as inner:
            ssd(inner)
        with ExitStack() as inner:
            ssd_gate(inner)

        def rwkv(outer):
            spans = [[xT, 0, 8 * T], [proj, XS0 * T, REV0 * T + 8 * T], [dt_cum, 0, 4 * T],
                     [area(outer, "rw_work", RW_WORDS), 0, RW_WORDS]]

            def take(words):
                for s in spans:
                    if s[1] + words <= s[2]:
                        s[1] += words
                        return s[0][:, s[1] - words:s[1]]
                raise ValueError("no room")

            r_st, v_st, a_t, sg0, sg1, kk, km, b_t = (take(T) for _ in range(8))
            assert spans[0][1] == spans[0][2]
            sg, ka1 = [sg0, sg1], b_t
            low, sq, rk = take(T), take(T), take(T)
            cum, cen, cex, pos, neg, prv = (take(T) for _ in range(6))
            b_i, k_i, v_r = take(T), take(T), take(T)
            x_m = [take(T), take(T)]
            y_m = [take(T), take(T)]
            o_t, osq = take(T), take(T)
            def chunks_of_pairs():
                return take(2 * NC * P).rearrange("p (c w t) -> p c w t", c=NC, w=2)

            kr = [chunks_of_pairs() for _ in range(2)]
            ac = [[chunks_of_pairs() for h in range(2)] for d in range(2)]
            be = [[chunks_of_pairs() for h in range(2)] for d in range(2)]
            x_t = [[take(T), take(T)] for d in range(2)]
            b_tok, k_tok, v_tok = ([take(T) for d in range(2)] for _ in range(3))
            state, added, rhs, sa = (take(P) for _ in range(4))
            vec, mid, carry = take(8), take(4), [take(4), take(4)]
            tanh_ad, gate_in = p3[:, 12, :], p3[:, 13, :]
            y_bank, z_bank, zt_bank = [4, 6], [3, 5], [7, 0]
            turn_bank = [3, 4, 5]
            score_bank = {("ac", 0, 0): 6, ("ac", 0, 1): 7, ("ac", 1, 0): 0, ("ac", 1, 1): 3,
                          ("be", 0, 0): 4, ("be", 0, 1): 5, ("be", 1, 0): 6, ("be", 1, 1): 7}
            nl = len(LEVELS) - 1
            heads = range(2)
            hs = [slice(h * HD, (h + 1) * HD) for h in heads]
            slot_list = ([("turn", n) for n in range(3)]
                         + [("score", m, h, q) for m in ("ac", "be") for h in heads for q in range(2)]
                         + [("x", h) for h in heads]
                         + [(kind, n, h) for n in range(1, nl + 1) for kind in ("y", "z") for h in heads])
            chain_at = {0: 11, 1: 3}
            chain_end = 4 * NC

            def vcol(name):
                return vec[:, RW_VECS.index(name):RW_VECS.index(name) + 1]

            def tile_col(name, ct):
                return cols[:, bass.ds(ct * 8 + (COL["rw"] + RW_VECS.index(name)), 1)]

            def tile_of(ap, ct, first=0):
                return ap[:, bass.ds(ct * T + first * T, T)]

            def level_names(kinds):
                return [f"{k}{n}{h}_%d" for n in range(1, nl + 1) for group in (["y"], ["z", "zt"]) for h in heads
                        for k in group if k in kinds and not (k == "z" and n == nl)]

            def both_dirs(names):
                return [n % d for d in range(2) for n in names]

            scores = [f"{m}{h}{q}_%d" for m in ("ac", "be") for h in heads for q in range(2)]
            masked = scores[:3] + ["xa0_%d", "xt0_%d"] + scores[3:5] + ["xa1_%d", "xt1_%d"] + scores[5:]
            with ExitStack() as scope:
                zero_s, pre_a = steps(rw_zero=[f"{m}{d}{h}" for d in range(2) for h in heads for m in ("ac", "be")] + ["y0", "y1"],
                                      rw_pre=["tanh", "gate"])
                i_pe, i_act, i_vec = steps(
                    rw_I_pe=both_dirs(["turn0_%d", "turn1_%d", "turn2_%d"] + scores + ["x0_%d", "x1_%d"]
                                             + level_names(["y", "z", "zt"])),
                    rw_I_act=both_dirs(["tok0_%d", "tok1_%d", "tok2_%d", "x0_%d", "x1_%d"] + level_names(["y"])),
                    rw_I_vec=both_dirs(masked + level_names(["z", "zt"])))
                chain = ["%s%d" % (s, c) for c in range(NC) for s in ("rhs", "sa", "s", "o") if not (s == "s" and c == NC - 1)]
                c_pe, c_act, c_vec = steps(
                    rw_C_pe=["^"] + both_dirs([n + "_%d" for n in chain]),
                    rw_C_act=[f"{s}{c}_0" for c in range(NC) for s in ("rhs", "sa")] + ["out_0"]
                    + [f"{s}{c}_1" for c in range(NC) for s in ("rhs", "sa")],
                    rw_C_vec=both_dirs(["zero_%d"] + [f"{s}{c}_%d" for c in range(NC - 1) for s in ("add", "s")]) + ["out_1"])
                e_act, e_vec, e_pool = steps(
                    rw_E_act=both_dirs(["pos_%d", "neg_%d", "prv_%d", "mid_%d"]),
                    rw_E_vec=both_dirs(["cum_%d", "cen_%d", "cex_%d", "kkP_%d", "bI_%d", "carry_%d"]),
                    rw_E_pool=both_dirs(["v_%d", "rP_%d", "kI_%d"]))
                p_pe, p_act, p_vec, p_pool = steps(
                    rw_P_pe=["a", "w0", "w1", "g", "norm", "bonus"], rw_P_act=["a", "w0", "w1", "g", "sq", "root"],
                    rw_P_vec=["kk0", "ka", "km", "rk", "nmax", "ninv", "kk", "b", "bonus"],
                    rw_P_pool=["low", "vec", "r", "v"])
                f_pe, f_act, f_vec = steps(
                    rw_F_pe=["mean", "var"], rw_F_act=["^", "osq", "oroot"],
                    rw_F_vec=["^", "centre", "oinv", "on", "og", "ob", "res"])

                def wait_chain(engine, ct, d, before):
                    if d:
                        engine.wait_ge(c_pe.sem, c_pe.passes(ct))
                    elif before is not None:
                        engine.wait_ge(c_pe.sem, c_pe.at("o3_0", before))

                def run(engine, slot_I, prep, chain_step, elementwise, finish):
                    slots_of_unit = range(len(slot_list))
                    for t in slots_of_unit:
                        prep(t, 0, None)
                        elementwise(t, 0, 0, None)
                    for t in slots_of_unit:
                        slot_I(t, 0, 0, None)
                        elementwise(t, 0, 1, None)
                    with fori(engine, 0, 3) as ct:
                        for t in slots_of_unit:
                            slot_I(t, ct, 1, None)
                            prep(t, ct + 1, ct)
                            chain_step(t - chain_at[0], ct, 0)
                            elementwise(t, ct + 1, 0, ct)
                        for t in slots_of_unit:
                            slot_I(t, ct + 1, 0, ct)
                            chain_step(t - chain_at[1], ct, 1)
                            finish(t, ct)
                            elementwise(t, ct + 1, 1, ct)
                    for t in slots_of_unit:
                        slot_I(t, 3, 1, None)
                        chain_step(t - chain_at[0], 3, 0)
                    for j in range(chain_end + 1):
                        chain_step(j, 3, 1)
                    for t in slots_of_unit:
                        finish(t, 3)

                with nc.Block() as block:
                    @block.sync
                    def _(sp):
                        ring.prefetch(sp, dram["ab_out"])
                        sp.wait_ge(e_vec.sem, e_vec.at("carry_1", 3))
                        sp.wait_ge(e_pool.sem, e_pool.at("kI_1", 3))
                        sp.dma_start(xT, dram["xT"]).then_inc(loads, 16)
                        sp.wait_ge(loads, 32)

                    @block.gpsimd
                    def _(pool):
                        def prep(t, ct, before):
                            if t != 0:
                                return
                            if before is not None:
                                pool.wait_ge(p_vec.sem, p_vec.at("bonus", before))
                                pool.wait_ge(p_pe.sem, p_pe.at("g", before))
                                pool.wait_ge(p_act.sem, p_act.at("w1", before))
                                pool.wait_ge(e_pool.sem, e_pool.at("kI_1", before))
                                hold(pool, "pool")
                            pool.tensor_copy(low.rearrange("p (m c) -> p m c", m=4),
                                             lora.rearrange("p (m c) -> p m c", m=4)[:, :, bass.ds(ct * P, P)]
                                             ).then_inc(p_pool.sem, p_pool.one("low"))
                            pool.tensor_copy(vec, cols[:, bass.ds(ct * 8 + COL["rw"], 8)]).then_inc(p_pool.sem, p_pool.one("vec"))
                            pool.tensor_copy(r_st, tile_of(proj, ct)).then_inc(p_pool.sem, p_pool.one("r"))
                            pool.tensor_copy(v_st, tile_of(proj, ct, 8)).then_inc(p_pool.sem, p_pool.one("v"))
                            if before is None:
                                for d in range(2):
                                    for h in heads:
                                        pool.memset(ac[d][h], 0.0).then_inc(zero_s.sem, zero_s.one(f"ac{d}{h}"))
                                        pool.memset(be[d][h], 0.0).then_inc(zero_s.sem, zero_s.one(f"be{d}{h}"))
                                for h in heads:
                                    pool.memset(y_m[h], 0.0).then_inc(zero_s.sem, zero_s.one(f"y{h}"))

                        def elementwise(t, ct, d, before):
                            if t != 0:
                                return
                            pool.wait_ge(p_pool.sem, p_pool.at("v", ct))
                            if d:
                                pool.wait_ge(i_pe.sem, i_pe.at("be11_0", ct))
                            elif before is not None:
                                pool.wait_ge(i_pe.sem, i_pe.at("be11_1", before))
                            hold(pool, "pool")
                            pool.tensor_copy(v_r, dirs[d](v_st)).then_inc(e_pool.sem, e_pool.one(f"v_{d}"))
                            pool.wait_ge(e_act.sem, e_act.at(f"neg_{d}", ct))
                            wait_chain(pool, ct, d, before)
                            pool.tensor_tensor(kr[d][:, :, 1, :], by_chunk(dirs[d](r_st)), by_chunk(pos), ALU.mult
                                               ).then_inc(e_pool.sem, e_pool.one(f"rP_{d}"))
                            pool.wait_ge(p_vec.sem, p_vec.at("b", ct))
                            pool.tensor_tensor(k_i, dirs[d](km), neg, ALU.mult).then_inc(e_pool.sem, e_pool.one(f"kI_{d}"))

                        def nothing(t, *unit):
                            pass

                        run(pool, nothing, prep, nothing, elementwise, nothing)

                    @block.tensor
                    def _(pe):
                        pe.wait_ge(pre_a.sem, pre_a.at("gate"))
                        pe.sem_inc(c_pe.sem, 1)

                        def prep(t, ct, before):
                            if t == 4:
                                pe.wait_ge(p_pool.sem, p_pool.at("low", ct))
                                if before is not None:
                                    pe.wait_ge(f_act.sem, f_act.passes(before))
                                    pe.wait_ge(f_vec.sem, f_vec.passes(before))
                                pe.matmul(banks[1], low[64:P, 2 * P:3 * P], tanh_ad[64:P, :], start=True, stop=True
                                          ).then_inc(p_pe.sem, p_pe.one("a"))
                                pe.matmul(banks[2], low[0:64, 0:P], tanh_ad[0:64, :], start=True, stop=True
                                          ).then_inc(p_pe.sem, p_pe.one("w0"))
                            if t == 5:
                                pe.wait_ge(p_act.sem, p_act.at("a", ct))
                                pe.matmul(banks[1], low[0:64, P:2 * P], tanh_ad[0:64, :], start=True, stop=True
                                          ).then_inc(p_pe.sem, p_pe.one("w1"))
                            if t == 6:
                                pe.wait_ge(p_act.sem, p_act.at("w0", ct))
                                pe.matmul(banks[2], low[:, 3 * P:4 * P], gate_in, start=True, stop=True
                                          ).then_inc(p_pe.sem, p_pe.one("g"))
                            if t == 8:
                                pe.wait_ge(p_act.sem, p_act.at("sq", ct))
                                pe.matmul(banks[1], blk, sq, start=True, stop=True).then_inc(p_pe.sem, p_pe.one("norm"))
                                pe.wait_ge(p_vec.sem, p_vec.at("rk", ct))
                                pe.matmul(banks[2], blk, rk, start=True, stop=True).then_inc(p_pe.sem, p_pe.one("bonus"))

                        def slot_I(t, ct, d, before):
                            kind, *which = slot_list[t]
                            prev = ("_0", ct) if d else ("_1", before)
                            if kind == "turn":
                                n, = which
                                src = (b_i, k_i, v_r)[n]
                                s, name = ((e_vec, "bI"), (e_pool, "kI"), (e_pool, "v"))[n]
                                pe.wait_ge(s.sem, s.at(f"{name}_{d}", ct))
                                if prev[1] is not None:
                                    s, name = ((i_vec, f"z{nl - 1}0"), (i_act, f"y{nl}0"), (i_vec, f"z{nl - 1}1"))[n]
                                    pe.wait_ge(s.sem, s.at(name + prev[0], prev[1]))
                                for c in range(NC):
                                    ins = pe.transpose(chunk(banks[turn_bank[n]], c), chunk(src, c), ident)
                                ins.then_inc(i_pe.sem, i_pe.one(f"turn{n}_{d}"))
                            if kind == "score":
                                m, h, q = which
                                if which == ["ac", 0, 0]:
                                    pe.wait_ge(e_vec.sem, e_vec.at(f"kkP_{d}", ct))
                                    pe.wait_ge(e_pool.sem, e_pool.at(f"rP_{d}", ct))
                                before_in_bank = {("ac", 0, 0): (i_act, f"y{nl}1"), ("ac", 0, 1): (i_vec, f"zt{nl}0"),
                                                  ("ac", 1, 0): (i_vec, f"zt{nl}1")}
                                now_in_bank = {("ac", 1, 1): (i_act, "tok0"), ("be", 0, 0): (i_act, "tok1"),
                                               ("be", 0, 1): (i_act, "tok2"), ("be", 1, 0): (i_vec, "ac00"),
                                               ("be", 1, 1): (i_vec, "ac01")}
                                if (m, h, q) in now_in_bank:
                                    s, name = now_in_bank[m, h, q]
                                    pe.wait_ge(s.sem, s.at(f"{name}_{d}", ct))
                                elif prev[1] is not None:
                                    s, name = before_in_bank[m, h, q]
                                    pe.wait_ge(s.sem, s.at(name + prev[0], prev[1]))
                                bank = banks[score_bank[m, h, q]].rearrange("p (c w) -> p c w", c=2)
                                for e in range(2):
                                    c = 2 * q + e
                                    ins = pe.matmul(bank[:, e, :], chunk(b_i if m == "ac" else k_i, c)[hs[h], :],
                                                    kr[d][hs[h], c, :, :], start=True, stop=True)
                                ins.then_inc(i_pe.sem, i_pe.one(f"{m}{h}{q}_{d}"))
                            if kind == "x":
                                h, = which
                                pe.wait_ge(i_vec.sem, i_vec.at(f"xt{h}_{d}", ct))
                                pe.wait_ge(i_vec.sem, i_vec.at(("ac11_%d", "be01_%d")[h] % d, ct))
                                for c in range(NC):
                                    ins = pe.transpose(chunk(banks[z_bank[h]], c), chunk(x_t[d][h], c), ident)
                                ins.then_inc(i_pe.sem, i_pe.one(f"x{h}_{d}"))
                            if kind == "y":
                                n, h = which
                                if n == 1:
                                    pe.wait_ge(i_act.sem, i_act.at(f"x{h}_{d}", ct))
                                    pe.wait_ge(i_vec.sem, i_vec.at(f"be11_{d}", ct))
                                else:
                                    pe.wait_ge(i_vec.sem, i_vec.at(f"zt{n - 1}{h}_{d}", ct))
                                for c in range(NC):
                                    ins = pe.matmul(chunk(banks[y_bank[h]], c), ac[d][h][:, c, 0, :], chunk(x_m[h], c),
                                                    start=True, stop=True)
                                ins.then_inc(i_pe.sem, i_pe.one(f"y{n}{h}_{d}"))
                            if kind == "z":
                                n, h = which
                                pe.wait_ge(i_act.sem, i_act.at(f"y{n}{h}_{d}", ct))
                                if n < nl:
                                    for c in range(NC):
                                        ins = pe.matmul(chunk(banks[z_bank[h]], c), chunk(x_t[d][h], c), chunk(y_m[h], c),
                                                        start=True, stop=True)
                                    ins.then_inc(i_pe.sem, i_pe.one(f"z{n}{h}_{d}"))
                                for c in range(NC):
                                    if n == nl:
                                        b = LEVELS[n]
                                        ins = pe.matmul(chunk(banks[zt_bank[h]], c)[0:b, b:P], chunk(y_m[h], c)[:, 0:b],
                                                        chunk(x_t[d][h], c)[:, b:P], start=True, stop=True)
                                        continue
                                    ins = pe.matmul(chunk(banks[zt_bank[h]], c), chunk(y_m[h], c), chunk(x_t[d][h], c),
                                                    start=True, stop=True)
                                ins.then_inc(i_pe.sem, i_pe.one(f"zt{n}{h}_{d}"))

                        def chain_step(j, ct, d):
                            if not 0 <= j < chain_end:
                                return
                            c, kind = j // 4, ("rhs", "sa", "s", "o")[j % 4]
                            if kind == "rhs":
                                pe.wait_ge(c_vec.sem, c_vec.at(f"s{c - 1}_{d}" if c else f"zero_{d}", ct))
                                if c == 0:
                                    pe.wait_ge(i_vec.sem, i_vec.at(f"zt{nl}1_{d}", ct))
                                    if d == 0 and not (isinstance(ct, int) and ct == 3):
                                        pe.wait_ge(p_act.sem, p_act.at("root", ct + 1))
                                        pe.wait_ge(p_vec.sem, p_vec.at("bonus", ct + 1))
                                    elif d == 0:
                                        pe.wait_ge(f_act.sem, f_act.passes(ct))
                                    else:
                                        pe.wait_ge(c_act.sem, c_act.at("out_0", ct))
                                pe.matmul(banks[1][:, 0:P], kr[d][:, c, 0, :], state, start=True, stop=False)
                                for h in heads:
                                    ins = pe.matmul(banks[1][:, hs[h]], be[d][h][:, c, 0, :], chunk(v_tok[d], c)[:, hs[h]],
                                                    start=False, stop=h == 1)
                                ins.then_inc(c_pe.sem, c_pe.one(f"rhs{c}_{d}"))
                            if kind == "sa":
                                pe.wait_ge(c_act.sem, c_act.at(f"rhs{c}_{d}", ct))
                                for h in heads:
                                    ins = pe.matmul(banks[1][:, P + h * HD:P + (h + 1) * HD], chunk(x_t[d][h], c), rhs[:, hs[h]],
                                                    start=True, stop=True)
                                ins.then_inc(c_pe.sem, c_pe.one(f"sa{c}_{d}"))
                            if kind == "s" and c < NC - 1:
                                pe.wait_ge(c_act.sem, c_act.at(f"sa{c}_{d}", ct))
                                pe.matmul(banks[1][:, 2 * P:3 * P], chunk(b_tok[d], c), sa, start=True, stop=False)
                                pe.matmul(banks[1][:, 2 * P:3 * P], chunk(k_tok[d], c), chunk(v_tok[d], c),
                                          start=False, stop=True).then_inc(c_pe.sem, c_pe.one(f"s{c}_{d}"))
                            if kind == "o":
                                pe.wait_ge(c_act.sem, c_act.at(f"sa{c}_{d}", ct))
                                out = chunk(banks[2], c)
                                pe.matmul(out, state, kr[d][:, c, 1, :], start=True, stop=False)
                                for h in heads:
                                    pe.matmul(out[hs[h], :], sa[:, hs[h]], ac[d][h][:, c, 1, :], start=False, stop=False)
                                    ins = pe.matmul(out[hs[h], :], chunk(v_tok[d], c)[:, hs[h]], be[d][h][:, c, 1, :],
                                                    start=False, stop=True)
                                ins.then_inc(c_pe.sem, c_pe.one(f"o{c}_{d}"))

                        def finish(t, ct):
                            if t == 20:
                                pe.wait_ge(c_vec.sem, c_vec.at("out_1", ct))
                                pe.matmul(banks[1], blk, o_t, start=True, stop=True).then_inc(f_pe.sem, f_pe.one("mean"))
                            if t == 23:
                                pe.wait_ge(f_act.sem, f_act.at("osq", ct))
                                pe.matmul(banks[2], blk, osq, start=True, stop=True).then_inc(f_pe.sem, f_pe.one("var"))

                        def nothing(t, *unit):
                            pass

                        run(pe, slot_I, prep, chain_step, nothing, finish)

                    @block.scalar
                    def _(act):
                        act.activation(tanh_ad[0:64, :], tanh_ad[0:64, :], ACT.Tanh).then_inc(pre_a.sem, pre_a.one("tanh"))
                        act.activation(gate_in, gate_in, ACT.Sigmoid).then_inc(pre_a.sem, pre_a.one("gate"))
                        act.sem_inc(f_act.sem, 1)

                        def prep(t, ct, before):
                            if t == 4:
                                act.wait_ge(p_pool.sem, p_pool.at("vec", ct))
                                if before is not None:
                                    act.wait_ge(e_vec.sem, e_vec.at("carry_1", before))
                                    act.wait_ge(p_vec.sem, p_vec.at("bonus", before))
                                for name, bank, dst, bias in (("a", 1, a_t, "a0"), ("w0", 2, sg0, "w0f")):
                                    act.wait_ge(p_pe.sem, p_pe.at(name, ct))
                                    act.activation(dst, banks[bank], ACT.Sigmoid, bias=vcol(bias)).then_inc(p_act.sem, p_act.one(name))
                            if t == 5:
                                act.wait_ge(p_pe.sem, p_pe.at("w1", ct))
                                act.activation(sg1, banks[1], ACT.Sigmoid, bias=vcol("w0b")).then_inc(p_act.sem, p_act.one("w1"))
                            if t == 7:
                                act.wait_ge(p_pe.sem, p_pe.at("g", ct))
                                act.wait_ge(p_vec.sem, p_vec.at("km", ct))
                                act.activation(tile_of(proj, ct, 4), banks[2], ACT.Copy).then_inc(p_act.sem, p_act.one("g"))
                                act.activation(sq, kk, ACT.Square).then_inc(p_act.sem, p_act.one("sq"))
                            if t == 8:
                                act.wait_ge(p_pe.sem, p_pe.at("norm", ct))
                                act.activation(sq, banks[1], ACT.Sqrt).then_inc(p_act.sem, p_act.one("root"))

                        def slot_I(t, ct, d, before):
                            kind, *which = slot_list[t]
                            if kind == "turn":
                                n, = which
                                if n == 0:
                                    wait_chain(act, ct, d, before)
                                act.wait_ge(i_pe.sem, i_pe.at(f"turn{n}_{d}", ct))
                                act.activation((b_tok, k_tok, v_tok)[n][d], banks[turn_bank[n]], ACT.Copy
                                               ).then_inc(i_act.sem, i_act.one(f"tok{n}_{d}"))
                            if kind == "x":
                                h, = which
                                act.wait_ge(i_pe.sem, i_pe.at(f"x{h}_{d}", ct))
                                act.activation(x_m[h], banks[z_bank[h]], ACT.Copy).then_inc(i_act.sem, i_act.one(f"x{h}_{d}"))
                            if kind == "y":
                                n, h = which
                                act.wait_ge(zero_s.sem, zero_s.at("y1"))
                                act.wait_ge(i_pe.sem, i_pe.at(f"y{n}{h}_{d}", ct))
                                act.activation(blocks(y_m[h], LEVELS[n], 0), blocks(banks[y_bank[h]], LEVELS[n], 0), ACT.Copy
                                               ).then_inc(i_act.sem, i_act.one(f"y{n}{h}_{d}"))

                        def chain_step(j, ct, d):
                            if 0 <= j < chain_end and j % 4 < 2:
                                c, kind = j // 4, ("rhs", "sa")[j % 4]
                                act.wait_ge(c_pe.sem, c_pe.at(f"{kind}{c}_{d}", ct))
                                if kind == "rhs":
                                    act.activation(rhs, banks[1][:, 0:P], ACT.Copy).then_inc(c_act.sem, c_act.one(f"rhs{c}_{d}"))
                                else:
                                    act.activation(sa, banks[1][:, P:2 * P], ACT.Copy).then_inc(c_act.sem, c_act.one(f"sa{c}_{d}"))
                            if j == chain_end and d == 0:
                                act.wait_ge(c_pe.sem, c_pe.at("o3_0", ct))
                                act.wait_ge(f_vec.sem, f_vec.passes(ct))
                                act.activation(o_t, banks[2], ACT.Copy).then_inc(c_act.sem, c_act.one("out_0"))

                        def elementwise(t, ct, d, before):
                            if t != 14:
                                return
                            if d:
                                act.wait_ge(e_vec.sem, e_vec.at("carry_0", ct))
                                act.wait_ge(e_pool.sem, e_pool.at("kI_0", ct))
                            elif before is not None:
                                act.wait_ge(e_vec.sem, e_vec.at("carry_1", before))
                                act.wait_ge(e_pool.sem, e_pool.at("kI_1", before))
                            act.wait_ge(e_vec.sem, e_vec.at(f"cex_{d}", ct))
                            act.activation(pos, cen, ACT.Exp, scale=-DECAY_SCALE).then_inc(e_act.sem, e_act.one(f"pos_{d}"))
                            act.activation(neg, cen, ACT.Exp, scale=DECAY_SCALE).then_inc(e_act.sem, e_act.one(f"neg_{d}"))
                            act.activation(prv, cex, ACT.Exp, scale=-DECAY_SCALE).then_inc(e_act.sem, e_act.one(f"prv_{d}"))
                            act.activation(mid, by_chunk(cum)[:, :, HD - 1], ACT.Exp, scale=-DECAY_SCALE
                                           ).then_inc(e_act.sem, e_act.one(f"mid_{d}"))

                        def finish(t, ct):
                            if t == 21:
                                act.wait_ge(f_vec.sem, f_vec.at("centre", ct))
                                act.activation(osq, o_t, ACT.Square).then_inc(f_act.sem, f_act.one("osq"))
                            if t == 24:
                                act.wait_ge(f_pe.sem, f_pe.at("var", ct))
                                act.activation(osq, banks[2], ACT.Sqrt, bias=col("gneps"), scale=1.0 / HD
                                               ).then_inc(f_act.sem, f_act.one("oroot"))

                        run(act, slot_I, prep, chain_step, elementwise, finish)

                    @block.vector
                    def _(dve):
                        dve.sem_inc(f_vec.sem, 1)
                        causal = table("strict", 2 * P).bitcast(U32)

                        def prep(t, ct, before):
                            k_in = tile_of(proj, ct, 4)
                            if t == 4:
                                dve.wait_ge(p_pool.sem, p_pool.at("vec", ct))
                                if before is not None:
                                    dve.wait_ge(e_vec.sem, e_vec.at("carry_1", before))
                                dve.tensor_scalar(kk, k_in, vcol("kk"), None, ALU.mult).then_inc(p_vec.sem, p_vec.one("kk0"))
                            if t == 5:
                                dve.wait_ge(p_act.sem, p_act.at("a", ct))
                                dve.tensor_scalar(ka1, a_t, vcol("ka"), vcol("ka"), ALU.mult, ALU.subtract).then_inc(p_vec.sem, p_vec.one("ka"))
                                dve.wait_ge(p_vec.sem, p_vec.at("ka", ct))
                                if before is not None:
                                    dve.wait_ge(e_pool.sem, e_pool.at("kI_1", before))
                                dve.scalar_tensor_tensor(km, ka1, 1.0, k_in, ALU.add, ALU.mult).then_inc(p_vec.sem, p_vec.one("km"))
                            if t == 6:
                                dve.wait_ge(p_vec.sem, p_vec.at("km", ct))
                                dve.wait_ge(p_pool.sem, p_pool.at("v", ct))
                                if before is not None:
                                    dve.wait_ge(p_pe.sem, p_pe.at("bonus", before))
                                dve.scalar_tensor_tensor(rk, r_st, vcol("rk"), km, ALU.mult, ALU.mult).then_inc(p_vec.sem, p_vec.one("rk"))
                            if t == 9:
                                dve.wait_ge(p_act.sem, p_act.at("root", ct))
                                dve.tensor_scalar(sq, sq, 1e-12, None, ALU.max).then_inc(p_vec.sem, p_vec.one("nmax"))
                                dve.wait_ge(p_vec.sem, p_vec.at("nmax", ct))
                                dve.reciprocal(sq, sq).then_inc(p_vec.sem, p_vec.one("ninv"))
                            if t == 10:
                                dve.wait_ge(p_vec.sem, p_vec.at("ninv", ct))
                                dve.tensor_tensor(kk, kk, sq, ALU.mult).then_inc(p_vec.sem, p_vec.one("kk"))
                                dve.wait_ge(p_vec.sem, p_vec.at("kk", ct))
                                dve.tensor_tensor(b_t, kk, a_t, ALU.mult).then_inc(p_vec.sem, p_vec.one("b"))
                                dve.wait_ge(p_pe.sem, p_pe.at("bonus", ct))
                                dve.tensor_tensor(tile_of(hT, ct), banks[2], v_st, ALU.mult).then_inc(p_vec.sem, p_vec.one("bonus"))

                        def elementwise(t, ct, d, before):
                            if t == (7 if before is None and d == 0 else 12):
                                dve.wait_ge(p_act.sem, p_act.at("w1", ct))
                                if d:
                                    dve.wait_ge(e_act.sem, e_act.at("mid_0", ct))
                                elif before is not None:
                                    dve.wait_ge(e_act.sem, e_act.at("mid_1", before))
                                dve.tensor_tensor_scan(cum, table("reset", T), dirs[d](sg[d]), 0.0, ALU.mult, ALU.add
                                                       ).then_inc(e_vec.sem, e_vec.one(f"cum_{d}"))
                                dve.wait_ge(e_vec.sem, e_vec.at(f"cum_{d}", ct))
                                dve.tensor_tensor(by_chunk(cen), by_chunk(cum), by_chunk(cum)[:, :, HD - 1:HD].broadcast_to([P, NC, P]),
                                                  ALU.subtract).then_inc(e_vec.sem, e_vec.one(f"cen_{d}"))
                                dve.wait_ge(e_vec.sem, e_vec.at(f"cen_{d}", ct))
                                dve.tensor_tensor(cex, cen, dirs[d](sg[d]), ALU.subtract).then_inc(e_vec.sem, e_vec.one(f"cex_{d}"))
                            if t == (22 if d else 28):
                                dve.wait_ge(e_act.sem, e_act.at(f"mid_{d}", ct))
                                dve.wait_ge(p_vec.sem, p_vec.at("b", ct))
                                wait_chain(dve, ct, d, before)
                                dve.scalar_tensor_tensor(kr[d][:, :, 0, :], by_chunk(dirs[d](kk)), -1.0, by_chunk(prv),
                                                         ALU.mult, ALU.mult).then_inc(e_vec.sem, e_vec.one(f"kkP_{d}"))
                                if d:
                                    dve.wait_ge(i_pe.sem, i_pe.at("be11_0", ct))
                                elif before is not None:
                                    dve.wait_ge(i_pe.sem, i_pe.at("be11_1", before))
                                dve.tensor_tensor(b_i, dirs[d](b_t), neg, ALU.mult).then_inc(e_vec.sem, e_vec.one(f"bI_{d}"))
                                dve.tensor_tensor(carry[d][:, 0:3], by_chunk(pos)[:, 0:3, P - 1], mid[:, 1:4], ALU.mult
                                                  ).then_inc(e_vec.sem, e_vec.one(f"carry_{d}"))

                        def slot_I(t, ct, d, before):
                            kind, *which = slot_list[t]
                            if kind == "score":
                                m, h, q = which
                                if which == ["ac", 0, 0]:
                                    dve.wait_ge(zero_s.sem, zero_s.at("y1"))
                                    wait_chain(dve, ct, d, before)
                                dve.wait_ge(i_pe.sem, i_pe.at(f"{m}{h}{q}_{d}", ct))
                                hold(dve, "vec")
                                dve.copy_predicated(
                                    (ac if m == "ac" else be)[d][h][:, 2 * q:2 * q + 2, :, :].rearrange("p c w t -> p c (w t)"),
                                    causal.unsqueeze(1).broadcast_to([P, 2, 2 * P]),
                                    banks[score_bank[m, h, q]].rearrange("p (c w) -> p c w", c=2)).then_inc(i_vec.sem, i_vec.one(f"{m}{h}{q}_{d}"))
                                if which in (["ac", 1, 0], ["be", 0, 0]):
                                    x = 0 if m == "ac" else 1
                                    dve.wait_ge(i_vec.sem, i_vec.at(f"ac{x}1_{d}", ct))
                                    dve.tensor_tensor(by_chunk(x_t[d][x]), ac[d][x][:, :, 0, :],
                                                      over_chunks(table("up")), ALU.mult).then_inc(i_vec.sem, i_vec.one(f"xa{x}_{d}"))
                                    dve.wait_ge(i_vec.sem, i_vec.at(f"xa{x}_{d}", ct))
                                    dve.tensor_tensor(by_chunk(x_t[d][x]), by_chunk(x_t[d][x]), over_chunks(ident), ALU.add
                                                      ).then_inc(i_vec.sem, i_vec.one(f"xt{x}_{d}"))
                            if kind == "z":
                                n, h = which
                                if n < nl:
                                    dve.wait_ge(i_pe.sem, i_pe.at(f"z{n}{h}_{d}", ct))
                                    hold(dve, "vec")
                                    dve.copy_predicated(blocks_of_chunks(x_m[h], LEVELS[n], 0), block_mask("low", n, 0),
                                                        blocks_of_chunks(banks[z_bank[h]], LEVELS[n], 0)).then_inc(i_vec.sem, i_vec.one(f"z{n}{h}_{d}"))
                                dve.wait_ge(i_pe.sem, i_pe.at(f"zt{n}{h}_{d}", ct))
                                hold(dve, "vec")
                                dve.copy_predicated(blocks_of_chunks(x_t[d][h], LEVELS[n], 1), block_mask("up", n, 1),
                                                    blocks_of_chunks(banks[zt_bank[h]], LEVELS[n], 1)).then_inc(i_vec.sem, i_vec.one(f"zt{n}{h}_{d}"))

                        def chain_step(j, ct, d):
                            if j == 0:
                                dve.wait_ge(c_pe.sem, c_pe.at("o3_0", ct) if d else c_pe.passes(ct))
                                dve.memset(state, 0.0).then_inc(c_vec.sem, c_vec.one(f"zero_{d}"))
                            if 0 <= j < 4 * (NC - 1) and j % 4 >= 2:
                                c = j // 4
                                if j % 4 == 2:
                                    dve.wait_ge(c_pe.sem, c_pe.at(f"s{c}_{d}", ct))
                                    dve.tensor_tensor(added, banks[1][:, 2 * P:3 * P], state, ALU.add).then_inc(c_vec.sem, c_vec.one(f"add{c}_{d}"))
                                else:
                                    dve.wait_ge(c_vec.sem, c_vec.at(f"add{c}_{d}", ct))
                                    dve.wait_ge(c_pe.sem, c_pe.at(f"o{c}_{d}", ct))
                                    dve.scalar_tensor_tensor(state, added, carry[d][:, c:c + 1], blk, ALU.mult, ALU.mult
                                                             ).then_inc(c_vec.sem, c_vec.one(f"s{c}_{d}"))
                            if j == chain_end and d:
                                dve.wait_ge(c_pe.sem, c_pe.at("o3_1", ct))
                                dve.wait_ge(c_act.sem, c_act.at("out_0", ct))
                                dve.tensor_tensor(o_t, banks[2][:, ::-1], o_t, ALU.add).then_inc(c_vec.sem, c_vec.one("out_1"))

                        def finish(t, ct):
                            if t == 20:
                                dve.wait_ge(f_pe.sem, f_pe.at("mean", ct))
                                dve.scalar_tensor_tensor(o_t, banks[1], -1.0 / HD, o_t, ALU.mult, ALU.add).then_inc(f_vec.sem, f_vec.one("centre"))
                            if t == 25:
                                dve.wait_ge(f_act.sem, f_act.at("oroot", ct))
                                dve.reciprocal(osq, osq).then_inc(f_vec.sem, f_vec.one("oinv"))
                                dve.wait_ge(f_vec.sem, f_vec.at("oinv", ct))
                                dve.tensor_tensor(o_t, o_t, osq, ALU.mult).then_inc(f_vec.sem, f_vec.one("on"))
                            if t == 27:
                                dve.wait_ge(f_vec.sem, f_vec.at("on", ct))
                                dve.tensor_scalar(o_t, o_t, tile_col("gnw", ct), tile_col("gnb", ct), ALU.mult, ALU.add
                                                  ).then_inc(f_vec.sem, f_vec.one("og"))
                                dve.wait_ge(f_vec.sem, f_vec.at("og", ct))
                                dve.tensor_tensor(o_t, o_t, tile_of(hT, ct), ALU.add).then_inc(f_vec.sem, f_vec.one("ob"))
                            if t == 29:
                                dve.wait_ge(f_vec.sem, f_vec.at("ob", ct))
                                dve.tensor_tensor(tile_of(hT, ct), o_t, tile_of(proj, ct, 4), ALU.mult).then_inc(f_vec.sem, f_vec.one("res"))

                        run(dve, slot_I, prep, chain_step, elementwise, finish)

        with ExitStack() as inner:
            rwkv(inner)
        clear_semaphores()
        with ExitStack() as inner:
            rhs = halves(inner, "mix0_h", KD)
            add_to_residual(inner, "mix0_out", dram["ab_out"], rhs, dram["wk0"], SplitSource(inner, "mix0", h3, rhs))
        mixer0.close()

        def cross_attention(n, outer):
            kT, vt, qT = (area(outer, f"xa{n}_{m}", w) for m, w in (("k", KD * MEM), ("v", KD * MEM), ("q", KD * T)))
            v3 = vt.rearrange("p (b d) -> p b d", b=2)
            rhs = halves(outer, f"xa{n}_h", KD)
            with ExitStack() as inner:
                memn = halves(inner, f"mem{n}", KD, MEM)
                name = f"keys{n}"
                wk = Projection(inner, name, dram[f"wk{n}"], memn, KD, n=MEM)
                project(name, wk, NormSource(inner, name, mem3, memn, f"mem{n}", MEM, keep=None if n else mem_inv, kept=mem_inv if n else None),
                        vector=lambda dve, i, u: dve.tensor_copy(kT[:, bass.ds(i * (2 * MEM) + u * MEM, MEM)], banks[u][:, 0:MEM]),
                        following=dram[f"wv{n}"])
                name = f"values{n}"
                wv = Projection(inner, name, dram[f"wv{n}"], memn, 4, k=4, cuts=2, token_major=True)

                def values(dve, i, u):
                    for b in range(2):
                        ins = dve.tensor_copy(v3[:, b, bass.ds(i * 512 + u * 256, 256)], banks[2 * u + b][:, 0:256])
                    return ins
                project(name, wv, vector=values, following=dram[f"wq{n}"])
            with ExitStack() as inner:
                name = f"queries{n}"
                wq = Projection(inner, name, dram[f"wq{n}"], rhs, KD)
                project(name, wq, NormSource(inner, name, x3, rhs, f"xa{n}", squares=x_squares), scalar=lambda act, i, u: act.activation(
                    qT[:, bass.ds(i * (2 * T) + u * T, T)], banks[u], ACT.Copy, scale=1.0 / 16), reader="a")

            prob, prob_t = ([area(outer, f"xa{n}_{m}{u}", 4 * MEM) for u in range(2)] for m in ("prob", "probt"))
            sums = area(outer, f"xa{n}_sums", 16)
            top, total = ([sums[:, 8 * m + 4 * u:8 * m + 4 * u + 4] for u in range(2)] for m in range(2))
            k3, q3 = kT.rearrange("p (n m) -> p n m", m=MEM), qT.rearrange("p (n t) -> p n t", t=T)
            heads = range(D // 256)
            sc_s, sa_s, sv_s = steps(**{f"xa{n}_scores": ["s0", "s1"], f"xa{n}_exp": [f"exp{c}" for c in range(NC)],
                                        f"xa{n}_top": ["top0", "top1", "minus"]})
            pe_s, a_s, v_s = steps(**{f"xa{n}_pe": ["turn0", "turn1", "o0", "o1"], f"xa{n}_act": ["p0", "o0", "o1"],
                                      f"xa{n}_vec": ["total", "prob", "p1", "lo0", "lo1"]})

            def in_turn(scores, rest):
                scores(0)
                for h in heads:
                    if h + 1 < len(heads):
                        scores(h + 1)
                    rest(h)

            def score(h, c):
                return banks[2 * (h % 2) + c // 2][:, (c % 2) * MEM:(c % 2 + 1) * MEM]

            def prob_of(h):
                return prob[h % 2].rearrange("p (c m) -> p c m", c=NC)

            def turned(h):
                return prob_t[h % 2].rearrange("p (b t) -> p b t", b=2)

            with nc.Block() as block:
                @block.sync
                def _(sp):
                    ring.prefetch(sp, dram[f"wo{n}"])

                @block.tensor
                def _(pe):
                    def scores(h):
                        if h >= 2:
                            pe.wait_ge(sa_s.sem, sa_s.at("exp3", h - 2))
                        for c in range(NC):
                            for k in range(2):
                                ins = pe.matmul(score(h, c), chunk(q3[:, 2 * h + k, :], c), k3[:, 2 * h + k, :],
                                                start=k == 0, stop=k == 1)
                            if c % 2:
                                ins.then_inc(sc_s.sem, sc_s.one(f"s{c // 2}"))

                    def rest(h):
                        pe.wait_ge(v_s.sem, v_s.at("prob", h))
                        for b in range(2):
                            if h:
                                s = a_s if b == 0 else v_s
                                pe.wait_ge(s.sem, s.at(f"p{b}", h - 1))
                            for c in range(NC):
                                ins = pe.transpose(chunk(banks[4 + b], c), prob_of(h)[:, c, b * P:(b + 1) * P], ident)
                            ins.then_inc(pe_s.sem, pe_s.one(f"turn{b}"))
                        pe.wait_ge(a_s.sem, a_s.at("p0", h))
                        pe.wait_ge(v_s.sem, v_s.at("p1", h))
                        for d in range(2):
                            if h:
                                pe.wait_ge(v_s.sem, v_s.at(f"lo{d}", h - 1))
                            for b in range(2):
                                ins = pe.matmul(banks[6 + d], v3[:, b, h * 256 + d * P:h * 256 + (d + 1) * P],
                                                turned(h)[:, b, :], start=b == 0, stop=b == 1)
                            ins.then_inc(pe_s.sem, pe_s.one(f"o{d}"))
                    in_turn(scores, rest)

                @block.vector
                def _(dve):
                    def scores(h):
                        if h >= 2:
                            dve.wait_ge(sa_s.sem, sa_s.at("exp3", h - 2))
                        for b in range(2):
                            dve.wait_ge(sc_s.sem, sc_s.at(f"s{b}", h))
                            dve.tensor_reduce(top[h % 2][:, 2 * b:2 * b + 2], banks[2 * (h % 2) + b].rearrange("p (c m) -> p c m", c=2),
                                              AXX, ALU.max).then_inc(sv_s.sem, sv_s.one(f"top{b}"))
                        dve.wait_ge(sv_s.sem, sv_s.at("top1", h))
                        dve.tensor_scalar(top[h % 2], top[h % 2], -1.0, None, ALU.mult).then_inc(sv_s.sem, sv_s.one("minus"))

                    def rest(h):
                        dve.wait_ge(sa_s.sem, sa_s.at("exp3", h))
                        dve.reciprocal(total[h % 2], total[h % 2]).then_inc(v_s.sem, v_s.one("total"))
                        dve.wait_ge(v_s.sem, v_s.at("total", h))
                        dve.tensor_tensor(prob_of(h), prob_of(h), total[h % 2].unsqueeze(2).broadcast_to([P, NC, MEM]), ALU.mult
                                          ).then_inc(v_s.sem, v_s.one("prob"))
                        dve.wait_ge(pe_s.sem, pe_s.at("turn1", h))
                        dve.tensor_copy(turned(h)[:, 1, :], banks[5]).then_inc(v_s.sem, v_s.one("p1"))
                        for d in range(2):
                            dve.wait_ge(a_s.sem, a_s.at(f"o{d}", h))
                            dve.tensor_tensor(rhs.lo[:, 2 * h + d, :], banks[6 + d], as_f32(rhs.hi[:, 2 * h + d, :]), ALU.subtract
                                              ).then_inc(v_s.sem, v_s.one(f"lo{d}"))
                    in_turn(scores, rest)

                @block.scalar
                def _(act):
                    def scores(h):
                        if h >= 2:
                            act.wait_ge(pe_s.sem, pe_s.at("turn1", h - 2))
                        act.wait_ge(sv_s.sem, sv_s.at("minus", h))
                        for c in range(NC):
                            act.activation(prob_of(h)[:, c, :], score(h, c), ACT.Exp, bias=top[h % 2][:, c:c + 1],
                                           accum_out=total[h % 2][:, c:c + 1]).then_inc(sa_s.sem, sa_s.one(f"exp{c}"))

                    def rest(h):
                        act.wait_ge(pe_s.sem, pe_s.at("turn0", h))
                        act.activation(turned(h)[:, 0, :], banks[4], ACT.Copy).then_inc(a_s.sem, a_s.one("p0"))
                        for d in range(2):
                            act.wait_ge(pe_s.sem, pe_s.at(f"o{d}", h))
                            act.activation(rhs.hi[:, 2 * h + d, :], banks[6 + d], ACT.Copy).then_inc(a_s.sem, a_s.one(f"o{d}"))
                    in_turn(scores, rest)

            add_to_residual(outer, f"xa_out{n}", dram[f"wo{n}"], rhs, dram[f"f_in{n}"])

        def swiglu(n, outer, following):
            gated = halves(outer, f"ffn{n}_a", FT)
            with ExitStack() as scope:
                rhs = halves(scope, f"ffn{n}_h", KD)
                w_in = Projection(scope, f"ffn{n}_in", dram[f"f_in{n}"], rhs, 2 * FT)
                source = NormSource(scope, f"ffn{n}", x3, rhs, f"ffn{n}", squares=x_squares)
                w_in.ready = source.ready
                silu, both = area(scope, f"ffn{n}_silu", T), area(scope, f"ffn{n}_both", T)
                a_s, v_s = steps(**{f"ffn{n}_act": ["silu", "hi"], f"ffn{n}_vec": ["^", "gated", "lo"]})
                with nc.Block() as block:
                    @block.sync
                    def _(sp):
                        w_in.sync(sp, dram[f"f_out{n}"])

                    @block.tensor
                    def _(pe):
                        source.tensor(pe)
                        w_in.tensor(pe, (FT - 1, lambda u, i: pe.wait_ge(v_s.sem, v_s.at("gated", i)) if u
                                         else pe.wait_ge(a_s.sem, a_s.at("silu", i))))

                    @block.scalar
                    def _(act):
                        w_in.first_hi(act, source)

                        def tile(i, u):
                            if u == 0:
                                act.wait_ge(v_s.sem, v_s.passes(i))
                                act.activation(silu, banks[0], ACT.Silu).then_inc(a_s.sem, a_s.one("silu"))
                            else:
                                act.wait_ge(v_s.sem, v_s.at("gated", i))
                                act.activation(gated.hi_flat[:, bass.ds(i * T, T)], both, ACT.Copy).then_inc(a_s.sem, a_s.one("hi"))
                        w_in.scalar(act, (FT, tile))

                    @block.vector
                    def _(dve):
                        dve.sem_inc(v_s.sem, 1)
                        w_in.first_lo(dve, source)

                        def tile(i, u):
                            if u:
                                dve.wait_ge(v_s.sem, v_s.passes(i))
                                dve.wait_ge(a_s.sem, a_s.at("silu", i))
                                dve.tensor_tensor(both, silu, banks[1], ALU.mult).then_inc(v_s.sem, v_s.one("gated"))
                                dve.wait_ge(a_s.sem, a_s.at("hi", i))
                                at = bass.ds(i * T, T)
                                dve.tensor_tensor(gated.lo_flat[:, at], both, as_f32(gated.hi_flat)[:, at],
                                                  ALU.subtract).then_inc(v_s.sem, v_s.one("lo"))
                        w_in.vector(dve, (FT, tile))

                    @block.gpsimd
                    def _(pool):
                        source.gpsimd(pool)
                w_in.end()
            with ExitStack() as scope:
                add_to_residual(scope, f"ffn{n}_out", dram[f"f_out{n}"], gated, following, k=FT // 2, cuts=2)

        Q1, FWD1, BWD1, I1, G1 = (HEADS * j for j in range(5))

        def hgrn_projection(outer):
            rhs = halves(outer, "hg_h", KD)
            pr = Projection(outer, "hg_in", dram["hg_in"], rhs, 5 * HEADS)
            source = NormSource(outer, "hg_in", x3, rhs, "mix1", squares=x_squares)
            pr.ready = source.ready
            room = area(outer, "hg_gates", 2 * T + 24)
            sig = [room[:, u * T:(u + 1) * T] for u in range(2)]
            low, rest, top = (room[:, 2 * T + 8 * j:2 * T + 8 * j + 8] for j in range(3))
            a_s, f_s, pre_v, pre_a = steps(hg_emptied=["a0", "a1"], hg_gate=["^", "f0", "f1"],
                                           hg_pre_vec=["top", "d0", "d1", "sum", "inv", "low", "rest"], hg_pre_act=["e0", "e1"])
            with nc.Block() as block:
                @block.sync
                def _(sp):
                    pr.sync(sp, None)

                @block.tensor
                def _(pe):
                    source.tensor(pe)
                    pr.tensor(pe, (pr.passes - 1, lambda u, i: pe.wait_ge(a_s.sem, a_s.at(f"a{u}", i))))

                @block.scalar
                def _(act):
                    act.wait_ge(pre_v.sem, pre_v.at("d1"))
                    act.activation(low, low, ACT.Exp).then_inc(pre_a.sem, pre_a.one("e0"))
                    act.activation(rest, rest, ACT.Exp).then_inc(pre_a.sem, pre_a.one("e1"))
                    pr.first_hi(act, source)

                    def emptier(func):
                        def tile(i, u):
                            act.activation(proj1[:, bass.ds(i * (2 * T) + u * T, T)], banks[u], func).then_inc(a_s.sem, a_s.one(f"a{u}"))
                        return tile

                    def gate(i, u):
                        act.wait_ge(f_s.sem, f_s.passes(i - HEADS // 2))
                        act.activation(sig[u], banks[u], ACT.Sigmoid).then_inc(a_s.sem, a_s.one(f"a{u}"))

                    pr.scalar(act, (HEADS // 2, emptier(ACT.Copy)), (HEADS, gate), (HEADS // 2, emptier(ACT.Copy)),
                              (HEADS // 2, emptier(ACT.Silu)))

                @block.vector
                def _(dve):
                    l0, l1 = col("lb0", 0, 8), col("lb1", 0, 8)
                    dve.tensor_tensor(top, l0, l1, ALU.max).then_inc(pre_v.sem, pre_v.one("top"))
                    dve.wait_ge(pre_v.sem, pre_v.at("top"))
                    dve.tensor_tensor(rest, l0, top, ALU.subtract).then_inc(pre_v.sem, pre_v.one("d0"))
                    dve.tensor_tensor(low, l1, top, ALU.subtract).then_inc(pre_v.sem, pre_v.one("d1"))
                    dve.wait_ge(pre_a.sem, pre_a.at("e1"))
                    dve.tensor_tensor(rest, low, rest, ALU.add).then_inc(pre_v.sem, pre_v.one("sum"))
                    dve.wait_ge(pre_v.sem, pre_v.at("sum"))
                    dve.reciprocal(rest, rest).then_inc(pre_v.sem, pre_v.one("inv"))
                    dve.wait_ge(pre_v.sem, pre_v.at("inv"))
                    dve.tensor_tensor(low, low, rest, ALU.mult).then_inc(pre_v.sem, pre_v.one("low"))
                    dve.wait_ge(pre_v.sem, pre_v.at("low"))
                    dve.tensor_scalar(rest, low, -1.0, 1.0, ALU.mult, ALU.add).then_inc(pre_v.sem, pre_v.one("rest"))
                    dve.wait_ge(pre_v.sem, pre_v.at("rest"))
                    dve.sem_inc(f_s.sem, 1)
                    pr.first_lo(dve, source)

                    def gate(d):
                        def tile(i, u):
                            first = (HEADS // 2) * (1 + d)
                            dve.wait_ge(a_s.sem, a_s.at(f"a{u}", i))
                            c = bass.ds(i * 2 + (u - 2 * first), 1)
                            dve.tensor_scalar(proj1[:, bass.ds(i * (2 * T) + u * T, T)], dirs[d](sig[u]), rest[:, c], low[:, c],
                                              ALU.mult, ALU.add).then_inc(f_s.sem, f_s.one(f"f{u}"))
                        return tile

                    pr.vector(dve, (HEADS // 2, None), (HEADS // 2, gate(0)), (HEADS // 2, gate(1)), (HEADS, None))

                @block.gpsimd
                def _(pool):
                    source.gpsimd(pool)
            pr.end()

        def hgrn(outer):
            nl = len(LEVELS)
            words = 15400
            work = area(outer, "hg_work", words)
            used = [0]

            def take(n):
                used[0] += n
                assert used[0] <= words
                return work[:, used[0] - n:used[0]]

            def pairs_of(n):
                return [[take(n), take(n)] for _ in range(2)]

            q_d, i_d = [take(T), take(T)], [take(T), take(T)]
            qp, ks, tot, att, tot2 = pairs_of(T), pairs_of(T), pairs_of(T), pairs_of(T), pairs_of(T // 2)
            k_tok, v_tok = [take(T), take(T)], [take(T), take(T)]
            states, o_t, sq = take(3 * P), take(T), take(T)
            root = take(4)
            m_bank = [[0, 1], [2, 3]]
            v_bank, k_bank, add_bank, o_bank, norm_bank = 4, 5, 6, [7, 4], [5, 6]
            slot_list = [("diag", 0, 0), ("diag", 0, 1)] + [("level", n, d) for n in range(nl) for d in range(2)]
            slots_of_head = range(len(slot_list))

            def tile_of(first, h):
                return proj1[:, bass.ds(h * T + first * T, T)]

            def per_level(names):
                return [f"{k}{n}_{d}" for n in range(nl) for d in range(2) for k in names]

            l_pe, l_vec, l_pool = steps(hg_L_pe=["diag_0", "diag_1"] + per_level(["m"]),
                                        hg_L_vec=["diag_0", "diag_1"] + per_level(["q", "t", "m"]),
                                        hg_L_pool=per_level(["k"]))
            p_act, p_vec, p_pool = steps(hg_P_act=["q", "tot_0", "tot_1", "ks_0", "ks_1"], hg_P_vec=["qp_0", "qp_1"],
                                         hg_P_pool=["q"])
            t_pe, t_act, t_vec, t_pool = steps(
                hg_T_pe=["^", "v_0", "k_0", "v_1", "k_1", "add_0", "o_0", "add_1", "o_1", "sum", "spread"],
                hg_T_act=["i", "v_0", "k_0", "v_1", "k_1", "o", "square", "root"],
                hg_T_vec=["^", "st0_0", "st1_0", "st2_0", "st0_1", "st1_1", "st2_1", "o", "inv", "norm", "out"],
                hg_T_pool=["i"])

            def run(engine, level, tail, prep):
                for t in slots_of_head:
                    prep(t, 0, 0)
                for t in slots_of_head:
                    level(t, 0, 0)
                    prep(t, 1, 1)
                with fori(engine, 0, HEADS // 2 - 1) as j:
                    for t in slots_of_head:
                        level(t, j * 2 + 1, 1)
                        tail(t, j * 2, 0)
                        prep(t, j * 2 + 2, 0)
                    for t in slots_of_head:
                        level(t, j * 2 + 2, 0)
                        tail(t, j * 2 + 1, 1)
                        prep(t, j * 2 + 3, 1)
                for t in slots_of_head:
                    level(t, HEADS - 1, 1)
                    tail(t, HEADS - 2, 0)
                for t in slots_of_head:
                    tail(t, HEADS - 1, 1)

            def is_first(h, count=1):
                return isinstance(h, int) and h < count

            with nc.Block() as block:
                @block.sync
                def _(sp):
                    ring.prefetch(sp, dram["hg_out"])

                @block.gpsimd
                def _(pool):
                    def level(t, h, p):
                        kind, n, d = slot_list[t]
                        if kind != "level":
                            return
                        b = LEVELS[n]
                        pairs = T // (2 * b)
                        t_in = (tot if n % 2 == 0 else tot2)[p][d][:, 0:2 * pairs].rearrange("p (n two) -> p n two", two=2)
                        k4 = ks[p][d].rearrange("p (n two b) -> p n two b", two=2, b=b)[:, :, 0, :]
                        pool.wait_ge(l_pe.sem, l_pe.at(f"m{n}_{d}", h))
                        if n:
                            pool.wait_ge(l_vec.sem, l_vec.at(f"t{n - 1}_{d}", h))
                            pool.wait_ge(l_pool.sem, l_pool.at(f"k{n - 1}_{d}", h))
                        pool.tensor_tensor(k4, k4, t_in[:, :, 1:2].broadcast_to([P, pairs, b]), ALU.mult
                                           ).then_inc(l_pool.sem, l_pool.one(f"k{n}_{d}"))

                    def tail(t, h, p):
                        if t == 1:
                            pool.wait_ge(t_act.sem, t_act.at("i", h))
                            pool.wait_ge(t_pe.sem, t_pe.passes(h))
                            hold(pool, "pool")
                            pool.tensor_copy(i_d[1], i_d[0][:, ::-1]).then_inc(t_pool.sem, t_pool.one("i"))

                    def prep(t, h, p):
                        if t == 10:
                            pool.wait_ge(p_act.sem, p_act.at("q", h))
                            if not is_first(h):
                                pool.wait_ge(l_pe.sem, l_pe.at("diag_1", h - 1))
                                pool.wait_ge(p_vec.sem, p_vec.at("qp_1", h - 1))
                            hold(pool, "pool")
                            pool.tensor_copy(q_d[1], q_d[0][:, ::-1]).then_inc(p_pool.sem, p_pool.one("q"))

                    run(pool, level, tail, prep)

                @block.scalar
                def _(act):
                    def level(t, h, p):
                        pass

                    def tail(t, h, p):
                        if t == 0:
                            act.wait_ge(t_pe.sem, t_pe.passes(h))
                            act.wait_ge(t_vec.sem, t_vec.passes(h))
                            act.activation(i_d[0], tile_of(I1, h), ACT.Copy).then_inc(t_act.sem, t_act.one("i"))
                        copies = {2: ("v", 0), 3: ("k", 0), 4: ("v", 1), 5: ("k", 1)}
                        if t in copies:
                            m, d = copies[t]
                            act.wait_ge(t_pe.sem, t_pe.at(f"{m}_{d}", h))
                            act.activation((v_tok if m == "v" else k_tok)[d], banks[v_bank if m == "v" else k_bank], ACT.Copy
                                           ).then_inc(t_act.sem, t_act.one(f"{m}_{d}"))
                        if t == 8:
                            act.wait_ge(t_pe.sem, t_pe.at("o_0", h))
                            act.activation(o_t, banks[o_bank[0]], ACT.Copy).then_inc(t_act.sem, t_act.one("o"))
                        if t == 11:
                            act.wait_ge(t_vec.sem, t_vec.at("o", h))
                            act.activation(sq, o_t, ACT.Square).then_inc(t_act.sem, t_act.one("square"))
                        if t == 12:
                            act.wait_ge(t_pe.sem, t_pe.at("sum", h))
                            act.activation(root, banks[norm_bank[0]][:, 0:NC], ACT.Sqrt, bias=col("eps"), scale=1.0 / P
                                           ).then_inc(t_act.sem, t_act.one("root"))

                    def prep(t, h, p):
                        if t == 9:
                            if not is_first(h):
                                act.wait_ge(l_pe.sem, l_pe.at("diag_1", h - 1))
                                act.wait_ge(p_vec.sem, p_vec.at("qp_1", h - 1))
                                act.wait_ge(p_pool.sem, p_pool.at("q", h - 1))
                            act.activation(q_d[0], tile_of(Q1, h), ACT.Copy).then_inc(p_act.sem, p_act.one("q"))
                        if t in (9, 10):
                            d = t - 9
                            if not is_first(h, 2) and d == 0:
                                act.wait_ge(t_vec.sem, t_vec.at("st2_1", h - 2))
                                act.wait_ge(t_pe.sem, t_pe.at("k_1", h - 2))
                            act.activation(tot[p][d], tile_of((FWD1, BWD1)[d], h), ACT.Copy).then_inc(p_act.sem, p_act.one(f"tot_{d}"))
                        if t == 11:
                            for d in range(2):
                                act.wait_ge(p_act.sem, p_act.at(f"tot_{d}", h))
                                act.activation(ks[p][d], tot[p][d], ACT.Identity, scale=-1.0, bias=col("one")).then_inc(p_act.sem, p_act.one(f"ks_{d}"))

                    run(act, level, tail, prep)

                @block.tensor
                def _(pe):
                    pe.sem_inc(t_pe.sem, 1)

                    def level(t, h, p):
                        kind, n, d = slot_list[t]
                        if kind == "diag":
                            pe.wait_ge(p_act.sem, p_act.at(f"ks_{d}", h))
                            if d:
                                pe.wait_ge(p_pool.sem, p_pool.at("q", h))
                            if not is_first(h):
                                pe.wait_ge(l_vec.sem, l_vec.at(f"m{nl - 2}_{d}", h - 1))
                            for c in range(NC):
                                ins = pe.matmul(chunk(banks[d], c), chunk(ks[p][d], c), chunk(q_d[d], c), start=True, stop=True)
                            ins.then_inc(l_pe.sem, l_pe.one(f"diag_{d}"))
                        else:
                            if n == 0:
                                pe.wait_ge(p_vec.sem, p_vec.at(f"qp_{d}", h))
                                if not is_first(h):
                                    pe.wait_ge(l_vec.sem, l_vec.at(f"m{nl - 1}_{d}", h - 1))
                            else:
                                pe.wait_ge(l_vec.sem, l_vec.at(f"q{n - 1}_{d}", h))
                                pe.wait_ge(l_pool.sem, l_pool.at(f"k{n - 1}_{d}", h))
                                pe.wait_ge(l_vec.sem, l_vec.at(f"m{n - 2}_{d}" if n > 1 else f"diag_{d}", h))
                            for c in range(NC):
                                if n == nl - 1:
                                    b = LEVELS[n]
                                    ins = pe.matmul(chunk(banks[m_bank[n % 2 == 0][d]], c)[0:b, b:P], chunk(ks[p][d], c)[:, 0:b],
                                                    chunk(qp[p][d], c)[:, b:P], start=True, stop=True)
                                    continue
                                ins = pe.matmul(chunk(banks[m_bank[n % 2 == 0][d]], c), chunk(ks[p][d], c), chunk(qp[p][d], c),
                                                start=True, stop=True)
                            ins.then_inc(l_pe.sem, l_pe.one(f"m{n}_{d}"))

                    def tail(t, h, p):
                        turns = {1: ("v", 0), 2: ("k", 0), 3: ("v", 1), 4: ("k", 1)}
                        if t in turns:
                            m, d = turns[t]
                            src, bank = (i_d[d], v_bank) if m == "v" else (ks[p][d], k_bank)
                            if m == "v" and d == 0:
                                pe.wait_ge(t_act.sem, t_act.at("i", h))
                                pe.wait_ge(t_vec.sem, t_vec.passes(h))
                            elif m == "k" and d == 0:
                                pe.wait_ge(l_pool.sem, l_pool.at(f"k{nl - 1}_1", h))
                            elif m == "v":
                                pe.wait_ge(t_pool.sem, t_pool.at("i", h))
                                pe.wait_ge(t_act.sem, t_act.at("v_0", h))
                            else:
                                pe.wait_ge(t_act.sem, t_act.at("k_0", h))
                            for c in range(NC):
                                ins = pe.transpose(chunk(banks[bank], c), chunk(src, c), ident)
                            ins.then_inc(t_pe.sem, t_pe.one(f"{m}_{d}"))
                        for d, at in ((0, 5), (1, 8)):
                            if t == at:
                                pe.wait_ge(t_act.sem, t_act.at(f"k_{d}", h))
                                if d:
                                    pe.wait_ge(t_vec.sem, t_vec.at("st2_0", h))
                                for c in range(NC - 1):
                                    ins = pe.matmul(chunk(banks[add_bank], c), chunk(k_tok[d], c), chunk(v_tok[d], c), start=True, stop=True)
                                ins.then_inc(t_pe.sem, t_pe.one(f"add_{d}"))
                        for d, at in ((0, 7), (1, 10)):
                            if t == at:
                                pe.wait_ge(t_vec.sem, t_vec.at(f"st2_{d}", h))
                                if d == 0:
                                    pe.wait_ge(l_vec.sem, l_vec.at(f"m{nl - 1}_1", h))
                                for c in range(NC):
                                    out = chunk(banks[o_bank[d]], c)
                                    ins = pe.matmul(out, chunk(v_tok[d], c), chunk(att[p][d], c), start=True, stop=c == 0)
                                    if c:
                                        ins = pe.matmul(out, chunk(states, c - 1), chunk(qp[p][d], c), start=False, stop=True)
                                ins.then_inc(t_pe.sem, t_pe.one(f"o_{d}"))
                        if t == 12:
                            pe.wait_ge(t_act.sem, t_act.at("square", h))
                            for c in range(NC):
                                ins = pe.matmul(banks[norm_bank[0]][:, c:c + 1], chunk(sq, c), ones[:, 0:1], start=True, stop=True)
                            ins.then_inc(t_pe.sem, t_pe.one("sum"))
                        if t == 14:
                            pe.wait_ge(t_vec.sem, t_vec.at("inv", h))
                            for c in range(NC):
                                ins = pe.matmul(chunk(banks[norm_bank[1]], c), root[:, c:c + 1].broadcast_to([P, P]), ident,
                                                start=True, stop=True)
                            ins.then_inc(t_pe.sem, t_pe.one("spread"))

                    def prep(t, h, p):
                        pass

                    run(pe, level, tail, prep)

                @block.vector
                def _(dve):
                    dve.sem_inc(t_vec.sem, 1)

                    def level(t, h, p):
                        kind, n, d = slot_list[t]
                        if kind == "diag":
                            dve.wait_ge(l_pe.sem, l_pe.at(f"diag_{d}", h))
                            dve.tensor_tensor(by_chunk(att[p][d]), by_chunk(banks[d]), over_chunks(ident), ALU.mult
                                              ).then_inc(l_vec.sem, l_vec.one(f"diag_{d}"))
                            return
                        b = LEVELS[n]
                        pairs = T // (2 * b)
                        t_in, t_out = (tot, tot2) if n % 2 == 0 else (tot2, tot)
                        t_in = t_in[p][d][:, 0:2 * pairs].rearrange("p (n two) -> p n two", two=2)
                        q4 = qp[p][d].rearrange("p (n two b) -> p n two b", two=2, b=b)[:, :, 1, :]
                        dve.wait_ge(l_pe.sem, l_pe.at(f"m{n}_{d}", h))
                        if n:
                            dve.wait_ge(l_vec.sem, l_vec.at(f"t{n - 1}_{d}", h))
                        dve.tensor_tensor(q4, q4, t_in[:, :, 0:1].broadcast_to([P, pairs, b]), ALU.mult).then_inc(l_vec.sem, l_vec.one(f"q{n}_{d}"))
                        if n:
                            dve.wait_ge(l_pool.sem, l_pool.at(f"k{n - 1}_{d}", h))
                        dve.tensor_tensor(t_out[p][d][:, 0:pairs], t_in[:, :, 0], t_in[:, :, 1], ALU.mult).then_inc(l_vec.sem, l_vec.one(f"t{n}_{d}"))
                        dve.wait_ge(l_vec.sem, l_vec.at(f"m{n - 1}_{d}" if n else f"diag_{d}", h))
                        hold(dve, "vec")
                        dve.copy_predicated(blocks_of_chunks(att[p][d], b, 1), block_mask("up", n, 1),
                                            blocks_of_chunks(banks[m_bank[n % 2 == 0][d]], b, 1)).then_inc(l_vec.sem, l_vec.one(f"m{n}_{d}"))

                    def tail(t, h, p):
                        for d, at in ((0, 6), (1, 9)):
                            if t == at:
                                whole = (tot2 if nl % 2 else tot)[p][d]
                                dve.wait_ge(l_vec.sem, l_vec.at(f"m{nl - 1}_1", h))
                                dve.wait_ge(t_pe.sem, t_pe.at(f"add_{d}", h))
                                dve.tensor_copy(chunk(states, 0), chunk(banks[add_bank], 0)).then_inc(t_vec.sem, t_vec.one(f"st0_{d}"))
                                for c in (1, 2):
                                    dve.wait_ge(t_vec.sem, t_vec.at(f"st{c - 1}_{d}", h))
                                    dve.scalar_tensor_tensor(chunk(states, c), chunk(states, c - 1), whole[:, c:c + 1],
                                                             chunk(banks[add_bank], c), ALU.mult, ALU.add).then_inc(t_vec.sem, t_vec.one(f"st{c}_{d}"))
                        if t == 11:
                            dve.wait_ge(t_act.sem, t_act.at("o", h))
                            dve.wait_ge(t_pe.sem, t_pe.at("o_1", h))
                            dve.tensor_tensor(o_t, banks[o_bank[1]][:, ::-1], o_t, ALU.add).then_inc(t_vec.sem, t_vec.one("o"))
                        if t == 13:
                            dve.wait_ge(t_act.sem, t_act.at("root", h))
                            dve.reciprocal(root, root).then_inc(t_vec.sem, t_vec.one("inv"))
                        if t == 15:
                            dve.wait_ge(t_pe.sem, t_pe.at("spread", h))
                            dve.scalar_tensor_tensor(o_t, o_t, cols[:, bass.ds(h + COL["hgw"], 1)], banks[norm_bank[1]],
                                                     ALU.mult, ALU.mult).then_inc(t_vec.sem, t_vec.one("norm"))
                            dve.wait_ge(t_vec.sem, t_vec.at("norm", h))
                            dve.tensor_tensor(hT1[:, bass.ds(h * T, T)], o_t, tile_of(G1, h), ALU.mult).then_inc(t_vec.sem, t_vec.one("out"))

                    def prep(t, h, p):
                        if t in (12, 13):
                            d = t - 12
                            if not is_first(h, 2):
                                dve.wait_ge(t_pe.sem, t_pe.at("o_1", h - 2))
                            if d:
                                dve.wait_ge(p_pool.sem, p_pool.at("q", h))
                            dve.wait_ge(p_act.sem, p_act.at(f"tot_{d}", h))
                            dve.tensor_tensor(qp[p][d], q_d[d], tot[p][d], ALU.mult).then_inc(p_vec.sem, p_vec.one(f"qp_{d}"))

                    run(dve, level, tail, prep)

        def final_norm(outer):
            name, src, width, gain = "norm_final", x3, T, "final"
            dst = area(outer, "normed", KD * T).rearrange("p (n t) -> p n t", t=T)
            root, inv = area(outer, "final_root", T), area(outer, "final_inverse", T)
            with ExitStack() as scope:
                act_s, pe_s, v_s = steps(**{
                    name + "_act": ["root"], name + "_pe": ["sum"],
                    name + "_vec": ["inverse"] + [f"out{k}" for k in range(KD)]})
                with nc.Block() as block:
                    @block.sync
                    def _(sp):
                        for k in range(KD):
                            sp.wait_ge(v_s.sem, v_s.at(f"out{k}"))
                            sp.dma_start(out_d[:, k, :], dst[:, k, :]).then_inc(stored, 16)
                        sp.wait_ge(stored, 16 * KD)

                    @block.scalar
                    def _(act):
                        act.wait_ge(pe_s.sem, pe_s.at("sum"))
                        act.activation(root, banks[0][:, 0:width], ACT.Sqrt, bias=col("eps"),
                                                  scale=1.0 / D).then_inc(act_s.sem, act_s.one("root"))

                    @block.tensor
                    def _(pe):
                        pe.matmul(banks[0][:, 0:width], ones, x_squares, start=True, stop=True).then_inc(pe_s.sem, pe_s.one("sum"))

                    @block.vector
                    def _(dve):
                        dve.wait_ge(act_s.sem, act_s.at("root"))
                        dve.reciprocal(inv, root).then_inc(v_s.sem, v_s.one("inverse"))
                        dve.wait_ge(v_s.sem, v_s.at("inverse"))
                        for k in range(KD):
                            dve.scalar_tensor_tensor(dst[:, k, :], src[:, k, :], col(gain, k), inv,
                                                              ALU.mult, ALU.mult).then_inc(v_s.sem, v_s.one(f"out{k}"))


        with ExitStack() as inner:
            cross_attention(0, inner)
        clear_semaphores()
        with ExitStack() as inner:
            swiglu(0, inner, dram["hg_in"])
        with ExitStack() as mixer1:
            proj1 = area(mixer1, "proj1", 5 * HEADS * T)
            with ExitStack() as inner:
                hgrn_projection(inner)
            hT1 = area(mixer1, "hT1", KD * T)
            with ExitStack() as inner:
                hgrn(inner)
            clear_semaphores()
            rhs = halves(mixer1, "mix1_h", KD)
            add_to_residual(mixer1, "mix1_out", dram["hg_out"], rhs, dram["wk1"],
                            SplitSource(mixer1, "mix1", hT1.rearrange("p (n t) -> p n t", t=T), rhs))
        with ExitStack() as inner:
            cross_attention(1, inner)
        clear_semaphores()
        with ExitStack() as inner:
            swiglu(1, inner, None)
        with ExitStack() as inner:
            final_norm(inner)


def tiles(w, width=P, cuts=1):
    k, n = w.shape
    w = w.reshape(cuts, k // P // cuts, P, n // width, width).transpose(3, 0, 2, 1, 4)
    return np.ascontiguousarray(w.reshape(n // width * cuts, P, -1))


def channels(v):
    return v.reshape(-1, P).T


def kernel(**inputs):
    import concourse.bacc as bacc
    from concourse.bass_utils import run_bass_kernel_spmd as run

    a = {k: np.asarray(v) for k, v in inputs.items()}
    f = np.float32
    ab = a["ab_w_in"][0]
    z0 = RW_TILES * P
    order = np.concatenate([ab[:, :z0], ab[:, z0 + 512:z0 + 1536], ab[:, z0:z0 + 512], ab[:, z0 + 1536:],
                            np.zeros((D, P - HEADS), f)], axis=1)
    zero = np.zeros((64, 512), f)
    lora = np.concatenate([
        np.concatenate([a["rw_w2"][0, 0], zero]).reshape(P, 512), np.concatenate([a["rw_w2"][0, 1], zero]),
        np.concatenate([zero, a["rw_a2"][0]]), a["rw_g2"][0]], axis=1)

    tri = np.arange(P)
    up, low = tri[:, None] < tri[None, :], tri[:, None] > tri[None, :]
    eye = np.eye(P, dtype=f)
    head = (tri[:, None] // HD == tri[None, :] // HD).astype(f)
    levels = [((tri[:, None] // b) % 2 == 0) & (tri[None, :] // b == tri[:, None] // b + 1) for b in LEVELS]
    reset = np.ones((P, T), f)
    reset[:, ::P] = 0.0
    tab = np.concatenate([eye, np.ones((P, P), f), head, up.astype(f), (up | (eye > 0)).astype(f), reset] + [m.astype(f) for m in levels]
                         + [m.T.astype(f) for m in levels], axis=1)

    cols = np.zeros((P, NCOLS), f)

    def put(name, block):
        cols[0:block.shape[0], COL[name]:COL[name] + block.shape[1]] = block

    put("one", np.ones((P, 1), f))
    put("eps", np.full((P, 1), 1e-6, f))
    put("gneps", np.full((P, 1), 64e-5, f))
    for n in range(2):
        put(f"mix{n}", channels(a["mix_norm"][n]))
        put(f"xa{n}", channels(a["xa_norm"][n]))
        put(f"mem{n}", channels(a["mem_norm"][n]))
        put(f"ffn{n}", channels(a["ffn_norm"][n]))
        put(f"lb{n}", channels(a["hg_lb"][n]))
    put("final", channels(a["final_norm"]))
    put("mu", channels(a["rw_mu"][0]))
    taps = [channels(v) for v in (*a["ssd_conv_w"][0], a["ssd_conv_b"][0])]
    put("taps", np.stack(taps, axis=2).reshape(P, 32))
    vecs = [a["rw_w0"][0, 0], a["rw_w0"][0, 1], a["rw_a0"][0], a["rw_k_k"][0], a["rw_k_a"][0],
            a["rw_r_k"][0].reshape(-1), a["rw_gn_w"][0], a["rw_gn_b"][0]]
    put("rw", np.stack([channels(v) for v in vecs], axis=2).reshape(P, -1))
    put("ssd_d", channels(np.repeat(a["ssd_d"][0], HD)))
    put("ssd_w", channels(a["ssd_norm_w"][0]))
    put("hgw", channels(a["hg_norm_w"][0]))
    put("dtb", a["ssd_dt_bias"][0].T)
    put("alog", a["ssd_a_log"][0].T)

    arrays = {
        "xT": np.ascontiguousarray(a["x"][0].T.reshape(KD, P, T).transpose(1, 0, 2).reshape(P, -1)),
        "memT": np.ascontiguousarray(a["mem"][0].T.reshape(KD, P, MEM).transpose(1, 0, 2).reshape(P, -1)),
        "tab": tab, "cols": cols, "lora": np.ascontiguousarray(lora),
        "ab_in": tiles(order), "ab_out": tiles(a["ab_w_out"][0]),
        "hg_in": tiles(a["hg_w_in"][0]), "hg_out": tiles(a["hg_w_out"][0]),
    }
    for n in range(2):
        arrays[f"wq{n}"] = tiles(a["xa_wq"][n])
        arrays[f"wk{n}"] = tiles(a["xa_wkv"][n][:, :D])
        arrays[f"wv{n}"] = tiles(a["xa_wkv"][n][:, D:], 256, 2)
        arrays[f"wo{n}"] = tiles(a["xa_wo"][n])
        w = a["ffn_w_in"][n]
        arrays[f"f_in{n}"] = tiles(np.ascontiguousarray(w.reshape(D, 2, FT, P).transpose(0, 2, 1, 3)).reshape(D, 2 * FFN))
        arrays[f"f_out{n}"] = tiles(a["ffn_w_out"][n], cuts=2)

    nc = bacc.Bacc("TRN2", target_bir_lowering=False, num_devices=1)
    dram = {k: nc.dram_tensor("in_" + k, v.shape, F32, kind="ExternalInput").ap() for k, v in arrays.items()}
    out_d = nc.dram_tensor("out_yT", (P, KD, T), F32, kind="ExternalOutput").ap()
    scratch_d = nc.dram_tensor("scratch_cum", (2 * 8 * T,), F32, kind="Internal").ap()
    build_program(nc, dram, out_d, scratch_d)
    r = run(nc, [{"in_" + k: v for k, v in arrays.items()}], core_ids=[0])
    y = r.results[0]["out_yT"]
    return np.ascontiguousarray(y.transpose(1, 0, 2).reshape(D, T).T.reshape(1, T, D))
```
